# Optimizing a Trainium2 kernel written in Bass

```python
import math
import jax, jax.numpy as jnp
from jax import lax
import numpy as np
import jax
import jax.numpy as jnp

D_MODEL = 2048
BATCH = 1
SEQ = 256
DEPTH = 1

HEAD_DIM = 64
Q_BLOCK = 128
RMS_EPS = 1e-6
MASK_VALUE = -1e30
ALIBI_MAX_EXP = 8.0
FOX_HEADS = 7
NSA_HEADS = 8
NSA_KV_GROUPS = 2
NSA_CMP_LEN = 32
NSA_CMP_STRIDE = 16
NSA_SEL_BLOCK = 64
NSA_TOP_N = 16
NSA_WINDOW = 512
NSA_FORCE_SCORE = 1e4
DIL_CONFIGS = ((128, 1), (512, 4), (2048, 16))
DIL_HEADS_PER_GROUP = 3
DIL_HEADS = DIL_HEADS_PER_GROUP * len(DIL_CONFIGS)
DIFF_HEADS = 4
DIFF_QK_DIM = 64
DIFF_V_DIM = 2 * DIFF_QK_DIM
MIX_WIDTH = (FOX_HEADS + NSA_HEADS + DIL_HEADS) * HEAD_DIM + DIFF_HEADS * DIFF_V_DIM
D_FF = ((8 * D_MODEL + 3 * 256 - 1) // (3 * 256)) * 256
NSA_KV = NSA_KV_GROUPS * HEAD_DIM
IN_SPLITS = (
    ('fox_q', FOX_HEADS * HEAD_DIM), ('fox_k', FOX_HEADS * HEAD_DIM), ('fox_v', FOX_HEADS * HEAD_DIM), ('fox_f', FOX_HEADS),
    ('nsa_q', NSA_HEADS * HEAD_DIM),
    ('nsa_cmp_k', NSA_KV), ('nsa_cmp_v', NSA_KV), ('nsa_slc_k', NSA_KV), ('nsa_slc_v', NSA_KV), ('nsa_win_k', NSA_KV), ('nsa_win_v', NSA_KV),
    ('nsa_gate', NSA_HEADS * 3),
    ('dil_q', DIL_HEADS * HEAD_DIM), ('dil_k', DIL_HEADS * HEAD_DIM), ('dil_v', DIL_HEADS * HEAD_DIM),
    ('diff_q', DIFF_HEADS * 2 * DIFF_QK_DIM), ('diff_k', DIFF_HEADS * 2 * DIFF_QK_DIM), ('diff_v', DIFF_HEADS * DIFF_V_DIM),
)
N_IN = sum(w for _, w in IN_SPLITS)


def rms_norm(x, gain):
    xf = x.astype(jnp.float32)
    y = xf * lax.rsqrt(jnp.mean(xf * xf, axis=-1, keepdims=True) + RMS_EPS)
    return (y * gain.astype(jnp.float32)).astype(x.dtype)

def masked_softmax(s, mask):
    p = jax.nn.softmax(jnp.where(mask, s, MASK_VALUE), axis=-1)
    return jnp.where(mask, p, 0.0)

def alibi_slopes(n_heads):
    return jnp.asarray(2.0 ** (-ALIBI_MAX_EXP * np.arange(1, n_heads + 1) / n_heads), jnp.float32)

def blocks_to_seq(o):
    o = jnp.moveaxis(o, 0, 1)
    return o.reshape(o.shape[0], o.shape[1] * o.shape[2], *o.shape[3:])

def fox_attention(q, k, v, f_logit, f_bias):
    B, S, H, dh = q.shape
    scale = dh ** -0.5
    log_f = jax.nn.log_sigmoid(f_logit.astype(jnp.float32) + f_bias.astype(jnp.float32))
    cum = jnp.cumsum(log_f, axis=1).transpose(0, 2, 1)
    pos = jnp.arange(S)

    def block(i):
        qs = i * Q_BLOCK
        tq = qs + jnp.arange(Q_BLOCK)
        qb = lax.dynamic_slice_in_dim(q, qs, Q_BLOCK, 1)
        cq = lax.dynamic_slice_in_dim(cum, qs, Q_BLOCK, 2)
        s = jnp.einsum('bqhd,bkhd->bhqk', qb, k).astype(jnp.float32) * scale
        s = s + cq[..., None] - cum[:, :, None, :]
        p = jax.nn.softmax(jnp.where(pos[None, :] <= tq[:, None], s, MASK_VALUE), axis=-1)
        return jnp.einsum('bhqk,bkhd->bqhd', p.astype(v.dtype), v)

    o = blocks_to_seq(lax.map(block, jnp.arange(S // Q_BLOCK)))
    return o.reshape(B, S, H * dh)

def cmp_to_sel_matrix(n_cmp, n_sel):
    a = NSA_SEL_BLOCK // NSA_CMP_STRIDE
    b = NSA_CMP_LEN // NSA_CMP_STRIDE
    j = np.arange(n_sel)[:, None, None]
    idx = a * j + np.arange(a)[None, :, None] - np.arange(b)[None, None, :]
    jj = np.broadcast_to(j, idx.shape)
    ok = (idx >= 0) & (idx < n_cmp)
    m = np.zeros((n_cmp, n_sel), np.float32)
    np.add.at(m, (idx[ok], jj[ok]), 1.0)
    return m

def nsa_attention(q, k_cmp, v_cmp, k_slc, v_slc, k_win, v_win, gate_logit, cmp_w1, cmp_w2, cmp_pos):
    B, S, H, dh = q.shape
    G = k_cmp.shape[2]
    hpg = H // G
    scale = dh ** -0.5
    slopes = alibi_slopes(H).reshape(G, hpg)[None, :, :, None, None]
    ratio = NSA_CMP_LEN // NSA_CMP_STRIDE
    n_chunk = S // NSA_CMP_STRIDE
    n_cmp = n_chunk - ratio + 1
    n_sel = S // NSA_SEL_BLOCK
    n_top = min(NSA_TOP_N, n_sel)

    def compress(t, w1, w2, pos_emb):
        ch = t.reshape(B, n_chunk, NSA_CMP_STRIDE, G, dh)
        blk = jnp.concatenate([ch[:, r:r + n_cmp] for r in range(ratio)], axis=2)
        blk = (blk + pos_emb[:, None, :]).transpose(0, 1, 3, 2, 4).reshape(B, n_cmp, G, NSA_CMP_LEN * dh)
        return jax.nn.gelu(blk @ w1) @ w2

    kc = compress(k_cmp, cmp_w1[0], cmp_w2[0], cmp_pos[0])
    vc = compress(v_cmp, cmp_w1[1], cmp_w2[1], cmp_pos[1])
    cmp_end = jnp.arange(n_cmp) * NSA_CMP_STRIDE + (NSA_CMP_LEN - 1)
    cmp_to_sel = jnp.asarray(cmp_to_sel_matrix(n_cmp, n_sel), jnp.float32)
    k_blocks = k_slc.transpose(0, 2, 1, 3).reshape(B, G, n_sel, NSA_SEL_BLOCK, dh)
    v_blocks = v_slc.transpose(0, 2, 1, 3).reshape(B, G, n_sel, NSA_SEL_BLOCK, dh)
    pad = ((0, 0), (NSA_WINDOW, 0), (0, 0), (0, 0))
    k_win_p = jnp.pad(k_win, pad)
    v_win_p = jnp.pad(v_win, pad)
    gates = jax.nn.sigmoid(gate_logit).reshape(B, S, G, hpg, 3)
    sel_ids = jnp.arange(n_sel)
    win_offsets = jnp.arange(Q_BLOCK + NSA_WINDOW) - NSA_WINDOW
    sel_offsets = jnp.arange(NSA_SEL_BLOCK)

    def block(i):
        qs = i * Q_BLOCK
        tq = qs + jnp.arange(Q_BLOCK)
        qb = lax.dynamic_slice_in_dim(q, qs, Q_BLOCK, 1).reshape(B, Q_BLOCK, G, hpg, dh)
        dist_c = (tq[:, None] - cmp_end[None, :]).astype(jnp.float32)
        s_c = jnp.einsum('bqgjd,bcgd->bgjqc', qb, kc).astype(jnp.float32) * scale - slopes * dist_c
        p_c = masked_softmax(s_c, dist_c >= 0)
        o_c = jnp.einsum('bgjqc,bcgd->bqgjd', p_c.astype(vc.dtype), vc)
        imp = jnp.einsum('bgjqc,cn->bgqn', p_c, cmp_to_sel)
        cur = (tq // NSA_SEL_BLOCK)[:, None]
        forced = (sel_ids == 0) | (sel_ids == cur) | (sel_ids == cur - 1)
        causal = sel_ids * NSA_SEL_BLOCK <= tq[:, None]
        score = jnp.where(causal, jnp.where(forced, NSA_FORCE_SCORE, imp), MASK_VALUE)
        _, top_idx = lax.top_k(score, n_top)
        flat = top_idx.reshape(B, G, Q_BLOCK * n_top)[..., None, None]
        ks = jnp.take_along_axis(k_blocks, flat, axis=2).reshape(B, G, Q_BLOCK, n_top * NSA_SEL_BLOCK, dh)
        vs = jnp.take_along_axis(v_blocks, flat, axis=2).reshape(B, G, Q_BLOCK, n_top * NSA_SEL_BLOCK, dh)
        kpos = (top_idx[..., None] * NSA_SEL_BLOCK + sel_offsets).reshape(B, G, Q_BLOCK, n_top * NSA_SEL_BLOCK)
        dist_s = (tq[:, None] - kpos).astype(jnp.float32)[:, :, None]
        s_s = jnp.einsum('bqgjd,bgqkd->bgjqk', qb, ks).astype(jnp.float32) * scale - slopes * dist_s
        p_s = masked_softmax(s_s, dist_s >= 0)
        o_s = jnp.einsum('bgjqk,bgqkd->bqgjd', p_s.astype(vs.dtype), vs)
        kw = lax.dynamic_slice_in_dim(k_win_p, qs, Q_BLOCK + NSA_WINDOW, 1)
        vw = lax.dynamic_slice_in_dim(v_win_p, qs, Q_BLOCK + NSA_WINDOW, 1)
        kpos_w = qs + win_offsets
        dist_w = tq[:, None] - kpos_w[None, :]
        mask_w = (dist_w >= 0) & (dist_w < NSA_WINDOW) & (kpos_w[None, :] >= 0)
        s_w = jnp.einsum('bqgjd,bkgd->bgjqk', qb, kw).astype(jnp.float32) * scale - slopes * dist_w.astype(jnp.float32)
        p_w = masked_softmax(s_w, mask_w)
        o_w = jnp.einsum('bgjqk,bkgd->bqgjd', p_w.astype(vw.dtype), vw)
        g = lax.dynamic_slice_in_dim(gates, qs, Q_BLOCK, 1)
        return g[..., 0:1] * o_c + g[..., 1:2] * o_s + g[..., 2:3] * o_w

    o = blocks_to_seq(lax.map(block, jnp.arange(S // Q_BLOCK)))
    return o.reshape(B, S, H * dh)

def dilated_attention(q, k, v):
    B, S, H, dh = q.shape
    scale = dh ** -0.5
    slopes = alibi_slopes(H)
    hpg = DIL_HEADS_PER_GROUP
    k_groups = [k[:, :, g * hpg:(g + 1) * hpg] for g in range(len(DIL_CONFIGS))]
    v_groups = [v[:, :, g * hpg:(g + 1) * hpg] for g in range(len(DIL_CONFIGS))]

    def block(i):
        qs = i * Q_BLOCK
        tq = qs + jnp.arange(Q_BLOCK)
        qb = lax.dynamic_slice_in_dim(q, qs, Q_BLOCK, 1)
        outs, lses = [], []
        for g, (window, dilation) in enumerate(DIL_CONFIGS):
            steps = jnp.arange(window // dilation + 1) * dilation
            kidx = tq[:, None] - steps[None, :]
            valid = kidx >= 0
            kidx = jnp.maximum(kidx, 0)
            kg = k_groups[g][:, kidx]
            vg = v_groups[g][:, kidx]
            s = jnp.einsum('bqhd,bqkhd->bhqk', qb[:, :, g * hpg:(g + 1) * hpg], kg).astype(jnp.float32) * scale
            s = s - slopes[g * hpg:(g + 1) * hpg][:, None, None] * steps.astype(jnp.float32)
            s = jnp.where(valid, s, MASK_VALUE)
            lse = jax.nn.logsumexp(s, axis=-1)
            p = jnp.exp(s - lse[..., None])
            outs.append(jnp.einsum('bhqk,bqkhd->bqhd', p.astype(vg.dtype), vg))
            lses.append(lse)
        w = jax.nn.softmax(jnp.stack(lses, axis=0), axis=0).transpose(0, 1, 3, 2)[..., None]
        return jnp.concatenate([o * w[g].astype(o.dtype) for g, o in enumerate(outs)], axis=2)

    o = blocks_to_seq(lax.map(block, jnp.arange(S // Q_BLOCK)))
    return o.reshape(B, S, H * dh)

def diff_attention(q, k, v, lam_vecs, subln_g, lam_init):
    B, S, H, _, dq = q.shape
    dv = v.shape[-1]
    scale = dq ** -0.5
    lv = lam_vecs.astype(jnp.float32)
    lam = jnp.exp(jnp.sum(lv[0] * lv[1])) - jnp.exp(jnp.sum(lv[2] * lv[3])) + lam_init
    slopes = alibi_slopes(H)[None, :, None, None, None]
    pos = jnp.arange(S)

    def block(i):
        qs = i * Q_BLOCK
        tq = qs + jnp.arange(Q_BLOCK)
        qb = lax.dynamic_slice_in_dim(q, qs, Q_BLOCK, 1)
        dist = tq[:, None] - pos[None, :]
        s = jnp.einsum('bqhmd,bkhmd->bhmqk', qb, k).astype(jnp.float32) * scale - slopes * dist.astype(jnp.float32)
        p = jax.nn.softmax(jnp.where(dist >= 0, s, MASK_VALUE), axis=-1)
        a = p[:, :, 0] - lam * p[:, :, 1]
        return jnp.einsum('bhqk,bkhd->bqhd', a.astype(v.dtype), v)

    o = blocks_to_seq(lax.map(block, jnp.arange(S // Q_BLOCK)))
    o = rms_norm(o, subln_g) * (1.0 - lam_init)
    return o.reshape(B, S, H * dv)

def hybrid_mixer(u, w_in, fox_f_bias, cmp_w1, cmp_w2, cmp_pos, diff_lambda, diff_subln_g, diff_lam_init, w_out):
    B, S, _ = u.shape
    proj = u @ w_in
    offsets = [int(o) for o in np.cumsum([w for _, w in IN_SPLITS])[:-1]]
    p = dict(zip([n for n, _ in IN_SPLITS], jnp.split(proj, offsets, axis=-1)))

    def hd(name, *shape):
        return p[name].reshape(B, S, *shape)

    o_fox = fox_attention(hd('fox_q', FOX_HEADS, HEAD_DIM), hd('fox_k', FOX_HEADS, HEAD_DIM),
                          hd('fox_v', FOX_HEADS, HEAD_DIM), p['fox_f'], fox_f_bias)
    o_nsa = nsa_attention(hd('nsa_q', NSA_HEADS, HEAD_DIM),
                          hd('nsa_cmp_k', NSA_KV_GROUPS, HEAD_DIM), hd('nsa_cmp_v', NSA_KV_GROUPS, HEAD_DIM),
                          hd('nsa_slc_k', NSA_KV_GROUPS, HEAD_DIM), hd('nsa_slc_v', NSA_KV_GROUPS, HEAD_DIM),
                          hd('nsa_win_k', NSA_KV_GROUPS, HEAD_DIM), hd('nsa_win_v', NSA_KV_GROUPS, HEAD_DIM),
                          hd('nsa_gate', NSA_HEADS, 3), cmp_w1, cmp_w2, cmp_pos)
    o_dil = dilated_attention(hd('dil_q', DIL_HEADS, HEAD_DIM), hd('dil_k', DIL_HEADS, HEAD_DIM),
                              hd('dil_v', DIL_HEADS, HEAD_DIM))
    o_diff = diff_attention(hd('diff_q', DIFF_HEADS, 2, DIFF_QK_DIM), hd('diff_k', DIFF_HEADS, 2, DIFF_QK_DIM),
                            hd('diff_v', DIFF_HEADS, DIFF_V_DIM), diff_lambda, diff_subln_g, diff_lam_init)
    o = jnp.concatenate([o_fox, o_nsa, o_dil, o_diff], axis=-1)
    return o @ w_out

def swiglu(u, w_gate, w_up, w_down):
    return (jax.nn.silu(u @ w_gate) * (u @ w_up)) @ w_down

def first_inputs(seed: int = 0) -> dict:
    key = jax.random.key(seed)
    ks = jax.random.split(key, 18)
    D = D_MODEL

    def nrm(k, shape, scale):
        return jax.random.normal(k, shape, jnp.float32) * scale

    return {
        'x': nrm(ks[0], (BATCH, SEQ, D), 1.0),
        'c': nrm(ks[1], (BATCH, D), 1.0),
        'ada_w': nrm(ks[2], (DEPTH, D, 6 * D), 0.5 * D ** -0.5),
        'ada_b': nrm(ks[3], (DEPTH, 6 * D), 0.02),
        'norm_mix_g': 1.0 + nrm(ks[4], (DEPTH, D), 0.02),
        'norm_ffn_g': 1.0 + nrm(ks[5], (DEPTH, D), 0.02),
        'w_in': nrm(ks[6], (DEPTH, D, N_IN), D ** -0.5),
        'fox_f_bias': 3.0 + nrm(ks[7], (DEPTH, FOX_HEADS), 0.5),
        'nsa_cmp_w1': nrm(ks[8], (DEPTH, 2, NSA_CMP_LEN * HEAD_DIM, HEAD_DIM), (NSA_CMP_LEN * HEAD_DIM) ** -0.5),
        'nsa_cmp_w2': nrm(ks[9], (DEPTH, 2, HEAD_DIM, HEAD_DIM), 1.5 * HEAD_DIM ** -0.5),
        'nsa_cmp_pos': nrm(ks[10], (DEPTH, 2, NSA_CMP_LEN, HEAD_DIM), 0.1),
        'diff_lambda': nrm(ks[11], (DEPTH, 4, DIFF_QK_DIM), 0.1),
        'diff_subln_g': 1.0 + nrm(ks[12], (DEPTH, DIFF_V_DIM), 0.02),
        'w_out': nrm(ks[13], (DEPTH, MIX_WIDTH, D), MIX_WIDTH ** -0.5),
        'ffn_w_gate': nrm(ks[14], (DEPTH, D, D_FF), D ** -0.5),
        'ffn_w_up': nrm(ks[15], (DEPTH, D, D_FF), D ** -0.5),
        'ffn_w_down': nrm(ks[16], (DEPTH, D_FF, D), D_FF ** -0.5),
        'final_norm_g': 1.0 + nrm(ks[17], (D,), 0.02),
    }

def first_block(x, c, ada_w, ada_b, norm_mix_g, norm_ffn_g, w_in, fox_f_bias, nsa_cmp_w1, nsa_cmp_w2,
              nsa_cmp_pos, diff_lambda, diff_subln_g, w_out, ffn_w_gate, ffn_w_up, ffn_w_down, final_norm_g):
    c_act = jax.nn.silu(c)
    h = x
    for layer in range(DEPTH):
        mod = c_act @ ada_w[layer] + ada_b[layer]
        sh1, sc1, g1, sh2, sc2, g2 = [m[:, None, :] for m in jnp.split(mod, 6, axis=-1)]
        lam_init = 0.8 - 0.6 * math.exp(-0.3 * layer)
        u = rms_norm(h, norm_mix_g[layer]) * (1.0 + sc1) + sh1
        h = h + g1 * hybrid_mixer(u, w_in[layer], fox_f_bias[layer], nsa_cmp_w1[layer], nsa_cmp_w2[layer],
                                  nsa_cmp_pos[layer], diff_lambda[layer], diff_subln_g[layer], lam_init, w_out[layer])
        u = rms_norm(h, norm_ffn_g[layer]) * (1.0 + sc2) + sh2
        h = h + g2 * swiglu(u, ffn_w_gate[layer], ffn_w_up[layer], ffn_w_down[layer])
    return rms_norm(h, final_norm_g)


CHUNK = 64
N_MEM = 256
NORM_EPS = 1e-6
NEG_INF = -1e30

A_HEADS = 8
A_HEAD_DIM = 128
A_WIDTH = A_HEADS * A_HEAD_DIM
A_LEFT_CHUNKS = 8
A_BAND = (A_LEFT_CHUNKS + 1) * CHUNK
REL_CLIP = 128

B_HEADS = 16
B_HEAD_DIM = 64
B_WIDTH = B_HEADS * B_HEAD_DIM
DECAY_LORA = 64
ICLR_LORA = 64
GN_EPS = 64e-5

C_HEADS = 4
C_HEAD_DIM = 256
C_WIDTH = C_HEADS * C_HEAD_DIM

IN_SPLITS_2 = (A_WIDTH,) * 4 + (B_WIDTH,) * 4 + (DECAY_LORA, ICLR_LORA) + (C_WIDTH,) * 2 + (D_MODEL,) * 3
IN_COLS = sum(IN_SPLITS_2)


def rms_norm_2(x, g):
    xf = x.astype(jnp.float32)
    y = xf * lax.rsqrt(jnp.mean(xf * xf, axis=-1, keepdims=True) + NORM_EPS)
    return (y * g.astype(jnp.float32)).astype(x.dtype)

def _rel_index():
    r = np.arange(CHUNK)[:, None]
    m = np.arange(A_BAND)[None, :]
    dist = r + A_LEFT_CHUNKS * CHUNK - m
    return np.clip(dist, -REL_CLIP, REL_CLIP) + REL_CLIP

def chunked_band_attention(q, k, v, rel_bias):
    bsz, s, h, dh = q.shape
    n_chunks = s // CHUNK
    pad = A_LEFT_CHUNKS * CHUNK
    kp = jnp.pad(k, ((0, 0), (pad, 0), (0, 0), (0, 0)))
    vp = jnp.pad(v, ((0, 0), (pad, 0), (0, 0), (0, 0)))
    bias = rel_bias[:, _rel_index()].astype(jnp.float32)
    band_pos = jnp.arange(A_BAND) - pad
    scale = dh ** -0.5

    def one_chunk(c):
        start = c * CHUNK
        qc = lax.dynamic_slice_in_dim(q, start, CHUNK, axis=1)
        kc = lax.dynamic_slice_in_dim(kp, start, A_BAND, axis=1)
        vc = lax.dynamic_slice_in_dim(vp, start, A_BAND, axis=1)
        sc = jnp.einsum('bqhd,bkhd->bhqk', qc, kc, preferred_element_type=jnp.float32) * scale + bias
        valid = (start + band_pos) >= 0
        sc = jnp.where(valid[None, None, None, :], sc, NEG_INF)
        p = jax.nn.softmax(sc, axis=-1)
        return jnp.einsum('bhqk,bkhd->bqhd', p.astype(vc.dtype), vc)

    out = lax.map(one_chunk, jnp.arange(n_chunks))
    return jnp.transpose(out, (1, 0, 2, 3, 4)).reshape(bsz, s, h * dh)

def token_shift_lerp(p, mu):
    prev = jnp.pad(p, ((0, 0), (1, 0), (0, 0)))[:, :-1]
    return p + mu * (prev - p)

def rwkv7_scan(r, decay, k, v, a_vec, b_vec):
    bsz, _, h, n = r.shape

    def step(state, inp):
        r_t, w_t, k_t, v_t, a_t, b_t = inp
        sa = jnp.einsum('bhij,bhj->bhi', state, a_t)
        state = state * w_t[:, :, None, :] + sa[..., None] * b_t[:, :, None, :] + v_t[..., None] * k_t[:, :, None, :]
        return state, jnp.einsum('bhij,bhj->bhi', state, r_t)

    xs = tuple(jnp.moveaxis(t, 1, 0) for t in (r, decay, k, v, a_vec, b_vec))
    s0 = jnp.zeros((bsz, h, n, n), jnp.float32)
    _, out = lax.scan(step, s0, xs)
    return jnp.moveaxis(out, 0, 1)

def rwkv7_time_mix(p_r, p_k, p_v, p_wd, p_ad, mu_rkv, mu_w, mu_a, w0, w2, a0, a2, k_k, k_a, r_k, ln_w, ln_b):
    f = lambda t: t.astype(jnp.float32)
    p_r, p_k, p_v, p_wd, p_ad = f(p_r), f(p_k), f(p_v), f(p_wd), f(p_ad)
    bsz, s, _ = p_r.shape
    r = token_shift_lerp(p_r, f(mu_rkv[0]))
    k = token_shift_lerp(p_k, f(mu_rkv[1]))
    v = token_shift_lerp(p_v, f(mu_rkv[2]))
    wd = token_shift_lerp(p_wd, f(mu_w))
    ad = token_shift_lerp(p_ad, f(mu_a))
    w = -jax.nn.softplus(-(f(w0) + jnp.tanh(wd) @ f(w2))) - 0.5
    decay = jnp.exp(-jnp.exp(w))
    a = jax.nn.sigmoid(f(a0) + ad @ f(a2))
    heads = lambda t: t.reshape(bsz, s, B_HEADS, B_HEAD_DIM)
    kk = heads(k * f(k_k))
    kk = kk * lax.rsqrt(jnp.maximum(jnp.sum(kk * kk, axis=-1, keepdims=True), 1e-24))
    k = k * (1.0 + (a - 1.0) * f(k_a))
    rh, kh, vh, ah, dh = heads(r), heads(k), heads(v), heads(a), heads(decay)
    o = rwkv7_scan(rh, dh, kh, vh, -kk, kk * ah)
    mean = jnp.mean(o, axis=-1, keepdims=True)
    var = jnp.mean(jnp.square(o - mean), axis=-1, keepdims=True)
    o = ((o - mean) * lax.rsqrt(var + GN_EPS)).reshape(bsz, s, B_WIDTH) * f(ln_w) + f(ln_b)
    bonus = jnp.sum(rh * kh * f(r_k), axis=-1, keepdims=True) * vh
    return o + bonus.reshape(bsz, s, B_WIDTH)

def memory_cross_attention(q, mk, mv):
    bsz, s, h, dh = q.shape
    sc = jnp.einsum('bshd,bmhd->bhsm', q, mk, preferred_element_type=jnp.float32) * (dh ** -0.5)
    p = jax.nn.softmax(sc, axis=-1)
    out = jnp.einsum('bhsm,bmhd->bshd', p.astype(mv.dtype), mv)
    return out.reshape(bsz, s, h * dh)

def hybrid_layer(x, mem, norm_g, w_in, a_q_g, a_k_g, a_rel_bias, w_up_a,
                 b_mu_rkv, b_mu_w, b_mu_a, b_w0, b_w2, b_a0, b_a2, b_k_k, b_k_a, b_r_k,
                 b_ln_w, b_ln_b, w_up_b, mem_norm_g, w_mem_kv, c_q_g, c_k_g, w_up_c, w_o):
    bsz, s, _ = x.shape
    h = rms_norm_2(x, norm_g)
    proj = h @ w_in
    offsets = np.cumsum(np.array(IN_SPLITS_2))[:-1].tolist()
    (aq, ak, av, az, br, bk, bv, bz, bwd, bad, cq, cz, ga, gb, gc) = jnp.split(proj, offsets, axis=-1)

    aq = rms_norm_2(aq.reshape(bsz, s, A_HEADS, A_HEAD_DIM), a_q_g)
    ak = rms_norm_2(ak.reshape(bsz, s, A_HEADS, A_HEAD_DIM), a_k_g)
    av = av.reshape(bsz, s, A_HEADS, A_HEAD_DIM)
    ya = chunked_band_attention(aq, ak, av, a_rel_bias) * jax.nn.silu(az)

    yb = rwkv7_time_mix(br, bk, bv, bwd, bad, b_mu_rkv, b_mu_w, b_mu_a, b_w0, b_w2, b_a0, b_a2,
                        b_k_k, b_k_a, b_r_k, b_ln_w, b_ln_b).astype(x.dtype) * jax.nn.silu(bz)

    m = rms_norm_2(mem, mem_norm_g)
    mk, mv = jnp.split(m @ w_mem_kv, 2, axis=-1)
    mk = rms_norm_2(mk.reshape(bsz, N_MEM, C_HEADS, C_HEAD_DIM), c_k_g)
    mv = mv.reshape(bsz, N_MEM, C_HEADS, C_HEAD_DIM)
    cq = rms_norm_2(cq.reshape(bsz, s, C_HEADS, C_HEAD_DIM), c_q_g)
    yc = memory_cross_attention(cq, mk, mv) * jax.nn.silu(cz)

    merged = (jax.nn.sigmoid(ga) * (ya @ w_up_a)
              + jax.nn.sigmoid(gb) * (yb @ w_up_b)
              + jax.nn.sigmoid(gc) * (yc @ w_up_c))
    return x + merged @ w_o

def second_inputs(seed: int = 0) -> dict:
    key = jax.random.key(seed)
    ks = jax.random.split(key, 32)
    nrm = lambda k, shape, sc: jax.random.normal(k, shape, jnp.float32) * sc
    L = DEPTH
    return {
        "x": nrm(ks[0], (BATCH, SEQ, D_MODEL), 1.0),
        "mem": nrm(ks[1], (BATCH, N_MEM, D_MODEL), 1.0),
        "norm_g": 1.0 + nrm(ks[2], (L, D_MODEL), 0.1),
        "w_in": nrm(ks[3], (L, D_MODEL, IN_COLS), D_MODEL ** -0.5),
        "a_q_g": 1.0 + nrm(ks[4], (L, A_HEAD_DIM), 0.1),
        "a_k_g": 1.0 + nrm(ks[5], (L, A_HEAD_DIM), 0.1),
        "a_rel_bias": nrm(ks[6], (L, A_HEADS, 2 * REL_CLIP + 1), 0.5),
        "w_up_a": nrm(ks[7], (L, A_WIDTH, D_MODEL), A_WIDTH ** -0.5),
        "b_mu_rkv": jax.random.uniform(ks[8], (L, 3, B_WIDTH), jnp.float32),
        "b_mu_w": jax.random.uniform(ks[9], (L, DECAY_LORA), jnp.float32),
        "b_mu_a": jax.random.uniform(ks[10], (L, ICLR_LORA), jnp.float32),
        "b_w0": jax.random.uniform(ks[11], (L, B_WIDTH), jnp.float32, minval=-3.0, maxval=0.5),
        "b_w2": nrm(ks[12], (L, DECAY_LORA, B_WIDTH), 0.1),
        "b_a0": nrm(ks[13], (L, B_WIDTH), 0.5),
        "b_a2": nrm(ks[14], (L, ICLR_LORA, B_WIDTH), 0.1),
        "b_k_k": 0.85 + nrm(ks[15], (L, B_WIDTH), 0.05),
        "b_k_a": 1.0 + nrm(ks[16], (L, B_WIDTH), 0.05),
        "b_r_k": nrm(ks[17], (L, B_HEADS, B_HEAD_DIM), 0.1),
        "b_ln_w": 1.0 + nrm(ks[18], (L, B_WIDTH), 0.1),
        "b_ln_b": nrm(ks[19], (L, B_WIDTH), 0.02),
        "w_up_b": nrm(ks[20], (L, B_WIDTH, D_MODEL), B_WIDTH ** -0.5),
        "mem_norm_g": 1.0 + nrm(ks[21], (L, D_MODEL), 0.1),
        "w_mem_kv": nrm(ks[22], (L, D_MODEL, 2 * C_WIDTH), D_MODEL ** -0.5),
        "c_q_g": 1.0 + nrm(ks[23], (L, C_HEAD_DIM), 0.1),
        "c_k_g": 1.0 + nrm(ks[24], (L, C_HEAD_DIM), 0.1),
        "w_up_c": nrm(ks[25], (L, C_WIDTH, D_MODEL), C_WIDTH ** -0.5),
        "w_o": nrm(ks[26], (L, D_MODEL, D_MODEL), D_MODEL ** -0.5),
    }

def second_block(x, mem, norm_g, w_in, a_q_g, a_k_g, a_rel_bias, w_up_a,
              b_mu_rkv, b_mu_w, b_mu_a, b_w0, b_w2, b_a0, b_a2, b_k_k, b_k_a, b_r_k,
              b_ln_w, b_ln_b, w_up_b, mem_norm_g, w_mem_kv, c_q_g, c_k_g, w_up_c, w_o):
    for l in range(DEPTH):
        x = hybrid_layer(x, mem, norm_g[l], w_in[l], a_q_g[l], a_k_g[l], a_rel_bias[l], w_up_a[l],
                         b_mu_rkv[l], b_mu_w[l], b_mu_a[l], b_w0[l], b_w2[l], b_a0[l], b_a2[l],
                         b_k_k[l], b_k_a[l], b_r_k[l], b_ln_w[l], b_ln_b[l], w_up_b[l],
                         mem_norm_g[l], w_mem_kv[l], c_q_g[l], c_k_g[l], w_up_c[l], w_o[l])
    return x


def setup_inputs(seed=0):
    out = dict(first_inputs(seed))
    for name, value in second_inputs(seed + 1).items():
        if name != "x":
            out[name + "_2"] = value
    return out


def reference(
    x, c, ada_w, ada_b, norm_mix_g, norm_ffn_g, w_in, fox_f_bias, nsa_cmp_w1, nsa_cmp_w2,
    nsa_cmp_pos, diff_lambda, diff_subln_g, w_out, ffn_w_gate, ffn_w_up, ffn_w_down,
    final_norm_g, mem_2, norm_g_2, w_in_2, a_q_g_2, a_k_g_2, a_rel_bias_2, w_up_a_2, b_mu_rkv_2,
    b_mu_w_2, b_mu_a_2, b_w0_2, b_w2_2, b_a0_2, b_a2_2, b_k_k_2, b_k_a_2, b_r_k_2, b_ln_w_2,
    b_ln_b_2, w_up_b_2, mem_norm_g_2, w_mem_kv_2, c_q_g_2, c_k_g_2, w_up_c_2, w_o_2,
):
    x = first_block(
        x, c, ada_w, ada_b, norm_mix_g, norm_ffn_g, w_in, fox_f_bias, nsa_cmp_w1, nsa_cmp_w2,
        nsa_cmp_pos, diff_lambda, diff_subln_g, w_out, ffn_w_gate, ffn_w_up, ffn_w_down,
        final_norm_g,
    )
    return second_block(
        x, mem_2, norm_g_2, w_in_2, a_q_g_2, a_k_g_2, a_rel_bias_2, w_up_a_2, b_mu_rkv_2,
        b_mu_w_2, b_mu_a_2, b_w0_2, b_w2_2, b_a0_2, b_a2_2, b_k_k_2, b_k_a_2, b_r_k_2, b_ln_w_2,
        b_ln_b_2, w_up_b_2, mem_norm_g_2, w_mem_kv_2, c_q_g_2, c_k_g_2, w_up_c_2, w_o_2,
    )


_drawn_inputs = setup_inputs


def setup_inputs(seed=0):
    import zlib

    import numpy as np

    out = dict(_drawn_inputs(seed))
    spreads = {}
    factors = {'norm_mix_g': 8.0,
     'norm_ffn_g': 7.757,
     'fox_f_bias': 3.138,
     'nsa_cmp_pos': 6.67,
     'diff_lambda': 3.861,
     'diff_subln_g': 8.0,
     'a_q_g_2': 8.0,
     'a_k_g_2': 8.0,
     'b_mu_w_2': 64.0,
     'b_k_k_2': 64.0,
     'b_k_a_2': 11.862,
     'b_ln_b_2': 22.434,
     'mem_norm_g_2': 8.0,
     'c_q_g_2': 8.0,
     'c_k_g_2': 8.0,
     'a_rel_bias_2': 8.0,
     'b_w2_2': 5.679,
     'b_ln_w_2': 4.788}
    for name, (base, spread) in spreads.items():
        noise = np.random.default_rng([zlib.crc32(name.encode()), seed]).standard_normal(out[name].shape)
        drawn = base * np.exp(spread * noise) if base else spread * noise
        out[name] = jnp.asarray(drawn.astype(out[name].dtype))
    for name, factor in factors.items():
        out[name] = (out[name] * factor).astype(out[name].dtype)
    return out
```

```python
import concourse.bass as bass
from concourse import mybir
from contextlib import ExitStack
import numpy as np

P = 128
SEQ = 256
TT = SEQ // P
D = 2048
KT = D // P
DH = 64
FOX, NSA, DIL, DIFF = 7, 8, 9, 4
N_CMP = 15
CMP_LEN, CMP_STRIDE = 32, 16
D_FF = 5632
KF = D_FF // P
CH = 512
LOAD = KT * CH
EPS = 1e-6
NEG = -1e30
LAM_INIT = 0.2

F32 = mybir.dt.float32
ALU = mybir.AluOpType
ACT = mybir.ActivationFunctionType
AX = mybir.AxisListType.X

PLAN = {}


def plan_loads():
    at = 0
    for name, n in (("ada_a", 8), ("w_in", 12), ("ada_b", 16), ("w_out", 4), ("ffn", 22), ("down", 12),
                    ("mem", 4), ("c_q", 2), ("a_qk", 4), ("a_v", 2), ("b_in", 6), ("z_in", 6), ("gates", 12),
                    ("ups", 6), ("w_o", 4)):
        PLAN[name] = (at, n)
        at += n
    return at


N_LOADS = plan_loads()

CONST = {}


def place(table, *items):
    at = 0
    for name, n in items:
        table[name] = (at, n)
        at += n
    return at


N_CONST = place(CONST, ("ident", 128), ("ones", 128), ("tri", 128), ("valid", 2))
N_ALIBI, N_DIL = 8, 9
N_TAB = N_ALIBI + N_DIL + 1
TAB_W = 3 * P

VEC = {}
N_VEC = place(VEC, ("c", 16), ("ada_b", 96), ("norm_mix", 16), ("norm_ffn", 16), ("norm_2", 16), ("mem_norm", 16),
              ("fox_b", FOX), ("lam", 4 * DH), ("subln", 128), ("cmp_pos", 2 * CMP_LEN), ("cmp_w2", 2 * DH))

FD_Q, NSA_Q, DIFF_Q, FD_K, DIFF_K, CMPK, CMPV, SLCK, WINK = 0, 8, 12, 16, 24, 28, 29, 30, 31
V_FD, V_SLC, V_WIN, V_DIFF, V_GATE, V_FOXF = 0, 1024, 1152, 1280, 1792, 1816
PAIRS = ([("fd", t, FD_Q + t, FD_K + t) for t in range(8)] + [("slc", t, NSA_Q + t, SLCK) for t in range(4)]
         + [("win", t, NSA_Q + t, WINK) for t in range(4)] + [("cmp", t, NSA_Q + t, None) for t in range(4)]
         + [("diff", t, DIFF_Q + t, DIFF_K + t) for t in range(4)])
NPAIR = len(PAIRS)
GROUPS = [range(0, 4), range(4, 8), range(8, 12), range(12, 16), range(16, 20), range(20, 22), range(22, 24)]
GROUP_OF = {p: g for g, r in enumerate(GROUPS) for p in r}


def table_of(kind, t, j):
    if kind == "fd":
        n = 2 * t + j
        return N_ALIBI + N_DIL if n < FOX else N_ALIBI + n - FOX
    if kind == "diff":
        return 2 * t + 1
    return t + 4 * j


def value_of(kind, t, j):
    if kind == "fd":
        return V_FD + (2 * t + j) * DH, DH
    if kind == "diff":
        return V_DIFF + t * 2 * DH, 2 * DH
    return (V_SLC if kind == "slc" else V_WIN) + j * DH, DH


def constants():
    c = np.zeros((P, N_CONST), np.float32)
    a, n = CONST["ident"]; c[:, a:a + n] = np.eye(P)
    a, n = CONST["ones"]; c[:, a:a + n] = 1
    a, n = CONST["tri"]; c[:, a:a + n] = np.triu(np.ones((P, P)))
    a, n = CONST["valid"]; c[:, a] = np.arange(P) >= CMP_LEN - 1; c[:, a + 1] = 1
    q = np.arange(SEQ)[:, None]
    k = np.arange(SEQ)[None]
    dist = (q - k).astype(np.float32)
    tabs = np.zeros((N_TAB, SEQ, SEQ), np.float32)
    for i in range(N_ALIBI):
        tabs[i] = np.where(dist >= 0, -np.float32(2.0 ** (-(i + 1))) * dist, NEG)
    for i in range(DIL):
        window, dil = ((128, 1), (512, 4), (2048, 16))[i // 3]
        ok = (dist >= 0) & (dist % dil == 0) & (dist <= window)
        tabs[N_ALIBI + i] = np.where(ok, -np.float32(2.0 ** (-8.0 * (i + 1) / DIL)) * dist, NEG)
    tabs[N_TAB - 1] = np.where(dist >= 0, 0, NEG)
    t = np.zeros((P, N_TAB, TAB_W), np.float32)
    t[:, :, :P] = tabs[:, :P, :P].transpose(1, 0, 2)
    t[:, :, P:] = tabs[:, P:, :].transpose(1, 0, 2)
    end = np.arange(N_CMP) * CMP_STRIDE + CMP_LEN - 1
    dc = (np.arange(SEQ)[:, None] - end[None]).astype(np.float32)
    cmp = np.stack([np.where(dc >= 0, -np.float32(2.0 ** (-(i + 1))) * dc, NEG) for i in range(8)])
    cmp = cmp.reshape(8, TT, P, N_CMP).transpose(2, 0, 1, 3).reshape(P, -1)
    return c, np.concatenate([t.reshape(P, -1), cmp], 1).astype(np.float32)


def tiles(w):
    k, n = w.shape
    return w.reshape(k // P, P, n // CH, CH).transpose(2, 1, 0, 3).reshape(n // CH, P, -1)


def cols(v):
    return v.reshape(-1, P).T


def rows(v):
    return np.broadcast_to(v.reshape(1, -1), (P, v.size))


def w_in_columns():
    names = (("fox_q", 448), ("fox_k", 448), ("fox_v", 448), ("fox_f", 7), ("nsa_q", 512), ("cmp_k", 128),
             ("cmp_v", 128), ("slc_k", 128), ("slc_v", 128), ("win_k", 128), ("win_v", 128), ("gate", 24),
             ("dil_q", 576), ("dil_k", 576), ("dil_v", 576), ("diff_q", 512), ("diff_k", 512), ("diff_v", 512))
    at, r = 0, {}
    for name, n in names:
        r[name] = np.arange(at, at + n)
        at += n
    pair = np.array([0, 4, 1, 5, 2, 6, 3, 7])
    order = [r["fox_q"], r["dil_q"], r["nsa_q"].reshape(8, 64)[pair].ravel(), r["diff_q"],
             r["fox_k"], r["dil_k"], r["diff_k"], r["cmp_k"], r["cmp_v"], r["slc_k"], r["win_k"],
             r["fox_v"], r["dil_v"], r["slc_v"], r["win_v"], r["diff_v"],
             r["gate"].reshape(8, 3)[pair].T.ravel(), r["fox_f"]]
    order = np.concatenate(order)
    return np.concatenate([order, np.full(12 * CH - order.size, -1)])


def w_out_rows():
    pair = np.array([0, 4, 1, 5, 2, 6, 3, 7])
    nsa = 448 + np.arange(512).reshape(8, 64)[pair].ravel()
    return np.concatenate([np.arange(448), 960 + np.arange(576), nsa, 1536 + np.arange(512)])


def take(w, columns):
    padded = np.concatenate([w, np.zeros((w.shape[0], 1), w.dtype)], 1)
    return padded[:, columns]


class Steps:

    def __init__(self, engine, semaphore, start=0):
        self.engine, self.semaphore, self.n = engine, semaphore, start

    def __call__(self, instruction):
        instruction.then_inc(self.semaphore, 1)
        self.n += 1
        return self.n

    def wait(self):
        self.engine.wait_ge(self.semaphore, self.n)


def hybrid_blocks(nc, A, out, debug=None, stop=None):
    ctx = ExitStack()
    with ctx:
        def sb(name, *shape):
            return ctx.enter_context(nc.sbuf_tensor(name, [P, *shape], F32))

        def sem(name):
            return ctx.enter_context(nc.semaphore(name))

        Wb = sb("weights", 2, LOAD)
        xT = sb("xT", KT, SEQ)
        h = sb("h", TT, D)
        xn = sb("xn", TT, D)
        arena = sb("arena", 22000)
        cst = sb("cst", N_CONST)
        misc = sb("misc", 870)
        psum = ctx.enter_context(nc.psum_tensor("psum", [P, 8, CH], F32))
        ACC, TRB, OB = 0, 4, 6

        def W(slot):
            return Wb[:, slot].rearrange("p (k n) -> p k n", n=CH)

        def const(name):
            a, n = CONST[name]
            return cst[:, a:a + n]

        ident, ones, tri = const("ident"), const("ones"), const("tri")

        used_misc = [0]

        def small(n):
            a = used_misc[0]
            used_misc[0] += n
            assert used_misc[0] <= 870, used_misc[0]
            return misc[:, a:a + n]

        qk = arena[:, 0:8192].rearrange("p (t s) -> p t s", s=SEQ)
        tm = arena[:, 8192:12288].rearrange("p (m n) -> p m n", m=TT)
        tabs = arena[:, 12288:12288 + N_TAB * TAB_W].rearrange("p (t w) -> p t w", w=TAB_W)
        at = 12288 + N_TAB * TAB_W
        cmp_tabs = arena[:, at:at + 8 * TT * N_CMP].rearrange("p (h m c) -> p h m c", h=8, m=TT)
        at += 8 * TT * N_CMP
        prob = arena[:, at:at + 1024].rearrange("p (b j k) -> p b j k", b=2, j=2)
        probT = arena[:, at + 1024:at + 2048].rearrange("p (b j k) -> p b j k", b=2, j=2)
        blk = arena[:, at:at + 2 * CMP_LEN * N_CMP].rearrange("p (v l c) -> p v l c", v=2, l=CMP_LEN)
        at += 2048
        ada_acc = arena[:, at:at + CH]
        at += CH
        assert at <= 22000, at
        cmp_w1 = xn[:].rearrange("p m n -> p (m n)").rearrange("p (v l e) -> p v l e", v=2, l=CMP_LEN)
        o = xn
        vec = sb("vec", 16 + 96 + 64 + FOX + 256 + 128 + 64 + 128)

        def v_(name):
            a, n = VEC[name]
            return vec[:, a:a + n]

        hT = arena[:, 0:KF * SEQ].rearrange("p (k s) -> p k s", s=SEQ)
        silu_g = arena[:, KF * SEQ:KF * SEQ + 1024]
        sig_g = arena[:, KF * SEQ + 1024:KF * SEQ + 2048]
        g_row = arena[:, 14336:14336 + D]
        g_tmp = arena[:, 16384:16384 + 1024].rearrange("p (m n) -> p m n", m=TT)
        diag = arena[:, 18432:18432 + 2048].rearrange("p (k n) -> p k n", n=P)

        c_act, mod, scale_col = small(16), small(96), small(16)
        stat, rstd = small(2), small(2)
        sums = small(2 * NPAIR * TT).rearrange("p (m i) -> p m i", m=TT)
        nmax = small(2 * NPAIR * TT).rearrange("p (m i) -> p m i", m=TT)
        fac = small(2 * NPAIR * TT).rearrange("p (m i) -> p m i", m=TT)
        gate = small(48).rearrange("p (m i) -> p m i", m=TT)
        logf = small(TT * FOX).rearrange("p (m i) -> p m i", m=TT)
        fz = small(TT * FOX).rearrange("p (m i) -> p m i", m=TT)
        fe = small(TT * FOX).rearrange("p (m i) -> p m i", m=TT)
        dil_e = small(DIL)
        dil_m = small(6)
        lam = small(4)
        kcT = small(N_CMP)
        vc = small(2 * DH).rearrange("p (g d) -> p g d", g=2)
        ada_tmp = sb("ada_tmp", CH)
        cz = ada_tmp[:, 0:6 * 4 * N_CMP].rearrange("p (n g v c) -> p n g v c", n=6, g=2, v=2)
        diff_ss = small(TT * DIFF).rearrange("p (m i) -> p m i", m=TT)
        crow = xT[0:1].rearrange("p k s -> p (k s)")[:, 0:2 * FOX * SEQ].rearrange("p (a h s) -> p a h s", a=2, h=FOX)

        S = {n: sem(n) for n in (
            "x_in", "const_in", "loaded0", "loaded1", "used0", "used1", "acc_free",
            "dve_step", "act_step", "ada_step", "ada_sum", "mod_ready",
            "c_exp", "stat_ready", "root_ready", "norm_ready", "tr_ready", "tr_free", 
            "tabs_in", "w1_in", "gate_exp", "gate_done", "f_abs", "f_ln", "logf_ready",
            "crow_sum", "crow_ready", "ncrow_ready",
            "blk_ready", "cmp_hidden", "cmp_exp_in", "cmp_exp", "gelu_ready", "cmp_out", "kc_ready",
            "scores", "scored", "exps", "pt_sum", "pt_ready", "pv", "pv_read", "dil_in", "dil_exp",
            "lam_in", "lam_exp", "o_ready", "diff_in", "g_diag", "g_sum", "g_row_ready",
            "h_ready", "out_stored",
            "final_in", "mem_in", "gain_in", "lora_in", "bias_in", "bcst_in", "row_in0", "row_in1", "row_in2",
            "row_in3", "row_in4", "shift_in0", "shift_in1", "shift_in2", "zero_row", "lerp", "w0_used",
            "a0_used", "pre_done", "masks_in", "x1_ready", "hroot_in", "hroot", "lora_sum", "lora_raw", "lora_lerp",
            "lora_ready", "head_ready", "z_used", "zw_in", "zw", "za_in", "za", "cum_sum", "c_end", "x2_free",
            "e_pos", "e_ex_in", "e_ex", "e_neg", "bt_sum", "bt", "p_sum", "p_mat", "y_sum", "y_mat", "ux_sum", "ux",
            "wz_sum", "wz", "yb_ready", "x2_done", "lora_out", "logw", "qt", "state", "o2", "g_prod", "l_mask", "dd",
            "dd_sum", "o1_sum", "qt_sum", "st_sum", "o2_sum", "up_half", "merged", "g_mask")
            + (("dbg", "out_stored2") if debug else ())}
        s_ = S
        LOADED, USED = [S["loaded0"], S["loaded1"]], [S["used0"], S["used1"]]
        block = ctx.enter_context(nc.Block())

        def wait_load(e, load):
            e.wait_ge(LOADED[load % 2], 16 * (load // 2 + 1))

        def wait_used(e, load):
            e.wait_ge(USED[load % 2], load // 2 + 1)

        small0 = small(2)
        DIL_AT = [qt * NPAIR + GROUPS[1][-1] + 3 for qt in range(TT)]

        def keys(n):
            qt, p = divmod(n, NPAIR)
            return N_CMP if PAIRS[p][0] == "cmp" else P * (qt + 1)

        AH, CHD, BH = 8, 4, 16
        W3 = 1024

        def tokens(at, n=W3):
            return arena[:, at:at + TT * n].rearrange("p (m n) -> p m n", m=TT)

        def tiles_at(at, n):
            return arena[:, at:at + n * SEQ].rearrange("p (t s) -> p t s", s=SEQ)

        R0 = 3 * TT * W3
        y_a, y_c, y_b = tokens(0), tokens(TT * W3), tokens(2 * TT * W3)
        mem_x, mem_kv, c_q = tokens(R0 + 10240, D), tokens(R0, D), tokens(R0 + 4096)
        c_qT, c_kT = tiles_at(R0 + 6144, 8), tiles_at(R0 + 8192, 8)
        prob2 = arena[:, R0 + 10240:R0 + 11264].rearrange("p (b j k) -> p b j k", b=2, j=2)
        prob2T = arena[:, R0 + 11264:R0 + 12288].rearrange("p (b j k) -> p b j k", b=2, j=2)
        final_row = arena[:, 14336:14336 + D]
        c_gain = vec[:, 176:176 + 512].rearrange("p (a d) -> p a d", a=2)
        a_gain = ada_tmp[:, 0:256].rearrange("p (a d) -> p a d", a=2)
        mu_wa = vec[:, 700:701]
        a_qk, a_v = tokens(R0, D), tokens(R0 + 4096)
        a_qT, a_kT = tiles_at(R0 + 6144, 8), tiles_at(R0 + 8192, 8)
        a_bias = arena[:, R0 + 12288:R0 + 12288 + AH * TAB_W].rearrange("p (h w) -> p h w", w=TAB_W)
        b_r, b_k, b_v = tokens(R0), tokens(R0 + 2048), tokens(R0 + 4096)
        b_a, b_b = tokens(R0 + 6144), tokens(R0 + 8192)
        row_slot = [arena[:, R0 + 10240 + s * W3:R0 + 10240 + (s + 1) * W3] for s in range(5)]
        silu_z = arena[:, R0 + 8192:R0 + 8192 + W3]
        silu_zb = row_slot[2]
        X1 = xn[:].rearrange("p m n -> p (m n)")[:, 0:2048].rearrange("p (m n) -> p m n", m=TT)
        X2 = xn[:].rearrange("p m n -> p (m n)")[:, 2048:4096].rearrange("p (m n) -> p m n", m=TT)
        lora_w = xn[:].rearrange("p m n -> p (m n)")[:, 0:2048].rearrange("p (k n) -> p k n", k=KT)
        lora = ada_tmp[:, 256:512]
        lora_d = arena[:, R0 + 15360:R0 + 15360 + SEQ]
        c_end = arena[:, R0 + 15616:R0 + 15616 + 32].rearrange("p (t c) -> p t c", t=8)
        AR = row_slot[0][:, 0:512].rearrange("p (m n) -> p m n", m=TT)
        BK = row_slot[0][:, 512:1024].rearrange("p (a s) -> p a s", a=2)
        WZ = row_slot[1][:, 0:512].rearrange("p (c a n) -> p c a n", c=4, a=2)
        ST = row_slot[1][:, 512:512 + 192].rearrange("p (c n) -> p c n", c=3)
        S_tmp = row_slot[1][:, 704:768]
        lev = row_slot[2][:, 0:768].rearrange("p (l n) -> p l n", l=6)
        XF = xn[:].rearrange("p m n -> p (m n)")
        Gs = XF[:, 0:2048].rearrange("p (u a n) -> p u a n", u=4, a=4)
        DD = XF[:, 2048:3072].rearrange("p (u a n) -> p u a n", u=4, a=2)
        Pm = XF[:, 3072:3584].rearrange("p (u n) -> p u n", u=4)
        Lm = XF[:, 3584:4096].rearrange("p (u n) -> p u n", u=4)
        Yb = XF[:, 3584:3840].rearrange("p (u n) -> p u n", u=4)
        UX = XF[:, 3072:3584].rearrange("p (u n) -> p u n", u=4)
        gmask = ada_tmp[:].rearrange("p (a n) -> p a n", a=4)
        b_cst = vec[:, 176:176 + 130]
        btri, bind = b_cst[:, 0:P], b_cst[:, P:P + 2]
        hs = small(96).rearrange("p (a m h) -> p a m h", a=3, m=TT)
        hs_a, hs_r, bonus = hs[:, 0], hs[:, 1], hs[:, 2]
        gates_ = arena[:, R0:R0 + TT * 6144].rearrange("p (m n) -> p m n", m=TT)
        yT = [xT[:, 0:8], xT[:, 8:16], tiles_at(R0 + 12288, 8)]
        up_tmp = ada_tmp

        def units(first, pairs):
            return [(first + i, i // pairs, i % pairs) for i in range(TT * pairs)]

        U0 = TT * NPAIR
        C_UNITS = units(U0, CHD // 2)
        A_UNITS = units(U0 + len(C_UNITS), AH // 2)
        G0 = TT * len(GROUPS) - U0

        def pool_block2(pool):
            if stop == "block1":
                pool.wait_ge(s_["h_ready"], 8)
                pool.dma_start(debug["h"].rearrange("(m p) n -> p m n", p=P), h[:]).then_inc(s_["out_stored"], 16)
                pool.wait_ge(s_["out_stored"], 16)
                return

            def repeated(dst, name, i=0, n=W3):
                return pool.dma_start(dst, A[name][i:i + 1, 0:n].broadcast_to([P, n]))

            pool.wait_ge(s_["h_ready"], 8)
            repeated(final_row, "final_g", 0, D).then_inc(s_["final_in"], 16)
            pool.dma_start(mem_x, A["mem"].rearrange("(m p) n -> p m n", p=P)).then_inc(s_["mem_in"], 16)
            pool.dma_start(vec[:, 176:176 + 512], A["vec2"][:, 0:512]).then_inc(s_["gain_in"], 16)
            pool.dma_start(ada_tmp[:, 0:256], A["vec2"][:, 512:768]).then_inc(s_["gain_in"], 16)
            pool.dma_start(mu_wa, A["vec2"][:, 768:769], allow_slow_non_contiguous=True).then_inc(s_["gain_in"], 16)
            pool.wait_ge(s_["tr_free"], 4 * 8 + 8)
            pool.dma_start(lora_w, A["lora_w"]).then_inc(s_["lora_in"], 16)
            pool.wait_ge(s_["pv"], C_UNITS[-1][0] + 1)
            pool.dma_start(a_bias.rearrange("p h w -> p (h w)"), A["a_bias"]).then_inc(s_["bias_in"], 16)
            pool.wait_ge(s_["pv_read"], G0 + A_UNITS[-1][0] + 1)
            pool.dma_start(b_cst, A["b_cst"]).then_inc(s_["bcst_in"], 16)
            pool.dma_start(row_slot[3], A["w2a2"]).then_inc(s_["row_in3"], 16)
            for slot, i in ((0, 0), (1, 1), (2, 2), (4, 3)):
                repeated(row_slot[slot], "b_rows", i).then_inc(s_[f"row_in{slot}"], 16)
            for i, (src, dst) in enumerate(((b_r, X1), (b_k, X2), (b_v, X1))):
                pool.wait_ge(s_["acc_free"], FIRST_ACC["b_in"] + 2 * i + 4)
                if i == 0:
                    pool.wait_ge(s_["lora_sum"], 1)
                    pool.memset(X1[0:1, 0], 0.0).then_inc(s_["zero_row"], 1)
                    pool.memset(X2[0:1, 0], 0.0).then_inc(s_["zero_row"], 1)
                if i == 2:
                    pool.wait_ge(s_["lerp"], 1)
                    pool.memset(X1[0:1, 0], 0.0).then_inc(s_["zero_row"], 1)
                pool.dma_start(dst[1:P, 0], src[0:P - 1, 0]).then_inc(s_[f"shift_in{i}"], 16)
                pool.dma_start(dst[1:P, 1], src[0:P - 1, 1]).then_inc(s_[f"shift_in{i}"], 16)
                pool.dma_start(dst[0:1, 1], src[P - 1:P, 0]).then_inc(s_[f"shift_in{i}"], 16)
            pool.wait_ge(s_["lerp"], 3)
            for slot, i in ((0, 5), (1, 6), (2, 7)):
                repeated(row_slot[slot], "b_rows", i).then_inc(s_[f"row_in{slot}"], 16)
            pool.wait_ge(s_["w0_used"], 1)
            repeated(row_slot[4], "b_rows", 4).then_inc(s_["row_in4"], 16)
            pool.wait_ge(s_["a0_used"], 1)
            repeated(row_slot[3], "b_rows", 8).then_inc(s_["row_in3"], 16)
            repeated(row_slot[4], "b_rows", 9).then_inc(s_["row_in4"], 16)
            pool.wait_ge(s_["pre_done"], 1)
            pool.dma_start(lev.rearrange("p l n -> p (l n)"), A["masks"][:, 512:1280]).then_inc(s_["masks_in"], 16)
            pool.dma_start(ada_tmp[:], A["masks"][:, 0:512]).then_inc(s_["masks_in"], 16)
            if debug:
                for i, (name, ap, w) in enumerate((("ya", y_a, W3), ("yc", y_c, W3), ("yb", y_b, W3))):
                    pool.wait_ge(s_["dbg"], 1)
                    pool.dma_start(debug[name].rearrange("(m p) n -> p m n", p=P), ap).then_inc(s_["out_stored2"], 16)
                    pool.wait_ge(s_["out_stored2"], 16 * i + 16)
                pool.memset(small0, 0.0).then_inc(s_["dbg"], 1)

        def act_block2(act, step, copy, square_sums, read_transposes):
            if stop == "block1":
                return
            A_ = nc.scalar.activation
            act.wait_ge(s_["h_ready"], 8)
            square_sums(h, 2)
            act.wait_ge(s_["mem_in"], 16)
            act.wait_ge(s_["x1_ready"], 2)
            square_sums(mem_x, 3)
            read_transposes(KT, v_("mem_norm"))
            square_sums(h, 4)

            def read_tokens(name, dst, first=0, count=None):
                base, n = PLAN[name]
                base, n = base + first, (n if count is None else count)
                for i in range(n):
                    wait_used(act, base + i)
                    copy(dst[:, :, i * CH:(i + 1) * CH], psum[:, 2 * (i % 2):2 * (i % 2) + 2])\
                        .then_inc(s_["acc_free"], 1)

            def head_roots(n):
                act.wait_ge(s_["hroot_in"], n + 1)
                A_(hs_a, hs_a, ACT.Sqrt).then_inc(s_["hroot"], 1)

            def unit_exps(n, qt, t, from_psum):
                act.wait_ge(s_["scored"], n + 1)
                if n - U0 >= 2 and from_psum:
                    act.wait_ge(s_["pt_sum"], n - 1)
                for j in range(2):
                    nk = SEQ if from_psum else P * (qt + 1)
                    src = psum[:, 2 * (n % 2) + j, 0:nk] if from_psum else prob2[:, n % 2, j, 0:nk]
                    A_(prob2[:, n % 2, j, 0:nk], src, ACT.Exp, bias=nmax[:, qt, 2 * t + j:2 * t + j + 1],
                       accum_out=sums[:, qt, 2 * t + j:2 * t + j + 1]).then_inc(s_["exps"], 1)

            def unit_probT(n, qt, from_psum):
                nk = SEQ if from_psum else P * (qt + 1)
                act.wait_ge(s_["pt_sum"], n + 1)
                act.wait_ge(s_["pv"], n - 1)
                copy(prob2T[:, n % 2, :, 0:nk], psum[:, TRB].rearrange("p (j k) -> p j k", j=2)[:, :, 0:nk])\
                    .then_inc(s_["pt_ready"], 1)

            def attention(list_, from_psum):
                for i in range(len(list_) + 1):
                    if i < len(list_):
                        unit_exps(*list_[i], from_psum)
                    if i:
                        unit_probT(*list_[i - 1][:2], from_psum)

            read_tokens("mem", mem_kv)
            read_transposes(KT, v_("norm_2"))
            act.wait_ge(s_["lora_sum"], 1)
            copy(lora, psum[:, OB, 0:SEQ]).then_inc(s_["lora_raw"], 1)
            act.wait_ge(s_["lora_lerp"], 1)
            A_(lora[0:DH], lora[0:DH], ACT.Tanh).then_inc(s_["lora_ready"], 1)
            read_tokens("c_q", c_q)
            head_roots(0)
            act.wait_ge(s_["head_ready"], 1)
            read_transposes(8, dst=c_qT, factor=256 ** -0.5)
            head_roots(1)
            act.wait_ge(s_["head_ready"], 2)
            read_transposes(8, dst=c_kT)
            attention(C_UNITS, True)
            act.wait_ge(s_["pv"], C_UNITS[-1][0] + 1)
            read_tokens("a_qk", a_qk)
            read_tokens("a_v", a_v)
            head_roots(2)
            read_transposes(8, dst=a_qT, factor=128 ** -0.5)
            head_roots(3)
            read_transposes(8, dst=a_kT)
            attention(A_UNITS, False)
            act.wait_ge(s_["pv_read"], G0 + A_UNITS[-1][0] + 1)
            for i, dst in enumerate((b_r, b_k, b_v)):
                read_tokens("b_in", dst, 2 * i, 2)
            for i in range(4):
                wait_used(act, PLAN["z_in"][0] + i)
                if i:
                    act.wait_ge(s_["z_used"], i)
                A_(silu_z, psum[:, 2 * (i % 2):2 * (i % 2) + 2].rearrange("p b n -> p (b n)"), ACT.Silu)\
                    .then_inc(s_["acc_free"], 1)
            act.wait_ge(s_["zw_in"], 1)
            A_(X1, X1, ACT.Tanh, scale=0.5).then_inc(s_["zw"], 1)
            act.wait_ge(s_["za_in"], 1)
            A_(b_b, b_b, ACT.Tanh, scale=0.5).then_inc(s_["za"], 1)
            act.wait_ge(s_["hroot_in"], 5)
            A_(hs_a, hs_a, ACT.Sqrt).then_inc(s_["hroot"], 1)
            cum = psum[:, 0:4].rearrange("p (m b) n -> p m (b n)", m=TT)
            act.wait_ge(s_["cum_sum"], 1)
            A_(c_end.rearrange("p t c -> p (t c)"), psum[:, OB, 0:32], ACT.Exp).then_inc(s_["c_end"], 1)
            act.wait_ge(s_["x2_free"], 1)
            A_(X2, cum, ACT.Exp).then_inc(s_["e_pos"], 1)
            act.wait_ge(s_["e_ex_in"], 1)
            A_(X2, X2, ACT.Exp).then_inc(s_["e_ex"], 1)
            act.wait_ge(s_["x2_free"], 2)
            A_(X2, cum, ACT.Exp, scale=-1.0).then_inc(s_["e_neg"], 1)
            for t in range(8):
                for r, dst in enumerate((AR.rearrange("p m n -> p (m n)"), BK.rearrange("p a n -> p (a n)"))):
                    act.wait_ge(s_["bt_sum"], 2 * t + r + 1)
                    if r == 0 and t:
                        act.wait_ge(s_["o2_sum"], t)
                    copy(dst, psum[:, 4 + r]).then_inc(s_["bt"], 1)
                for l in range(6):
                    act.wait_ge(s_["p_sum"], 6 * t + l + 1)
                    copy(Pm.rearrange("p u n -> p (u n)"), psum[:, 4]).then_inc(s_["p_mat"], 1)
                act.wait_ge(s_["y_sum"], t + 1)
                copy(Yb.rearrange("p u n -> p (u n)"), psum[:, 7, 0:256]).then_inc(s_["y_mat"], 1)
                act.wait_ge(s_["ux_sum"], t + 1)
                copy(UX.rearrange("p u n -> p (u n)"), psum[:, 4]).then_inc(s_["ux"], 1)
                act.wait_ge(s_["wz_sum"], t + 1)
                for c in range(4):
                    ins = copy(WZ[:, c].rearrange("p a n -> p (a n)"),
                               psum[:, c % 2, (c // 2) * P:(c // 2 + 1) * P])
                ins.then_inc(s_["wz"], 1)
            act.wait_ge(s_["hroot_in"], 6)
            A_(hs_a, hs_a, ACT.Sqrt).then_inc(s_["hroot"], 1)
            for i in range(4, 6):
                wait_used(act, PLAN["z_in"][0] + i)
                if i == 5:
                    act.wait_ge(s_["z_used"], 5)
                else:
                    act.wait_ge(s_["yb_ready"], 1)
                A_(silu_zb, psum[:, 2 * (i % 2):2 * (i % 2) + 2].rearrange("p b n -> p (b n)"), ACT.Silu)\
                    .then_inc(s_["acc_free"], 1)
            act.wait_ge(s_["z_used"], 6)
            base = PLAN["gates"][0]
            with act.Fori(0, 6) as i:
                for s in range(2):
                    act.wait_ge(USED[s], i + base // 2 + 1)
                    A_(gates_[:, :, bass.ds(i * 1024 + s * CH, CH)], psum[:, 2 * s:2 * s + 2], ACT.Sigmoid)\
                        .then_inc(s_["acc_free"], 1)
            for b in range(3):
                read_transposes(8, dst=yT[b])
            read_transposes(KT)
            act.wait_ge(s_["x2_done"], 4)
            act.dma_start(out.rearrange("(m p) n -> p m n", p=P), h[:]).then_inc(s_["out_stored"], 16)

        def pe_block2(pe, transposes, tokens_product, rounds):
            if stop == "block1":
                return
            mm = nc.tensor.matmul

            def attention(list_, scores_of, v_of, from_psum):
                def scores(n, qt, t):
                    if n - U0 >= 2 or list_ is A_UNITS:
                        if from_psum or list_[0][0] + 2 > n:
                            pe.wait_ge(s_["exps"], 2 * (n - 1))
                        else:
                            pe.wait_ge(s_["scored"], n - 1)
                    for j in range(2):
                        ins = scores_of(psum[:, 2 * (n % 2) + j], qt, 2 * t + j)
                    ins.then_inc(s_["scores"], 1)

                def probT(n, qt, t):
                    nk = SEQ if from_psum else P * (qt + 1)
                    pe.wait_ge(s_["exps"], 2 * n + 2)
                    pe.wait_ge(s_["pt_ready"], n)
                    for j in range(2):
                        for a in range(0, nk, P):
                            ins = nc.tensor.transpose(psum[:, TRB, j * SEQ + a:j * SEQ + a + P],
                                                      prob2[:, n % 2, j, a:a + P], ident)
                    ins.then_inc(s_["pt_sum"], 1)

                def values(n, qt, t):
                    nk = SEQ if from_psum else P * (qt + 1)
                    pe.wait_ge(s_["pt_ready"], n + 1)
                    pe.wait_ge(s_["pv_read"], G0 + n - 1)
                    for j in range(2):
                        v, w = v_of(2 * t + j)
                        for m in range(nk // P):
                            ins = mm(psum[:, OB + n % 2, j * w:(j + 1) * w], prob2T[:, n % 2, j, m * P:(m + 1) * P],
                                     v[:, m], start=(m == 0), stop=(m == nk // P - 1))
                    ins.then_inc(s_["pv"], 1)

                for i in range(len(list_) + 2):
                    if i < len(list_):
                        scores(*list_[i])
                    if 1 <= i <= len(list_):
                        probT(*list_[i - 1])
                    if i >= 2:
                        values(*list_[i - 2])

            pe.wait_ge(s_["norm_ready"], 6)
            transposes(xn, KT)
            pe.wait_ge(s_["tr_free"], rounds[0])
            tokens_product("mem")
            pe.wait_ge(s_["norm_ready"], 8)
            transposes(xn, KT)
            pe.wait_ge(s_["tr_free"], rounds[0])
            pe.wait_ge(s_["lora_in"], 16)
            for k in range(KT):
                ins = mm(psum[:, OB, 0:SEQ], lora_w[:, k], xT[:, k], start=(k == 0), stop=(k == KT - 1))
            ins.then_inc(s_["lora_sum"], 1)
            tokens_product("c_q")
            for i, src in enumerate((c_q, mem_kv)):
                pe.wait_ge(s_["head_ready"], i + 1)
                transposes(src, 8)
            pe.wait_ge(s_["tr_free"], rounds[0])

            def c_scores(bank, qt, n):
                for a in range(2):
                    ins = mm(bank[:, 0:SEQ], c_qT[:, 2 * n + a, qt * P:(qt + 1) * P], c_kT[:, 2 * n + a],
                             start=(a == 0), stop=(a == 1))
                return ins

            attention(C_UNITS, c_scores, lambda n: (mem_kv[:, :, W3 + n * 256:W3 + (n + 1) * 256], 256), True)
            tokens_product("a_qk")
            tokens_product("a_v")
            for i in range(2):
                pe.wait_ge(s_["head_ready"], i + 3)
                transposes(a_qk[:, :, i * W3:(i + 1) * W3], 8)
            pe.wait_ge(s_["tr_free"], rounds[0])

            def a_scores(bank, qt, n):
                nk = P * (qt + 1)
                return mm(bank[:, 0:nk], a_qT[:, n, qt * P:(qt + 1) * P], a_kT[:, n, 0:nk], start=True, stop=True)

            attention(A_UNITS, a_scores, lambda n: (a_v[:, :, n * P:(n + 1) * P], P), False)
            tokens_product("b_in")
            tokens_product("z_in", 0, 4)
            pe.wait_ge(s_["acc_free"], FIRST_ACC["z_in"] + 4 + 2)
            pe.wait_ge(s_["row_in3"], 16)
            pe.wait_ge(s_["lora_ready"], 1)
            for a in range(2):
                r = slice(a * DH, (a + 1) * DH)
                for m in range(TT):
                    for c in range(2):
                        ins = mm(psum[:, 4 * a + 2 * m + c], lora[r, m * P:(m + 1) * P],
                                 row_slot[3][r, c * CH:(c + 1) * CH], start=True, stop=True)
                ins.then_inc(s_["lora_out"], 1)
            pe.wait_ge(s_["logw"], 1)
            pe.wait_ge(s_["bcst_in"], 16)
            for m in range(TT):
                for t in range(8):
                    mm(psum[:, OB, t * 4 + 2 * m:t * 4 + 2 * m + 2], X1[:, m, t * P:(t + 1) * P], bind,
                       start=True, stop=True)
            for m in range(TT):
                for c in range(2):
                    ins = mm(psum[:, 2 * m + c], btri, X1[:, m, c * CH:(c + 1) * CH], start=True, stop=True)
            ins.then_inc(s_["cum_sum"], 1)
            pe.wait_ge(s_["pre_done"], 1)
            for t in range(8):
                cs = slice(t * P, (t + 1) * P)
                if t:
                    pe.wait_ge(s_["wz"], t)
                    pe.wait_ge(s_["qt"], t)
                for r, order in enumerate((((b_a, 0), (b_r, 0), (b_a, 1), (b_r, 1)),
                                           ((b_b, 0), (b_b, 1), (b_k, 0), (b_k, 1)))):
                    for i, (src, m) in enumerate(order):
                        ins = nc.tensor.transpose(psum[:, 4 + r, i * P:(i + 1) * P], src[:, m, cs], ident)
                    ins.then_inc(s_["bt_sum"], 1)
                pe.wait_ge(s_["bt"], 2 * t + 2)
                if t:
                    pe.wait_ge(s_["state"], 3 * t)
                    pe.wait_ge(s_["o2"], t)
                for u in range(4):
                    r = slice((u // 2) * DH, (u // 2 + 1) * DH)
                    m = u % 2
                    for a in range(2):
                        ins = mm(psum[:, u, a * 256:(a + 1) * 256], BK[r, a, m * P:(m + 1) * P], AR[r, m],
                                 start=True, stop=True)
                ins.then_inc(s_["g_prod"], 1)
                for l in range(6):
                    pe.wait_ge(s_["l_mask"], 6 * t + l + 1)
                    pe.wait_ge(s_["dd"], 7 * t + l + 1)
                    for u in range(4):
                        ins = mm(psum[:, 4, u * P:(u + 1) * P], Lm[:, u], DD[:, u, 0], start=True, stop=True)
                    ins.then_inc(s_["p_sum"], 1)
                    pe.wait_ge(s_["p_mat"], 6 * t + l + 1)
                    for u in range(4):
                        bank = psum[:, 5 + u // 2]
                        o_ = (u % 2) * 256
                        mm(bank[:, o_:o_ + P], DD[:, u, 1], Pm[:, u], start=True, stop=True)
                        ins = mm(bank[:, o_ + P:o_ + 256], Pm[:, u], DD[:, u, 1], start=True, stop=True)
                    ins.then_inc(s_["dd_sum"], 1)
                for u in range(4):
                    hc = slice(t * P + (u // 2) * DH, t * P + (u // 2 + 1) * DH)
                    ins = mm(psum[:, 7, u * DH:(u + 1) * DH], Gs[:, u, 2], b_v[:, u % 2, hc], start=True, stop=True)
                ins.then_inc(s_["y_sum"], 1)
                pe.wait_ge(s_["dd"], 7 * t + 7)
                pe.wait_ge(s_["y_mat"], t + 1)
                for u in range(4):
                    hc = slice(t * P + (u // 2) * DH, t * P + (u // 2 + 1) * DH)
                    mm(psum[:, 4, u * P:u * P + DH], DD[:, u, 1], Yb[:, u], start=True, stop=True)
                    ins = mm(psum[:, 4, u * P + DH:(u + 1) * P], DD[:, u, 1], b_a[:, u % 2, hc], start=True, stop=True)
                ins.then_inc(s_["ux_sum"], 1)
                pe.wait_ge(s_["ux"], t + 1)
                for u in range(4):
                    hc = slice(t * P + (u // 2) * DH, t * P + (u // 2 + 1) * DH)
                    mm(psum[:, 7, u * DH:(u + 1) * DH], Gs[:, u, 1], UX[:, u, 0:DH], start=True, stop=False)
                    ins = mm(psum[:, 7, u * DH:(u + 1) * DH], Gs[:, u, 3], b_v[:, u % 2, hc], start=False, stop=True)
                ins.then_inc(s_["o1_sum"], 1)
                for u in range(4):
                    r = slice((u // 2) * DH, (u // 2 + 1) * DH)
                    ins = mm(psum[r, 5, (u % 2) * P:(u % 2 + 1) * P], UX[:, u, DH:P], Gs[:, u, 1],
                             start=True, stop=True)
                ins.then_inc(s_["qt_sum"], 1)
                for c2 in range(2):
                    kr = slice(c2 * DH, (c2 + 1) * DH)
                    for u in range(4):
                        m = u % 2
                        hc = slice(t * P + (u // 2) * DH, t * P + (u // 2 + 1) * DH)
                        r = slice((u // 2) * DH, (u // 2 + 1) * DH)
                        at = m * P
                        mm(psum[r, c2, at:at + DH], UX[kr, u, DH:P], b_b[kr, m, hc], start=True, stop=True)
                        mm(psum[r, c2, at + DH:at + P], b_b[kr, m, hc], UX[kr, u, 0:DH], start=True, stop=False)
                        ins = mm(psum[r, c2, at + DH:at + P], b_k[kr, m, hc], b_v[kr, m, hc], start=False, stop=True)
                ins.then_inc(s_["wz_sum"], 1)
                pe.wait_ge(s_["wz"], t + 1)
                for c in range(1, 3):
                    pe.wait_ge(s_["state"], 3 * t + c)
                    for h2 in range(2):
                        r = slice(h2 * DH, (h2 + 1) * DH)
                        ins = mm(psum[r, 2, c * DH:(c + 1) * DH], WZ[r, c, 0], ST[r, c - 1], start=True, stop=True)
                    ins.then_inc(s_["st_sum"], 1)
                pe.wait_ge(s_["state"], 3 * t + 3)
                pe.wait_ge(s_["qt"], t + 1)
                pe.wait_ge(s_["dd"], 7 * t + 7)
                for h2 in range(2):
                    r = slice(h2 * DH, (h2 + 1) * DH)
                    for c in range(1, 4):
                        kr = slice((c % 2) * DH, (c % 2 + 1) * DH)
                        ins = mm(psum[kr, (6, 3)[h2], (c // 2) * DH:(c // 2 + 1) * DH],
                                 AR[r, c // 2, P + (c % 2) * DH:P + (c % 2 + 1) * DH], ST[r, c - 1],
                                 start=True, stop=True)
                ins.then_inc(s_["o2_sum"], 1)
            pe.wait_ge(s_["state"], 24)
            pe.wait_ge(s_["o2"], 8)
            tokens_product("z_in", 4, 2)
            tokens_product("gates")
            pe.wait_ge(s_["z_used"], 6)
            for y in (y_a, y_b, y_c):
                transposes(y, 8)
            pe.wait_ge(s_["tr_free"], rounds[0])
            base, acc = PLAN["ups"][0], FIRST_ACC["ups"]
            for i in range(6):
                load = base + i
                wait_load(pe, load)
                for n2 in range(2):
                    pe.wait_ge(s_["acc_free"], acc + 2 * i + n2 + 1)
                    for m in range(TT):
                        for k in range(8):
                            ins = mm(psum[:, 2 * n2 + m], yT[i // 2][:, k, m * P:(m + 1) * P], W(load % 2)[:, 8 * n2 + k],
                                     start=(k == 0), stop=(k == 7))
                    if n2 == 0:
                        ins.then_inc(s_["up_half"], 1)
                ins.then_inc(USED[load % 2], 1)
            pe.wait_ge(s_["merged"], 12)
            transposes(xn, KT)
            pe.wait_ge(s_["tr_free"], rounds[0])
            tokens_product("w_o")

        def dve_block2(dve, step, rms, scale_tokens):
            if stop == "block1":
                return
            V = nc.vector
            rms(2)
            dve.wait_ge(s_["final_in"], 16)
            for m in range(TT):
                V.scalar_tensor_tensor(h[:, m], h[:, m], rstd[:, m:m + 1], final_row, ALU.mult, ALU.mult)\
                    .then_inc(s_["x1_ready"], 1)
            rms(3)
            scale_tokens(mem_x)
            rms(4)
            scale_tokens(h)
            dve.wait_ge(s_["gain_in"], 48)
            dve.wait_ge(s_["lora_raw"], 1)
            step(V.tensor_scalar(lora_d[:, 0:1], lora[:, 0:1], -1.0, None, ALU.mult))
            step(V.tensor_tensor(lora_d[:, 1:SEQ], lora[:, 0:SEQ - 1], lora[:, 1:SEQ], ALU.subtract)); step.wait()
            V.scalar_tensor_tensor(lora, lora_d, mu_wa, lora, ALU.mult, ALU.add).then_inc(s_["lora_lerp"], 1)

            def head_norm(x, heads, gain, n, last, width=None, tmp=X1):
                w = W3 // heads
                xh = x.rearrange("p m (h d) -> p m h d", h=heads)
                th = tmp.rearrange("p m (h d) -> p m h d", h=heads)
                step(V.tensor_tensor(tmp, x, x, ALU.mult)); step.wait()
                step(V.tensor_reduce(hs_r[:, :, 0:heads], th, AX, ALU.add)); step.wait()
                if n == 0:
                    step(V.memset(hs_a, 1.0)); step.wait()
                V.tensor_scalar(hs_a[:, :, 0:heads], hs_r[:, :, 0:heads], 1.0 / w, EPS, ALU.mult, ALU.add)\
                    .then_inc(s_["hroot_in"], 1)
                dve.wait_ge(s_["hroot"], n + 1)
                step(V.reciprocal(hs_r[:, :, 0:heads], hs_a[:, :, 0:heads])); step.wait()
                for m in range(TT):
                    step(V.tensor_tensor(th[:, m], xh[:, m], hs_r[:, m, 0:heads].unsqueeze(2).broadcast_to([P, heads, w]),
                                         ALU.mult))
                step.wait()
                for m in range(TT):
                    ins = V.tensor_tensor(xh[:, m], th[:, m], gain.unsqueeze(1).broadcast_to([P, heads, w]), ALU.mult)
                    if m == 0:
                        step(ins)
                step.wait()
                ins.then_inc(s_["head_ready"], 1)
                dve.wait_ge(s_["head_ready"], n + 1)

            acc = FIRST_ACC["c_q"]
            dve.wait_ge(s_["acc_free"], acc + 4)
            head_norm(c_q, CHD, c_gain[:, 0], 0, False)
            head_norm(mem_kv[:, :, 0:W3], CHD, c_gain[:, 1], 1, False)

            def finish(n, qt, t, w, y):
                dve.wait_ge(s_["pv"], n + 1)
                f = fac[:, qt, 2 * t:2 * t + 2]
                step(V.reciprocal(f, sums[:, qt, 2 * t:2 * t + 2])); step.wait()
                V.tensor_tensor(y[:, qt, 2 * t * w:(2 * t + 2) * w].rearrange("p (j d) -> p j d", j=2),
                                psum[:, OB + n % 2, 0:2 * w].rearrange("p (j d) -> p j d", j=2),
                                f.unsqueeze(2).broadcast_to([P, 2, w]), ALU.mult).then_inc(s_["pv_read"], 1)

            def attention(list_, score, w, y):
                for i in range(len(list_) + 2):
                    if i < len(list_):
                        score(*list_[i])
                    if i >= 2:
                        finish(*list_[i - 2], w, y)

            def c_score(n, qt, t):
                dve.wait_ge(s_["scores"], n + 1)
                V.tensor_reduce(nmax[:, qt, 2 * t:2 * t + 2], psum[:, 2 * (n % 2):2 * (n % 2) + 2, 0:SEQ], AX, ALU.max,
                                negate=True).then_inc(s_["scored"], 1)

            attention(C_UNITS, c_score, 256, y_c)
            dve.wait_ge(s_["acc_free"], FIRST_ACC["a_v"] + 4)
            head_norm(a_qk[:, :, 0:W3], AH, a_gain[:, 0], 2, False)
            head_norm(a_qk[:, :, W3:2 * W3], AH, a_gain[:, 1], 3, False)
            dve.wait_ge(s_["bias_in"], 16)

            def a_score(n, qt, t):
                nk = P * (qt + 1)
                dve.wait_ge(s_["scores"], n + 1)
                dve.wait_ge(s_["pt_sum"], n - 1)
                for j in range(2):
                    tab = a_bias[:, 2 * t + j, 0:P] if qt == 0 else a_bias[:, 2 * t + j, P:3 * P]
                    step(V.tensor_tensor_reduce(prob2[:, n % 2, j, 0:nk], psum[:, 2 * (n % 2) + j, 0:nk], tab,
                                                1.0, -3.0e38, ALU.add, ALU.max, nmax[:, qt, 2 * t + j:2 * t + j + 1]))
                step.wait()
                V.tensor_scalar(nmax[:, qt, 2 * t:2 * t + 2], nmax[:, qt, 2 * t:2 * t + 2], -1.0, None, ALU.mult)\
                    .then_inc(s_["scored"], 1)

            attention(A_UNITS, a_score, P, y_a)

            def over(row):
                return row.unsqueeze(1).broadcast_to([P, TT, W3])

            def heads(x):
                return x.rearrange("p m (h d) -> p m h d", h=BH)

            for i, (x, prev) in enumerate(((b_r, X1), (b_k, X2), (b_v, X1))):
                dve.wait_ge(s_[f"shift_in{i}"], 48)
                dve.wait_ge(s_["zero_row"], 3 if i == 2 else 2)
                dve.wait_ge(s_[f"row_in{i}"], 16)
                step(V.tensor_tensor(prev, prev, x, ALU.subtract)); step.wait()
                step(V.tensor_tensor(prev, prev, over(row_slot[i]), ALU.mult)); step.wait()
                V.tensor_tensor(x, x, prev, ALU.add).then_inc(s_["lerp"], 1)
            for i in range(4):
                y = (y_a, y_c)[i // 2][:, :, (i % 2) * CH:(i % 2 + 1) * CH]
                dve.wait_ge(s_["acc_free"], FIRST_ACC["z_in"] + i + 3)
                V.tensor_tensor(y, y, silu_z.rearrange("p (m n) -> p m n", m=TT), ALU.mult).then_inc(s_["z_used"], 1)
            low = [psum[:, 4 * a:4 * a + 4].rearrange("p (m b) n -> p m (b n)", m=TT) for a in range(2)]
            dve.wait_ge(s_["lora_out"], 2)
            dve.wait_ge(s_["row_in4"], 16)
            dve.wait_ge(s_["lerp"], 3)
            V.tensor_tensor(X1, low[0], over(row_slot[4]), ALU.add).then_inc(s_["zw_in"], 1)
            dve.wait_ge(s_["zw_in"], 1)
            V.tensor_copy(small0[:, 0:1], cst[:, 0:1]).then_inc(s_["w0_used"], 1)
            dve.wait_ge(s_["z_used"], 4)
            dve.wait_ge(s_["row_in4"], 32)
            V.tensor_tensor(b_b, low[1], over(row_slot[4]), ALU.add).then_inc(s_["za_in"], 1)
            dve.wait_ge(s_["za_in"], 1)
            V.tensor_copy(small0[:, 1:2], cst[:, 0:1]).then_inc(s_["a0_used"], 1)
            dve.wait_ge(s_["zw"], 1)
            half = 0.5 * 0.6065306597126334
            V.tensor_scalar(X1, X1, -half, -half, ALU.mult, ALU.add).then_inc(s_["logw"], 1)
            dve.wait_ge(s_["za"], 1)
            step(V.tensor_scalar(b_b, b_b, 0.5, 0.5, ALU.mult, ALU.add))
            dve.wait_ge(s_["row_in0"], 32)
            step(V.tensor_tensor(b_a, b_k, over(row_slot[0]), ALU.mult)); step.wait()
            step(V.tensor_tensor(X2, b_a, b_a, ALU.mult)); step.wait()
            step(V.tensor_reduce(hs_r, heads(X2), AX, ALU.add)); step.wait()
            V.tensor_scalar(hs_a, hs_r, 1e-24, None, ALU.max).then_inc(s_["hroot_in"], 1)
            dve.wait_ge(s_["row_in1"], 32)
            step(V.scalar_tensor_tensor(X2, b_b, -1.0, over(row_slot[1]), ALU.add, ALU.mult)); step.wait()
            step(V.scalar_tensor_tensor(b_k, X2, 1.0, b_k, ALU.add, ALU.mult)); step.wait()
            dve.wait_ge(s_["row_in2"], 32)
            step(V.tensor_tensor(X2, b_r, b_k, ALU.mult)); step.wait()
            step(V.tensor_tensor(X2, X2, over(row_slot[2]), ALU.mult)); step.wait()
            step(V.tensor_reduce(bonus, heads(X2), AX, ALU.add)); step.wait()
            dve.wait_ge(s_["hroot"], 5)
            step(V.reciprocal(hs_r, hs_a)); step.wait()
            for m in range(TT):
                step(V.tensor_tensor(heads(b_a)[:, m], heads(b_a)[:, m],
                                     hs_r[:, m].unsqueeze(2).broadcast_to([P, BH, DH]), ALU.mult))
            step.wait()
            V.tensor_tensor(b_b, b_b, b_a, ALU.mult).then_inc(s_["x2_free"], 1)
            dve.wait_ge(s_["e_pos"], 1)
            step(V.tensor_tensor(b_r, b_r, X2, ALU.mult)); step.wait()
            cum = psum[:, 0:4].rearrange("p (m b) n -> p m (b n)", m=TT)
            V.tensor_tensor(X2, cum, X1, ALU.subtract).then_inc(s_["e_ex_in"], 1)
            dve.wait_ge(s_["e_ex"], 1)
            V.scalar_tensor_tensor(b_a, b_a, -1.0, X2, ALU.mult, ALU.mult).then_inc(s_["x2_free"], 1)
            dve.wait_ge(s_["e_neg"], 1)
            step(V.tensor_tensor(b_b, b_b, X2, ALU.mult))
            step.wait()
            dve.wait_ge(s_["x2_free"], 2)
            V.tensor_tensor(b_k, b_k, X2, ALU.mult).then_inc(s_["pre_done"], 1)
            dve.wait_ge(s_["pre_done"], 1)
            dve.wait_ge(s_["masks_in"], 32)

            for t in range(8):
                cs = slice(t * P, (t + 1) * P)
                dve.wait_ge(s_["g_prod"], t + 1)
                for u in range(4):
                    ins = V.tensor_tensor(Gs[:, u], psum[:, u].rearrange("p (a n) -> p a n", a=4), gmask, ALU.mult)
                    ins.then_inc(s_["g_mask"], 1)
                if t:
                    dve.wait_ge(s_["ux_sum"], t)
                    dve.wait_ge(s_["y_sum"], t)
                for a in range(2):
                    ins = V.tensor_copy(DD[:, :, a], ident.unsqueeze(1).broadcast_to([P, 4, P]))
                    if a == 0:
                        step(ins)
                        step.wait()
                ins.then_inc(s_["dd"], 1)
                dve.wait_ge(s_["g_mask"], 4 * t + 4)
                for l in range(6):
                    if l:
                        dve.wait_ge(s_["p_sum"], 6 * t + l)
                    elif t:
                        dve.wait_ge(s_["wz_sum"], t)
                    V.tensor_tensor(Lm, Gs[:, :, 0], lev[:, l].unsqueeze(1).broadcast_to([P, 4, P]), ALU.mult)\
                        .then_inc(s_["l_mask"], 1)
                    dve.wait_ge(s_["dd_sum"], 6 * t + l + 1)
                    flat = DD.rearrange("p u a n -> p (u a n)")
                    dve.wait_ge(s_["dd"], 7 * t + l + 1)
                    V.tensor_tensor(flat, flat, psum[:, 5:7].rearrange("p b n -> p (b n)"), ALU.add)\
                        .then_inc(s_["dd"], 1)
                dve.wait_ge(s_["o1_sum"], t + 1)
                for m in range(TT):
                    src = psum[:, 7, 0:256].rearrange("p (j m d) -> p m j d", j=2, m=TT)[:, m]
                    step(V.tensor_copy(y_b[:, m, cs].rearrange("p (j d) -> p j d", j=2), src))
                dve.wait_ge(s_["qt_sum"], t + 1)
                V.tensor_tensor(AR[:, :, P:2 * P], AR[:, :, P:2 * P], psum[:, 5, 0:256].rearrange("p (m n) -> p m n", m=TT),
                                ALU.add).then_inc(s_["qt"], 1)
                dve.wait_ge(s_["wz"], t + 1)
                dve.wait_ge(s_["c_end"], 1)
                if t:
                    dve.wait_ge(s_["o2_sum"], t)
                V.tensor_scalar(ST[:, 0], WZ[:, 0, 1], c_end[:, t, 0:1], None, ALU.mult).then_inc(s_["state"], 1)
                for c in range(1, 3):
                    dve.wait_ge(s_["state"], 3 * t + c)
                    step(V.tensor_tensor(S_tmp, ST[:, c - 1], WZ[:, c, 1], ALU.add)); step.wait()
                    dve.wait_ge(s_["st_sum"], 2 * t + c)
                    step(V.tensor_tensor(S_tmp, S_tmp, psum[:, 2, c * DH:(c + 1) * DH], ALU.add)); step.wait()
                    V.tensor_scalar(ST[:, c], S_tmp, c_end[:, t, c:c + 1], None, ALU.mult).then_inc(s_["state"], 1)
                dve.wait_ge(s_["o2_sum"], t + 1)
                step.wait()
                for h2 in range(2):
                    hc = slice(t * P + h2 * DH, t * P + (h2 + 1) * DH)
                    bank = (6, 3)[h2]
                    step(V.tensor_tensor(y_b[DH:P, 0, hc], y_b[DH:P, 0, hc], psum[DH:P, bank, 0:DH], ALU.add))
                    ins = V.tensor_tensor(y_b[:, 1, hc], y_b[:, 1, hc], psum[:, bank, DH:P], ALU.add)
                    if h2 == 0:
                        step(ins)
                        step.wait()
                step.wait()
                ins.then_inc(s_["o2"], 1)
            dve.wait_ge(s_["o2"], 8)

            yh = heads(y_b)

            def per_head(m, v):
                return v[:, m].unsqueeze(2).broadcast_to([P, BH, DH])

            step(V.tensor_reduce(hs_r, yh, AX, ALU.add)); step.wait()
            step(V.tensor_scalar(hs_r, hs_r, 1.0 / DH, None, ALU.mult)); step.wait()
            for m in range(TT):
                step(V.tensor_tensor(yh[:, m], yh[:, m], per_head(m, hs_r), ALU.subtract))
            step.wait()
            step(V.tensor_tensor(X1, y_b, y_b, ALU.mult)); step.wait()
            step(V.tensor_reduce(hs_r, heads(X1), AX, ALU.add)); step.wait()
            V.tensor_scalar(hs_a, hs_r, 1.0 / DH, 64e-5, ALU.mult, ALU.add).then_inc(s_["hroot_in"], 1)
            dve.wait_ge(s_["row_in3"], 32)
            dve.wait_ge(s_["row_in4"], 48)
            for m in range(TT):
                step(V.tensor_tensor(heads(b_v)[:, m], heads(b_v)[:, m], per_head(m, bonus), ALU.mult))
            step.wait()
            step(V.tensor_tensor(b_v, b_v, over(row_slot[4]), ALU.add)); step.wait()
            dve.wait_ge(s_["hroot"], 6)
            step(V.reciprocal(hs_r, hs_a)); step.wait()
            for m in range(TT):
                step(V.tensor_tensor(yh[:, m], yh[:, m], per_head(m, hs_r), ALU.mult))
            step.wait()
            step(V.tensor_tensor(y_b, y_b, over(row_slot[3]), ALU.mult)); step.wait()
            V.tensor_tensor(y_b, y_b, b_v, ALU.add).then_inc(s_["yb_ready"], 1)
            dve.wait_ge(s_["yb_ready"], 1)
            if debug:
                V.tensor_copy(small0[:, 0:1], cst[:, 0:1]).then_inc(s_["dbg"], 1)
                dve.wait_ge(s_["dbg"], 2)
            for i in range(4, 6):
                y = y_b[:, :, (i % 2) * CH:(i % 2 + 1) * CH]
                dve.wait_ge(s_["acc_free"], FIRST_ACC["z_in"] + i + 3)
                V.tensor_tensor(y, y, silu_zb.rearrange("p (m n) -> p m n", m=TT), ALU.mult).then_inc(s_["z_used"], 1)
            base, acc = PLAN["ups"][0], FIRST_ACC["ups"]
            t_ = up_tmp
            for i in range(6):
                for n2 in range(2):
                    if n2 == 0:
                        dve.wait_ge(s_["up_half"], i + 1)
                    else:
                        wait_used(dve, base + i)
                    b, nb = i // 2, 2 * (i % 2) + n2
                    c = slice(nb * CH, (nb + 1) * CH)
                    src = psum[:, 2 * n2:2 * n2 + 2]
                    g = gates_[:, :, b * D + nb * CH:b * D + (nb + 1) * CH]
                    if i == 0 and n2 == 0:
                        dve.wait_ge(s_["acc_free"], acc + 2)
                    V.tensor_tensor(g, src, g, ALU.mult).then_inc(s_["acc_free"], 1)
                    dve.wait_ge(s_["acc_free"], acc + 2 * i + n2 + 3)
                    if b == 0:
                        V.tensor_copy(xn[:, :, c], g).then_inc(s_["merged"], 1)
                    else:
                        if nb == 0:
                            dve.wait_ge(s_["merged"], 4 * b)
                        V.tensor_tensor(xn[:, :, c], xn[:, :, c], g, ALU.add).then_inc(s_["merged"], 1)
            acc = FIRST_ACC["w_o"]
            for nb in range(4):
                wait_used(dve, PLAN["w_o"][0] + nb)
                c = slice(nb * CH, (nb + 1) * CH)
                s = nb % 2
                V.tensor_tensor(h[:, :, c], h[:, :, c], psum[:, 2 * s:2 * s + 2], ALU.add).then_inc(s_["x2_done"], 1)
                if nb < 2:
                    dve.wait_ge(s_["x2_done"], nb + 1)
                    V.tensor_copy(small0[:, 0:1], cst[:, 0:1]).then_inc(s_["acc_free"], 1)
                    dve.wait_ge(s_["acc_free"], acc + nb + 3)

        FIRST_ACC = {}
        n = 0
        for name, count in (("w_in", 12), ("w_out", 4), ("ffn", 22), ("down", 4), ("mem", 4), ("c_q", 2),
                            ("a_qk", 4), ("a_v", 2), ("b_in", 6), ("z_in", 6), ("gates", 12), ("ups", 12),
                            ("w_o", 4)):
            FIRST_ACC[name] = n
            n += count

        @block.sync
        def _(sp):
            sp.dma_start(h[:], A["x"].rearrange("(m p) n -> p m n", p=P)).then_inc(s_["x_in"], 16)
            sp.dma_start(vec[:], A["vec"][:, 0:vec.shape[1]]).then_inc(s_["x_in"], 16)
            sp.dma_start(cst[:], A["const"]).then_inc(s_["const_in"], 16)
            for slot in range(2):
                sp.dma_start(Wb[:, slot], A["loads"][slot]).then_inc(LOADED[slot], 16)
            with sp.Fori(1, N_LOADS // 2) as i:
                for slot in range(2):
                    sp.wait_ge(USED[slot], i)
                    sp.dma_start(Wb[:, slot], A["loads"][i * 2 + slot]).then_inc(LOADED[slot], 16)
            if not stop:
                sp.wait_ge(s_["out_stored"], 16)

        @block.gpsimd
        def _(pool):
            nc.gpsimd.dma_start(arena[:, 12288:12288 + A["tabs"].shape[1]], A["tabs"]).then_inc(s_["tabs_in"], 16)
            pool.wait_ge(s_["tr_ready"], 8)
            for half in range(2):
                nc.gpsimd.dma_start(cmp_w1[half * DH:half * DH + DH], A["cmp_w1"]).then_inc(s_["w1_in"], 16)
            pool_block2(pool)

        @block.scalar
        def _(act):
            step = Steps(act, s_["act_step"])
            rounds = [0]

            def copy(out_, in_, scale=1.0):
                return nc.scalar.activation(out_, in_, ACT.Copy, scale=scale)

            def square_sums(src, n):
                for m in range(TT):
                    nc.scalar.activation(xn[:, m], src[:, m], ACT.Square, accum_out=stat[:, m:m + 1])\
                      .then_inc(s_["stat_ready"], 1)
                act.wait_ge(s_["root_ready"], 2 * n + 1)
                nc.scalar.activation(rstd[:], stat[:], ACT.Sqrt).then_inc(s_["root_ready"], 1)

            def read_transposes(n_tiles, scale=None, bias=None, dst=None, factor=1.0):
                dst = xT if dst is None else dst
                for r in range(n_tiles // 2):
                    bank = TRB + rounds[0] % 2
                    rounds[0] += 1
                    act.wait_ge(s_["tr_ready"], rounds[0])
                    src = psum[:, bank].rearrange("p (k s) -> p k s", k=2)
                    for j in range(2):
                        k = 2 * r + j
                        if scale is None:
                            ins = copy(dst[:, k], src[:, j], scale=factor)
                        elif bias is None:
                            ins = copy(dst[:, k], src[:, j], scale=scale[:, k:k + 1])
                        else:
                            ins = nc.scalar.activation(dst[:, k], src[:, j], ACT.Identity,
                                                       bias=bias[:, k:k + 1], scale=scale[:, k:k + 1])
                    ins.then_inc(s_["tr_free"], 1)

            act.wait_ge(s_["const_in"], 16)
            for i in range(2):
                copy(small0[:, i:i + 1], cst[:, 0:1]).then_inc(s_["acc_free"], 1)

            act.wait_ge(s_["x_in"], 32)
            nc.scalar.activation(c_act[:], v_("c"), ACT.Tanh, scale=0.5).then_inc(s_["c_exp"], 1)
            square_sums(h, 0)
            act.wait_ge(s_["mod_ready"], 9)
            read_transposes(KT, scale_col, mod[:, 0:16])

            base, acc = PLAN["w_in"][0], FIRST_ACC["w_in"]
            for first, scale in ((0, DH ** -0.5), (4, 1.0)):
                with act.Fori(0, 2) as i:
                    for s in range(2):
                        act.wait_ge(USED[s], i + (base + first) // 2 + 1)
                        copy(qk[:, bass.ds(i * 8 + (first + s) * 4, 4), :],
                             psum[:, 2 * s:2 * s + 2].rearrange("p b (c s) -> p (b c) s", s=SEQ), scale=scale)\
                            .then_inc(s_["acc_free"], 1)
            with act.Fori(0, 2) as i:
                for s in range(2):
                    act.wait_ge(USED[s], i + (base + 8) // 2 + 1)
                    copy(tm[:, :, bass.ds(i * 1024 + s * CH, CH)], psum[:, 2 * s:2 * s + 2])\
                        .then_inc(s_["acc_free"], 1)
            act.wait_ge(s_["acc_free"], acc + 14)
            nc.scalar.activation(gate[:], tm[:, :, V_GATE:V_GATE + 24], ACT.Tanh, scale=0.5)\
              .then_inc(s_["gate_exp"], 1)
            act.wait_ge(s_["f_abs"], 1)
            nc.scalar.activation(fe[:], fe[:], ACT.Exp).then_inc(s_["f_ln"], 1)
            act.wait_ge(s_["f_ln"], 1)
            nc.scalar.activation(fe[:], fe[:], ACT.Ln, bias=1.0).then_inc(s_["f_ln"], 1)
            act.wait_ge(s_["crow_sum"], 1)
            copy(crow[:, 0], psum[0:1, 0:4].rearrange("p b (c s) -> p (b c) s", s=SEQ)[:, 0:FOX])\
                .then_inc(s_["crow_ready"], 1)
            act.wait_ge(s_["cmp_hidden"], 1)
            for g in range(2):
                copy(cz[0:DH, 0, g], psum[0:DH, OB + g, 0:32].rearrange("p (v c) -> p v c", v=2)[:, :, 0:N_CMP])\
                    .then_inc(s_["cmp_exp_in"], 1)
            act.wait_ge(s_["cmp_exp_in"], 3)
            nc.scalar.activation(cz[0:DH, 3], cz[0:DH, 2], ACT.Tanh).then_inc(s_["cmp_exp"], 1)
            act.wait_ge(s_["cmp_out"], 1)
            copy(kcT[:], psum[:, OB, 0:N_CMP]).then_inc(s_["kc_ready"], 1)
            copy(vc[0:N_CMP], psum[0:N_CMP, OB + 1, 0:2 * DH].rearrange("p (g d) -> p g d", g=2))\
                .then_inc(s_["kc_ready"], 1)

            act.wait_ge(s_["lam_in"], 1)
            nc.scalar.activation(lam[:, 0:2], lam[:, 0:2], ACT.Exp).then_inc(s_["lam_exp"], 1)

            def exps(n):
                qt, p = divmod(n, NPAIR)
                nk = keys(n)
                act.wait_ge(s_["scored"], n + 1)
                for j in range(2):
                    nc.scalar.activation(prob[:, n % 2, j, 0:nk], prob[:, n % 2, j, 0:nk], ACT.Exp,
                                         bias=nmax[:, qt, 2 * p + j:2 * p + j + 1],
                                         accum_out=sums[:, qt, 2 * p + j:2 * p + j + 1]).then_inc(s_["exps"], 1)

            def read_probT(n):
                nk = keys(n)
                act.wait_ge(s_["pt_sum"], n + 1)
                if n >= 2:
                    act.wait_ge(s_["pv"], n - 1)
                rows_ = P if nk > N_CMP else N_CMP
                w = max(nk, P)
                copy(probT[0:rows_, n % 2, :, 0:w],
                     psum[0:rows_, TRB].rearrange("p (j k) -> p j k", j=2)[:, :, 0:w]).then_inc(s_["pt_ready"], 1)

            for n in range(TT * NPAIR + 1):
                if n < TT * NPAIR:
                    exps(n)
                if n >= 1:
                    read_probT(n - 1)
                if n in DIL_AT:
                    qt = DIL_AT.index(n)
                    act.wait_ge(s_["dil_in"], qt + 1)
                    nc.scalar.activation(dil_e[:], dil_e[:], ACT.Exp).then_inc(s_["dil_exp"], 1)
            act.wait_ge(s_["diff_in"], 1)
            nc.scalar.activation(diff_ss[:], diff_ss[:], ACT.Sqrt).then_inc(s_["diff_in"], 1)
            act.wait_ge(s_["o_ready"], 1)
            read_transposes(KT)

            def read_g_row(n):
                act.wait_ge(s_["g_sum"], n + 1)
                copy(g_row, psum[:, 4:8].rearrange("p b n -> p (b n)")).then_inc(s_["g_row_ready"], 1)

            read_g_row(0)
            act.wait_ge(s_["h_ready"], 4)
            square_sums(h, 1)
            act.wait_ge(s_["mod_ready"], 26)
            read_transposes(KT, scale_col, mod[:, 48:64])
            base, acc = PLAN["ffn"][0], FIRST_ACC["ffn"]
            with act.Fori(0, 11) as i:
                act.wait_ge(USED[0], i + base // 2 + 1)
                act.wait_ge(s_["acc_free"], i * 2 + acc + 2)
                nc.scalar.activation(silu_g, psum[:, 0:2].rearrange("p b n -> p (b n)"), ACT.Silu)\
                  .then_inc(s_["acc_free"], 1)
            read_g_row(1)
            act_block2(act, step, copy, square_sums, read_transposes)

        @block.tensor
        def _(pe):
            rounds = [0]

            def transposes(src, n_tiles):
                for r in range(n_tiles // 2):
                    bank = TRB + rounds[0] % 2
                    if rounds[0] >= 2:
                        pe.wait_ge(s_["tr_free"], rounds[0] - 1)
                    rounds[0] += 1
                    for j in range(2):
                        for m in range(TT):
                            k = 2 * r + j
                            ins = nc.tensor.transpose(psum[:, bank, (2 * j + m) * P:(2 * j + m + 1) * P],
                                                      src[:, m, k * P:(k + 1) * P], ident)
                    ins.then_inc(s_["tr_ready"], 1)

            def tokens_product(name, first=0, count=None, k_tiles=KT, act_T=None):
                base, n = PLAN[name]
                acc = FIRST_ACC[name] + first
                count = n - first if count is None else count
                base += first
                act_T = xT if act_T is None else act_T
                with pe.Fori(0, count // 2) as i:
                    for s in range(2):
                        pe.wait_ge(LOADED[s], i * 16 + 16 * (base // 2 + 1))
                        pe.wait_ge(s_["acc_free"], i * 2 + (acc + s + 1))
                        for m in range(TT):
                            for k in range(k_tiles):
                                ins = nc.tensor.matmul(psum[:, 2 * s + m], act_T[:, k, m * P:(m + 1) * P],
                                                       W(s)[:, k], start=(k == 0), stop=(k == k_tiles - 1))
                        ins.then_inc(USED[s], 1)

            def features_product(name, first=0, count=None):
                base, n = PLAN[name]
                acc = FIRST_ACC[name] + first
                count = n - first if count is None else count
                base += first
                with pe.Fori(0, count // 2) as i:
                    for s in range(2):
                        pe.wait_ge(LOADED[s], i * 16 + 16 * (base // 2 + 1))
                        pe.wait_ge(s_["acc_free"], i * 2 + (acc + s + 1))
                        for c in range(4):
                            for k in range(KT):
                                ins = nc.tensor.matmul(psum[:, 2 * s + c // 2, (c % 2) * SEQ:(c % 2 + 1) * SEQ],
                                                       W(s)[:, k, c * P:(c + 1) * P], xT[:, k],
                                                       start=(k == 0), stop=(k == KT - 1))
                        ins.then_inc(USED[s], 1)

            def ada_sum(i, load):
                wait_used(pe, load)
                if i:
                    pe.wait_ge(s_["mod_ready"], i + (i > 8))
                for j in range(4):
                    ins = nc.tensor.matmul(psum[:, TRB + 1, j:j + 1], ada_acc[:, j * P:(j + 1) * P], ones[:, 0:1],
                                           start=True, stop=True)
                ins.then_inc(s_["ada_sum"], 1)

            pe.wait_ge(s_["const_in"], 16)
            for i in range(8):
                ada_sum(i, PLAN["ada_a"][0] + i)
            pe.wait_ge(s_["mod_ready"], 8)
            pe.wait_ge(s_["norm_ready"], 2)
            transposes(xn, KT)
            pe.wait_ge(s_["tr_free"], rounds[0])
            features_product("w_in", 0, 8)
            tokens_product("w_in", 8, 4)

            pe.wait_ge(s_["logf_ready"], 1)
            pe.wait_ge(s_["acc_free"], FIRST_ACC["w_in"] + 14)
            for f in range(FOX):
                row = psum[0:1, f // 2, (f % 2) * SEQ:(f % 2 + 1) * SEQ]
                nc.tensor.matmul(row[:, 0:P], logf[:, 0, f:f + 1], tri, start=True, stop=True)
                nc.tensor.matmul(row[:, P:SEQ], logf[:, 0, f:f + 1], ones, start=True, stop=False)
                ins = nc.tensor.matmul(row[:, P:SEQ], logf[:, 1, f:f + 1], tri, start=False, stop=True)
            ins.then_inc(s_["crow_sum"], 1)

            pe.wait_ge(s_["w1_in"], 32)
            pe.wait_ge(s_["blk_ready"], 4)
            for g in range(2):
                for v in range(2):
                    for l in range(CMP_LEN):
                        r = slice(g * DH, g * DH + DH)
                        ins = nc.tensor.matmul(psum[0:DH, OB + g, v * 16:v * 16 + N_CMP], cmp_w1[r, v, l],
                                               blk[r, v, l], start=(l == 0), stop=(l == CMP_LEN - 1))
            ins.then_inc(s_["cmp_hidden"], 1)
            pe.wait_ge(s_["gelu_ready"], 1)
            w2 = v_("cmp_w2").rearrange("p (v e) -> p v e", v=2)
            for g in range(2):
                nc.tensor.matmul(psum[g * DH:(g + 1) * DH, OB, 0:N_CMP], w2[0:DH, 0], cz[0:DH, 5, g, 0],
                                 start=True, stop=True)
            for g in range(2):
                ins = nc.tensor.matmul(psum[0:N_CMP, OB + 1, g * DH:(g + 1) * DH], cz[0:DH, 5, g, 1],
                                       w2[0:DH, 1], start=True, stop=True)
            ins.then_inc(s_["cmp_out"], 1)
            pe.wait_ge(s_["kc_ready"], 2)
            pe.wait_ge(s_["crow_ready"], 1)
            pe.wait_ge(s_["ncrow_ready"], 1)

            def scores(n):
                qt, p = divmod(n, NPAIR)
                kind, t, q, k = PAIRS[p]
                nk = keys(n)
                if n >= 2:
                    pe.wait_ge(s_["scored"], n - 1)
                qs = slice(qt * P, qt * P + P)
                for j in range(2):
                    bank = psum[:, 2 * (n % 2) + j, 0:nk]
                    r = slice(j * DH, j * DH + DH)
                    fox = kind == "fd" and 2 * t + j < FOX
                    key = kcT[r, :] if kind == "cmp" else qk[r, k, 0:nk]
                    ins = nc.tensor.matmul(bank, qk[r, q, qs], key, start=True, stop=not fox)
                    if fox:
                        f = 2 * t + j
                        nc.tensor.matmul(bank, crow[:, 0, f, qs], ones[0:1, 0:1].broadcast_to([1, nk]),
                                         start=False, stop=False)
                        ins = nc.tensor.matmul(bank, ones[0:1, :], crow[:, 1, f, 0:nk], start=False, stop=True)
                ins.then_inc(s_["scores"], 1)

            def transpose_probs(n):
                nk = keys(n)
                pe.wait_ge(s_["exps"], 2 * n + 2)
                if n >= 1:
                    pe.wait_ge(s_["pt_ready"], n)
                for j in range(2):
                    for a in range(0, nk, P):
                        w = min(P, nk - a)
                        ins = nc.tensor.transpose(psum[0:w, TRB, j * SEQ + a:j * SEQ + a + P],
                                                  prob[:, n % 2, j, a:a + w], ident)
                ins.then_inc(s_["pt_sum"], 1)

            def values(n):
                qt, p = divmod(n, NPAIR)
                kind, t, _, _ = PAIRS[p]
                nk = keys(n)
                g = GROUP_OF[p]
                G = qt * len(GROUPS) + g
                pe.wait_ge(s_["pt_ready"], n + 1)
                if p == GROUPS[g][0] and G >= 2:
                    pe.wait_ge(s_["pv_read"], G - 1)
                for j in range(2):
                    i = 2 * (p - GROUPS[g][0]) + j
                    if kind == "cmp":
                        ins = nc.tensor.matmul(psum[:, OB + G % 2, i * DH:(i + 1) * DH], probT[0:N_CMP, n % 2, j, 0:P],
                                               vc[0:N_CMP, j], start=True, stop=True)
                        continue
                    at, w = value_of(kind, t, j)
                    for m in range(nk // P):
                        ins = nc.tensor.matmul(psum[:, OB + G % 2, i * w:(i + 1) * w],
                                               probT[:, n % 2, j, m * P:(m + 1) * P], tm[:, m, at:at + w],
                                               start=(m == 0), stop=(m == nk // P - 1))
                ins.then_inc(s_["pv"], 1)

            for n in range(TT * NPAIR + 2):
                if n < TT * NPAIR:
                    scores(n)
                if 1 <= n <= TT * NPAIR:
                    transpose_probs(n - 1)
                if n >= 2:
                    values(n - 2)
                if n % 3 == 2 and n // 3 < 16:
                    ada_sum(8 + n // 3, PLAN["ada_b"][0] + n // 3)
            pe.wait_ge(s_["mod_ready"], 25)
            pe.wait_ge(s_["o_ready"], 1)
            transposes(o, KT)
            pe.wait_ge(s_["tr_free"], rounds[0])

            def g_rows(n):
                pe.wait_ge(s_["g_diag"], n + 1)
                for b in range(4):
                    ins = nc.tensor.matmul(psum[:, 4 + b], ones, diag[:, 4 * b:4 * b + 4].rearrange("p k n -> p (k n)"),
                                           start=True, stop=True)
                ins.then_inc(s_["g_sum"], 1)

            g_rows(0)
            tokens_product("w_out")
            pe.wait_ge(s_["norm_ready"], 4)
            pe.wait_ge(s_["g_row_ready"], 1)
            transposes(xn, KT)
            pe.wait_ge(s_["tr_free"], rounds[0])
            features_product("ffn")
            g_rows(1)
            base = PLAN["down"][0]
            pe.wait_ge(s_["acc_free"], FIRST_ACC["ffn"] + 24)
            for nb in range(4):
                pe.wait_ge(s_["acc_free"], FIRST_ACC["down"] + nb + 1)
                for part in range(3):
                    load = base + 3 * nb + part
                    wait_load(pe, load)
                    kn = min(KT, KF - part * KT)
                    for m in range(TT):
                        for k in range(kn):
                            kk = part * KT + k
                            ins = nc.tensor.matmul(psum[:, 2 * (nb % 2) + m], hT[:, kk, m * P:(m + 1) * P],
                                                   W(load % 2)[:, k], start=(kk == 0), stop=(kk == KF - 1),
                                                   skip_group_check=True)
                    ins.then_inc(USED[load % 2], 1)
            pe_block2(pe, transposes, tokens_product, rounds)

        @block.vector
        def _(dve):
            step = Steps(dve, s_["dve_step"])
            V = nc.vector

            def rms(n, width=D):
                dve.wait_ge(s_["stat_ready"], 2 * n + 2)
                V.tensor_scalar(stat[:], stat[:], 1.0 / width, EPS, ALU.mult, ALU.add)\
                    .then_inc(s_["root_ready"], 1)
                dve.wait_ge(s_["root_ready"], 2 * n + 2)
                step(V.reciprocal(rstd[:], rstd[:]))
                step.wait()

            def scale_tokens(src):
                for m in range(TT):
                    V.tensor_scalar(xn[:, m], src[:, m], rstd[:, m:m + 1], None, ALU.mult)\
                        .then_inc(s_["norm_ready"], 1)

            ada_n = [0]

            def ada_part(load, k0, k1):
                for k in range(k0, k1):
                    if k == 0:
                        wait_load(dve, load)
                        if ada_n[0]:
                            dve.wait_ge(s_["ada_sum"], ada_n[0])
                        ins = V.tensor_scalar(ada_acc, W(load % 2)[:, 0], c_act[:, 0:1], None, ALU.mult)
                    else:
                        dve.wait_ge(s_["ada_step"], ada_n[0] * (KT - 1) + k)
                        ins = V.scalar_tensor_tensor(ada_acc, W(load % 2)[:, k], c_act[:, k:k + 1], ada_acc,
                                                     ALU.mult, ALU.add)
                    if k < KT - 1:
                        ins.then_inc(s_["ada_step"], 1)
                    else:
                        ins.then_inc(USED[load % 2], 1)
                        ada_n[0] += 1

            def ada_read(i):
                dve.wait_ge(s_["ada_sum"], i + 1)
                a = VEC["ada_b"][0]
                V.tensor_tensor(mod[:, 4 * i:4 * i + 4], psum[:, TRB + 1, 0:4], vec[:, a + 4 * i:a + 4 * i + 4],
                                ALU.add).then_inc(s_["mod_ready"], 1)

            dve.wait_ge(s_["c_exp"], 1)
            step(V.tensor_scalar(c_act[:], c_act[:], 0.5, 0.5, ALU.mult, ALU.add)); step.wait()
            step(V.tensor_tensor(c_act[:], c_act[:], v_("c"), ALU.mult)); step.wait()
            rms(0)
            scale_tokens(h)
            for i in range(8):
                ada_part(PLAN["ada_a"][0] + i, 0, KT)
                ada_read(i)
            dve.wait_ge(s_["mod_ready"], 8)
            V.scalar_tensor_tensor(scale_col[:], mod[:, 16:32], 1.0, v_("norm_mix"), ALU.add, ALU.mult)\
                .then_inc(s_["mod_ready"], 1)

            acc = FIRST_ACC["w_in"]
            dve.wait_ge(s_["acc_free"], acc + 14)
            a = VEC["fox_b"][0]
            step(V.tensor_tensor(fz[:], tm[:, :, V_FOXF:V_FOXF + FOX],
                                 vec[:, a:a + FOX].unsqueeze(1).broadcast_to([P, TT, FOX]), ALU.add)); step.wait()
            V.scalar_tensor_tensor(fe[:], fz[:], -1.0, fz[:], ALU.mult, ALU.min).then_inc(s_["f_abs"], 1)
            dve.wait_ge(s_["f_ln"], 2)
            step(V.tensor_scalar(fz[:], fz[:], 0.0, None, ALU.min)); step.wait()
            V.tensor_tensor(logf[:], fz[:], fe[:], ALU.subtract).then_inc(s_["logf_ready"], 1)
            dve.wait_ge(s_["gate_exp"], 1)
            step(V.tensor_scalar(gate[:], gate[:], 0.5, 0.5, ALU.mult, ALU.add))
            dve.wait_ge(s_["crow_ready"], 1)
            V.tensor_scalar(crow[:, 1], crow[:, 0], -1.0, None, ALU.mult).then_inc(s_["ncrow_ready"], 1)
            pos = v_("cmp_pos").rearrange("p (v l) -> p v l", v=2)
            for v, tile in ((0, CMPK), (1, CMPV)):
                chunks = qk[:, tile].rearrange("p (c r) -> p r c", r=CMP_STRIDE)
                for half in range(2):
                    ls = slice(half * CMP_STRIDE, (half + 1) * CMP_STRIDE)
                    V.tensor_tensor(blk[:, v, ls], chunks[:, :, half:half + N_CMP],
                                    pos[:, v, ls].unsqueeze(2).broadcast_to([P, CMP_STRIDE, N_CMP]), ALU.add)\
                        .then_inc(s_["blk_ready"], 1)
            dve.wait_ge(s_["cmp_exp_in"], 2)
            z = [cz[0:DH, i] for i in range(6)]
            step(V.tensor_tensor(z[1], z[0], z[0], ALU.mult)); step.wait()
            step(V.tensor_scalar(z[1], z[1], 0.044715, 1.0, ALU.mult, ALU.add)); step.wait()
            V.scalar_tensor_tensor(z[2], z[1], 0.7978845608028654, z[0], ALU.mult, ALU.mult)\
                .then_inc(s_["cmp_exp_in"], 1)
            dve.wait_ge(s_["cmp_exp"], 1)
            step(V.tensor_scalar(z[4], z[3], 0.5, 0.5, ALU.mult, ALU.add)); step.wait()
            V.tensor_tensor(z[5], z[4], z[0], ALU.mult).then_inc(s_["gelu_ready"], 1)
            lv = v_("lam").rearrange("p (i d) -> p i d", i=4)
            for i in range(2):
                step(V.tensor_tensor_reduce(lv[:, 2 * i], lv[:, 2 * i], lv[:, 2 * i + 1], 1.0, 0.0, ALU.mult, ALU.add,
                                            lam[:, i:i + 1]))
            step.wait()
            V.tensor_copy(lam[:, 3:4], lam[:, 0:1]).then_inc(s_["lam_in"], 1)
            dve.wait_ge(s_["lam_exp"], 1)
            step(V.tensor_tensor(lam[:, 2:3], lam[:, 1:2], lam[:, 0:1], ALU.subtract)); step.wait()
            step(V.tensor_scalar(lam[:, 2:3], lam[:, 2:3], -LAM_INIT, None, ALU.add))
            dve.wait_ge(s_["tabs_in"], 16)

            def score(n):
                qt, p = divmod(n, NPAIR)
                kind, t, _, _ = PAIRS[p]
                nk = keys(n)
                dve.wait_ge(s_["scores"], n + 1)
                if n >= 2:
                    dve.wait_ge(s_["pt_sum"], n - 1)
                elif n == 0:
                    dve.wait_ge(s_["cmp_hidden"], 1)
                for j in range(2):
                    if kind == "cmp":
                        tab = cmp_tabs[:, t + 4 * j, qt]
                    else:
                        i = table_of(kind, t, j)
                        tab = tabs[:, i, 0:P] if qt == 0 else tabs[:, i, P:P + nk]
                    step(V.tensor_tensor_reduce(prob[:, n % 2, j, 0:nk], psum[:, 2 * (n % 2) + j, 0:nk], tab,
                                                1.0, -3.0e38, ALU.add, ALU.max,
                                                nmax[:, qt, 2 * p + j:2 * p + j + 1]))
                step.wait()
                V.tensor_scalar(nmax[:, qt, 2 * p:2 * p + 2], nmax[:, qt, 2 * p:2 * p + 2], -1.0, None, ALU.mult)\
                    .then_inc(s_["scored"], 1)

            def bank_of(G):
                return psum[:, OB + G % 2]

            def items(x, w):
                return x.rearrange("p (i d) -> p i d", d=w)

            def finish(G):
                qt, g = divmod(G, len(GROUPS))
                last = qt * NPAIR + GROUPS[g][-1]
                dve.wait_ge(s_["pv"], last + 1)
                i0, i1 = 2 * GROUPS[g][0], 2 * GROUPS[g][-1] + 2
                f = fac[:, qt, i0:i1]
                if g <= 1:
                    if g == 1:
                        m9 = nmax[:, qt, FOX:16].rearrange("p (g j) -> p j g", g=3)
                        step(V.tensor_reduce(dil_m[:, 0:3], m9, AX, ALU.min)); step.wait()
                        V.tensor_tensor(dil_e[:].rearrange("p (g j) -> p g j", g=3),
                                        dil_m[:, 0:3].unsqueeze(1).broadcast_to([P, 3, 3]),
                                        nmax[:, qt, FOX:16].rearrange("p (g j) -> p g j", g=3), ALU.subtract)\
                            .then_inc(s_["dil_in"], 1)
                    V.tensor_copy(o[:, qt, 512 * g:512 * g + 512], bank_of(G)).then_inc(s_["pv_read"], 1)
                    if g == 1:
                        step(V.reciprocal(fac[:, qt, 0:FOX], sums[:, qt, 0:FOX]))
                        dve.wait_ge(s_["dil_exp"], qt + 1)
                        fd = fac[:, qt, FOX:16]
                        step(V.tensor_tensor(fd, dil_e[:], sums[:, qt, FOX:16], ALU.mult)); step.wait()
                        step(V.tensor_reduce(dil_m[:, 3:6], fd.rearrange("p (g j) -> p j g", g=3), AX, ALU.add))
                        step.wait()
                        step(V.reciprocal(dil_m[:, 3:6], dil_m[:, 3:6])); step.wait()
                        step(V.tensor_tensor(fd.rearrange("p (g j) -> p g j", g=3),
                                             dil_e[:].rearrange("p (g j) -> p g j", g=3),
                                             dil_m[:, 3:6].unsqueeze(1).broadcast_to([P, 3, 3]), ALU.mult))
                        dve.wait_ge(s_["pv_read"], G + 1)
                        step.wait()
                        oo = items(o[:, qt, 0:1024], DH)
                        step(V.tensor_tensor(oo, oo, fac[:, qt, 0:16].unsqueeze(2).broadcast_to([P, 16, DH]), ALU.mult))
                    return
                step(V.reciprocal(f, sums[:, qt, i0:i1])); step.wait()
                if g <= 4:
                    branch = {2: 1, 3: 2, 4: 0}[g]
                    step(V.tensor_tensor(f, f, gate[:, qt, branch * 8:branch * 8 + 8], ALU.mult)); step.wait()
                    dst = items(o[:, qt, 1024:1536], DH)
                    if g == 4:
                        step(V.tensor_scalar(f, f, const("valid")[:, qt:qt + 1], None, ALU.mult)); step.wait()
                    tmp = items(ada_tmp if g > 2 else o[:, qt, 1024:1536], DH)
                    V.tensor_tensor(tmp, items(bank_of(G), DH), f.unsqueeze(2).broadcast_to([P, 8, DH]), ALU.mult)\
                        .then_inc(s_["pv_read"], 1)
                    if g > 2:
                        dve.wait_ge(s_["pv_read"], G + 1)
                        step(V.tensor_tensor(dst, dst, tmp, ALU.add)); step.wait()
                    return
                ff = f.rearrange("p (h a) -> p h a", a=2)
                step(V.tensor_scalar(ff[:, :, 1], ff[:, :, 1], lam[:, 2:3], None, ALU.mult)); step.wait()
                tmp = ada_tmp.rearrange("p (h a d) -> p h a d", h=2, a=2)
                V.tensor_tensor(items(ada_tmp, 2 * DH), items(bank_of(G), 2 * DH),
                                f.unsqueeze(2).broadcast_to([P, 4, 2 * DH]), ALU.mult).then_inc(s_["pv_read"], 1)
                dve.wait_ge(s_["pv_read"], G + 1)
                c0 = 1536 + (g - 5) * 256
                dst = o[:, qt, c0:c0 + 256].rearrange("p (h d) -> p h d", h=2)
                step(V.tensor_tensor(dst, tmp[:, :, 0], tmp[:, :, 1], ALU.add)); step.wait()

            ends = {qt * NPAIR + r[-1]: qt * len(GROUPS) + g for qt in range(TT) for g, r in enumerate(GROUPS)}
            for n in range(TT * NPAIR + 3):
                if n < TT * NPAIR:
                    score(n)
                if n - 3 in ends:
                    finish(ends[n - 3])
                if n < TT * NPAIR:
                    a, b = divmod(n, 3)
                    ada_part(PLAN["ada_b"][0] + a, (0, 6, 11)[b], (6, 11, 16)[b])
                    if b == 0 and a >= 1:
                        ada_read(8 + a - 1)
            ada_read(23)
            step.wait()
            od = o[:, :, 1536:2048].rearrange("p m (h d) -> p m h d", h=DIFF)
            for m in range(TT):
                step(V.tensor_tensor(ada_tmp[:].rearrange("p (h d) -> p h d", h=DIFF), od[:, m], od[:, m], ALU.mult))
                step.wait()
                step(V.tensor_reduce(diff_ss[:, m], ada_tmp[:].rearrange("p (h d) -> p h d", h=DIFF), AX, ALU.add))
                step.wait()
            V.tensor_scalar(diff_ss[:], diff_ss[:], 1.0 / (2 * DH), EPS, ALU.mult, ALU.add).then_inc(s_["diff_in"], 1)
            dve.wait_ge(s_["diff_in"], 2)
            step(V.reciprocal(diff_ss[:], diff_ss[:])); step.wait()
            for m in range(TT):
                for f in range(DIFF):
                    step(V.scalar_tensor_tensor(od[:, m, f], od[:, m, f], diff_ss[:, m, f:f + 1], v_("subln"),
                                                ALU.mult, ALU.mult))
            step.wait()
            V.tensor_scalar(o[:, :, 1536:2048], o[:, :, 1536:2048], 1.0 - LAM_INIT, None, ALU.mult)\
                .then_inc(s_["o_ready"], 1)
            dve.wait_ge(s_["mod_ready"], 25)
            dve.wait_ge(s_["tr_free"], 8)
            V.scalar_tensor_tensor(scale_col[:], mod[:, 64:80], 1.0, v_("norm_ffn"), ALU.add, ALU.mult)\
                .then_inc(s_["mod_ready"], 1)

            def g_diag(n, col):
                V.tensor_tensor(diag[:], ident.unsqueeze(1).broadcast_to([P, KT, P]),
                                mod[:, col:col + KT].unsqueeze(2).broadcast_to([P, KT, P]), ALU.mult)\
                    .then_inc(s_["g_diag"], 1)

            def residual(name, n, used_of, rows_ready):
                acc = FIRST_ACC[name]
                dve.wait_ge(s_["g_row_ready"], rows_ready)
                for nb in range(4):
                    used_of(nb)
                    c = slice(nb * CH, nb * CH + CH)
                    s = nb % 2
                    V.tensor_tensor(g_tmp, psum[:, 2 * s:2 * s + 2], g_row[:, c].unsqueeze(1).broadcast_to([P, TT, CH]),
                                    ALU.mult).then_inc(s_["acc_free"], 1)
                    dve.wait_ge(s_["acc_free"], acc + nb + 3)
                    V.tensor_tensor(h[:, :, c], h[:, :, c], g_tmp, ALU.add).then_inc(s_["h_ready"], 1)
                    dve.wait_ge(s_["h_ready"], 4 * n + nb + 1)

            dve.wait_ge(s_["o_ready"], 1)
            dve.wait_ge(s_["pv"], TT * NPAIR)
            g_diag(0, 32)
            residual("w_out", 0, lambda nb: wait_used(dve, PLAN["w_out"][0] + nb), 1)
            rms(1)
            scale_tokens(h)
            dve.wait_ge(s_["g_sum"], 1)
            g_diag(1, 80)
            base, acc = PLAN["ffn"][0], FIRST_ACC["ffn"]
            with dve.Fori(0, 11) as i:
                dve.wait_ge(USED[1], i + base // 2 + 1)
                dve.wait_ge(s_["acc_free"], i * 2 + acc + 3)
                V.tensor_tensor(hT[:, bass.ds(i * 4, 4), :].rearrange("p k s -> p (k s)"), silu_g,
                                psum[:, 2:4].rearrange("p b n -> p (b n)"), ALU.mult).then_inc(s_["acc_free"], 1)
            residual("down", 1, lambda nb: wait_used(dve, PLAN["down"][0] + 3 * nb + 2), 2)
            dve_block2(dve, step, rms, scale_tokens)

    return nc


def layout(inputs):
    f = {k: np.asarray(v) for k, v in inputs.items()}
    one = {k: (v[0] if v.ndim and v.shape[0] == 1 else v) for k, v in f.items()}
    loads = np.zeros((N_LOADS, P, LOAD), np.float32)

    def put(name, w, first=0):
        t = tiles(w)
        loads[PLAN[name][0] + first:PLAN[name][0] + first + len(t), :, :t.shape[2]] = t

    ada = tiles(one["ada_w"])
    loads[0:8] = ada[0:8]
    loads[PLAN["ada_b"][0]:PLAN["ada_b"][0] + 16] = ada[8:]
    put("w_in", take(one["w_in"], w_in_columns()))
    put("w_out", one["w_out"][w_out_rows()])
    fa, _ = PLAN["ffn"]
    loads[fa:fa + 22:2] = tiles(one["ffn_w_gate"])
    loads[fa + 1:fa + 22:2] = tiles(one["ffn_w_up"])
    da, _ = PLAN["down"]
    down = tiles(one["ffn_w_down"]).reshape(4, P, KF, CH)
    for nb in range(4):
        for part in range(3):
            piece = down[nb, :, part * KT:(part + 1) * KT].reshape(P, -1)
            loads[da + 3 * nb + part, :, :piece.shape[1]] = piece
    block2_layout(one, loads, put)
    const, tabs = constants()
    vec = np.zeros((P, N_VEC), np.float32)

    def vput(name, a):
        at, n = VEC[name]
        vec[:a.shape[0], at:at + n] = a

    vput("c", cols(one["c"].reshape(-1)))
    vput("ada_b", cols(one["ada_b"]))
    vput("norm_mix", cols(one["norm_mix_g"]))
    vput("norm_ffn", cols(one["norm_ffn_g"]))
    vput("norm_2", cols(one["norm_g_2"]))
    vput("mem_norm", cols(one["mem_norm_g_2"]))
    vput("fox_b", rows(one["fox_f_bias"]))
    vput("lam", rows(one["diff_lambda"]))
    vput("subln", rows(one["diff_subln_g"]))
    vput("cmp_pos", np.tile(one["nsa_cmp_pos"].transpose(2, 0, 1).reshape(DH, -1), (2, 1)))
    vput("cmp_w2", one["nsa_cmp_w2"].transpose(1, 0, 2).reshape(DH, -1))
    w1 = one["nsa_cmp_w1"].reshape(2, CMP_LEN, DH, DH).transpose(2, 0, 1, 3)
    arrays = {"x": one["x"], "loads": loads, "const": const, "tabs": tabs, "vec": vec, "cmp_w1": w1}
    arrays.update(block2_arrays(one))
    return {k: np.ascontiguousarray(v) for k, v in arrays.items()}


def block2_layout(one, loads, put):
    put("mem", one["w_mem_kv_2"])
    w = one["w_in_2"]
    put("a_qk", w[:, 0:2048])
    put("a_v", w[:, 2048:3072])
    put("z_in", w[:, 3072:4096])
    put("b_in", w[:, 4096:7168])
    put("z_in", w[:, 7168:8192], 4)
    put("c_q", w[:, 8320:9344])
    put("z_in", w[:, 9344:10368], 2)
    put("gates", w[:, 10368:16512])
    at = PLAN["ups"][0]
    for i, name in enumerate(("w_up_a_2", "w_up_b_2", "w_up_c_2")):
        t = tiles(one[name])
        for j in range(2):
            loads[at + 2 * i + j] = np.concatenate([t[2 * j], t[2 * j + 1]], 1)
    put("w_o", one["w_o_2"])


def block2_arrays(one):
    q, k = np.arange(SEQ)[:, None], np.arange(SEQ)[None]
    rel = np.concatenate([one["a_rel_bias_2"], np.full((8, 1), NEG, np.float32)], 1)
    index = np.where(k // 64 <= q // 64, np.clip(q - k, -128, 128) + 128, 257)
    bias = rel[:, index]
    t = np.concatenate([bias[:, :P, :P], bias[:, P:, :]], 2).transpose(1, 0, 2).reshape(P, -1)
    gains = np.concatenate([rows(one["c_q_g_2"]), rows(one["c_k_g_2"]), rows(one["a_q_g_2"]), rows(one["a_k_g_2"]),
                            np.concatenate([one["b_mu_w_2"], one["b_mu_a_2"]])[:, None]], 1)
    b_rows = np.stack([*one["b_mu_rkv_2"], one["b_w0_2"], one["b_a0_2"], one["b_k_k_2"], one["b_k_a_2"],
                       one["b_r_k_2"].reshape(-1), one["b_ln_w_2"], one["b_ln_b_2"]])
    s, c = np.arange(P)[:, None], np.arange(P)[None]
    same = s // 64 == c // 64
    b_cst = np.concatenate([same & (s <= c), s // 64 == np.arange(2)[None]], 1).astype(np.float32)
    strict, incl = same & (s < c), same & (s <= c)
    levels = [(s // (2 * b) == c // (2 * b)) & (s // b % 2 == 0) & (c // b % 2 == 1) for b in (1, 2, 4, 8, 16, 32)]
    masks = np.concatenate([strict, incl, strict, incl, *levels], 1).astype(np.float32)
    return {"final_g": one["final_norm_g"][None], "mem": one["mem_2"], "vec2": gains, "b_rows": b_rows,
            "w2a2": np.concatenate([one["b_w2_2"], one["b_a2_2"]]), "b_cst": b_cst, "masks": masks, "a_bias": t,
            "lora_w": one["w_in_2"][:, 8192:8320].reshape(KT, P, P).transpose(1, 0, 2)}


def kernel(**inputs):
    import concourse.bacc as bacc
    from concourse.bass_utils import run_bass_kernel_spmd

    arrays = layout(inputs)
    nc = bacc.Bacc("TRN2", target_bir_lowering=False, num_devices=1)
    A = {k: nc.dram_tensor(f"in_{k}", v.shape, F32, kind="ExternalInput").ap() for k, v in arrays.items()}
    out = nc.dram_tensor("out_x", (SEQ, D), F32, kind="ExternalOutput").ap()
    hybrid_blocks(nc, A, out)
    r = run_bass_kernel_spmd(nc, [{f"in_{k}": v for k, v in arrays.items()}], core_ids=[0])
    return r.results[0]["out_x"].reshape(1, SEQ, D)
```

```python
import concourse.bass as bass
from concourse import mybir
from contextlib import ExitStack
import numpy as np

P = 128
SEQ = 256
TT = SEQ // P
D = 2048
KT = D // P
DH = 64
FOX, NSA, DIL, DIFF = 7, 8, 9, 4
N_CMP = 15
CMP_LEN, CMP_STRIDE = 32, 16
D_FF = 5632
KF = D_FF // P
CH = 512
LOAD = KT * CH
EPS = 1e-6
NEG = -1e30
LAM_INIT = 0.2

F32 = mybir.dt.float32
F32R = mybir.dt.float32r
ALU = mybir.AluOpType
ACT = mybir.ActivationFunctionType
AX = mybir.AxisListType.X

N_ADA, N_EARLY = 24, 20

PLAN = {}


def plan_loads():
    at = 0
    for name, n in (("mem", 4), ("w_in", 12), ("ada_b", N_ADA - N_EARLY), ("w_out", 4), ("ffn", 22), ("down", 12),
                    ("c_q", 2), ("a_qk", 4), ("a_v", 2), ("b_in", 6), ("z_in", 6), ("gates", 12),
                    ("ups", 6), ("w_o", 4)):
        PLAN[name] = (at, n)
        at += n
    return at


N_LOADS = plan_loads()

CONST = {}


def place(table, *items):
    at = 0
    for name, n in items:
        table[name] = (at, n)
        at += n
    return at


N_CONST = place(CONST, ("ident", 128), ("ones", 128), ("tri", 128), ("valid", 2))
N_ALIBI, N_DIL = 8, 9
N_TAB = N_ALIBI + N_DIL + 1
TAB_W = 3 * P

VEC = {}
N_VEC = place(VEC, ("c", 16), ("ada_b", 96), ("norm_mix", 16), ("norm_ffn", 16), ("norm_2", 16), ("mem_norm", 16),
              ("fox_b", FOX), ("lam", 4 * DH), ("subln", 128), ("cmp_pos", 2 * CMP_LEN), ("cmp_w2", 2 * DH))

FD_Q, NSA_Q, DIFF_Q, FD_K, DIFF_K, CMPK, CMPV, SLCK, WINK = 0, 8, 12, 16, 24, 28, 29, 30, 31
V_FD, V_SLC, V_WIN, V_DIFF, V_GATE, V_FOXF = 0, 1024, 1152, 1280, 1792, 1816
PAIRS = ([("fd", t, FD_Q + t, FD_K + t) for t in range(8)] + [("slc", t, NSA_Q + t, SLCK) for t in range(4)]
         + [("win", t, NSA_Q + t, WINK) for t in range(4)] + [("cmp", t, NSA_Q + t, None) for t in range(4)]
         + [("diff", t, DIFF_Q + t, DIFF_K + t) for t in range(4)])
NPAIR = len(PAIRS)
GROUPS = [range(0, 4), range(4, 8), range(8, 12), range(12, 16), range(16, 20), range(20, 22), range(22, 24)]
GROUP_OF = {p: g for g, r in enumerate(GROUPS) for p in r}


STEPS = [("bt", 0), ("g0", 3), ("g1", 3)]
for _l in range(6):
    STEPS += [(f"p{_l}", 2), (f"d{_l}", 4)]
STEPS += [("y", 2), ("ux", 2), ("o1", 4), ("wz", 3), ("s1", 3), ("s2", 3), ("o2", 3)]
N_BETWEEN = 14


def plan_between():
    parts, before, load, q = {}, {}, 0, 0
    for t in range(8):
        for name, n in STEPS:
            before[t, name] = load
            parts[t, name] = []
            while n and load < N_BETWEEN:
                parts[t, name].append((load, q))
                q, n = q + 1, n - 1
                if q == 2 * KT:
                    load, q = load + 1, 0
                    break
    assert q == 0 and load == N_BETWEEN, (load, q)
    return parts, before


BETWEEN, BEFORE = plan_between()


def table_of(kind, t, j):
    if kind == "fd":
        n = 2 * t + j
        return N_ALIBI + N_DIL if n < FOX else N_ALIBI + n - FOX
    if kind == "diff":
        return 2 * t + 1
    return t + 4 * j


def value_of(kind, t, j):
    if kind == "fd":
        return V_FD + (2 * t + j) * DH, DH
    if kind == "diff":
        return V_DIFF + t * 2 * DH, 2 * DH
    return (V_SLC if kind == "slc" else V_WIN) + j * DH, DH


def constants():
    c = np.zeros((P, N_CONST), np.float32)
    a, n = CONST["ident"]; c[:, a:a + n] = np.eye(P)
    a, n = CONST["ones"]; c[:, a:a + n] = 1
    a, n = CONST["tri"]; c[:, a:a + n] = np.triu(np.ones((P, P)))
    a, n = CONST["valid"]; c[:, a] = np.arange(P) >= CMP_LEN - 1; c[:, a + 1] = 1
    q = np.arange(SEQ)[:, None]
    k = np.arange(SEQ)[None]
    dist = (q - k).astype(np.float32)
    tabs = np.zeros((N_TAB, SEQ, SEQ), np.float32)
    for i in range(N_ALIBI):
        tabs[i] = np.where(dist >= 0, -np.float32(2.0 ** (-(i + 1))) * dist, NEG)
    for i in range(DIL):
        window, dil = ((128, 1), (512, 4), (2048, 16))[i // 3]
        ok = (dist >= 0) & (dist % dil == 0) & (dist <= window)
        tabs[N_ALIBI + i] = np.where(ok, -np.float32(2.0 ** (-8.0 * (i + 1) / DIL)) * dist, NEG)
    tabs[N_TAB - 1] = np.where(dist >= 0, 0, NEG)
    t = np.zeros((P, N_TAB, TAB_W), np.float32)
    t[:, :, :P] = tabs[:, :P, :P].transpose(1, 0, 2)
    t[:, :, P:] = tabs[:, P:, :].transpose(1, 0, 2)
    end = np.arange(N_CMP) * CMP_STRIDE + CMP_LEN - 1
    dc = (np.arange(SEQ)[:, None] - end[None]).astype(np.float32)
    cmp = np.stack([np.where(dc >= 0, -np.float32(2.0 ** (-(i + 1))) * dc, NEG) for i in range(8)])
    cmp = cmp.reshape(8, TT, P, N_CMP).transpose(2, 0, 1, 3).reshape(P, -1)
    return c, np.concatenate([t.reshape(P, -1), cmp], 1).astype(np.float32)


def tiles(w):
    k, n = w.shape
    return w.reshape(k // P, P, n // CH, CH).transpose(2, 1, 0, 3).reshape(n // CH, P, -1)


def cols(v):
    return v.reshape(-1, P).T


def rows(v):
    return np.broadcast_to(v.reshape(1, -1), (P, v.size))


def w_in_columns():
    names = (("fox_q", 448), ("fox_k", 448), ("fox_v", 448), ("fox_f", 7), ("nsa_q", 512), ("cmp_k", 128),
             ("cmp_v", 128), ("slc_k", 128), ("slc_v", 128), ("win_k", 128), ("win_v", 128), ("gate", 24),
             ("dil_q", 576), ("dil_k", 576), ("dil_v", 576), ("diff_q", 512), ("diff_k", 512), ("diff_v", 512))
    at, r = 0, {}
    for name, n in names:
        r[name] = np.arange(at, at + n)
        at += n
    pair = np.array([0, 4, 1, 5, 2, 6, 3, 7])
    order = [r["fox_q"], r["dil_q"], r["nsa_q"].reshape(8, 64)[pair].ravel(), r["diff_q"],
             r["fox_k"], r["dil_k"], r["diff_k"], r["cmp_k"], r["cmp_v"], r["slc_k"], r["win_k"],
             r["fox_v"], r["dil_v"], r["slc_v"], r["win_v"], r["diff_v"],
             r["gate"].reshape(8, 3)[pair].T.ravel(), r["fox_f"]]
    order = np.concatenate(order)
    return np.concatenate([order, np.full(12 * CH - order.size, -1)])


def w_out_rows():
    pair = np.array([0, 4, 1, 5, 2, 6, 3, 7])
    nsa = 448 + np.arange(512).reshape(8, 64)[pair].ravel()
    return np.concatenate([np.arange(448), 960 + np.arange(576), nsa, 1536 + np.arange(512)])


def take(w, columns):
    padded = np.concatenate([w, np.zeros((w.shape[0], 1), w.dtype)], 1)
    return padded[:, columns]


class Steps:

    def __init__(self, engine, semaphore, start=0):
        self.engine, self.semaphore, self.n = engine, semaphore, start

    def __call__(self, instruction):
        instruction.then_inc(self.semaphore, 1)
        self.n += 1
        return self.n

    def wait(self):
        self.engine.wait_ge(self.semaphore, self.n)


def hybrid_blocks(nc, A, out):
    ctx = ExitStack()
    with ctx:
        at_byte = {}

        def sb(name, *shape):
            at_byte[name] = nc.sbuf_base
            return ctx.enter_context(nc.sbuf_tensor(name, [P, *shape], F32))

        def sem(name):
            return ctx.enter_context(nc.semaphore(name))

        Wb = sb("weights", 2, LOAD)
        xT = sb("xT", KT, SEQ)
        h = sb("h", TT, D)
        xn = sb("xn", TT, D)
        arena = sb("arena", 22000)
        cst = sb("cst", N_CONST)
        misc = sb("misc", 870)
        psum = ctx.enter_context(nc.psum_tensor("psum", [P, 8, CH], F32))
        ACC, TRB, OB = 0, 4, 6

        def ada_buf(i):
            if i % 2 == 0:
                return ada_acc
            return ada_tmp[:] if i < N_EARLY else xT[:, 14:16].rearrange("p k s -> p (k s)")

        def W(slot):
            return Wb[:, slot].rearrange("p (k n) -> p k n", n=CH)

        def const(name):
            a, n = CONST[name]
            return cst[:, a:a + n]

        ident, ones, tri = const("ident"), const("ones"), const("tri")

        used_misc = [0]

        def small(n):
            a = used_misc[0]
            used_misc[0] += n
            assert used_misc[0] <= 870, used_misc[0]
            return misc[:, a:a + n]

        early = arena[:, 12288:12288 + LOAD].rearrange("p (k n) -> p k n", n=CH)
        qk = arena[:, 0:8192].rearrange("p (t s) -> p t s", s=SEQ)
        tm = arena[:, 8192:12288].rearrange("p (m n) -> p m n", m=TT)
        tabs = arena[:, 12288:12288 + N_TAB * TAB_W].rearrange("p (t w) -> p t w", w=TAB_W)
        at = 12288 + N_TAB * TAB_W
        cmp_tabs = arena[:, at:at + 8 * TT * N_CMP].rearrange("p (h m c) -> p h m c", h=8, m=TT)
        at += 8 * TT * N_CMP
        prob = arena[:, at:at + 1024].rearrange("p (b j k) -> p b j k", b=2, j=2)
        probT = arena[:, at + 1024:at + 2048].rearrange("p (b j k) -> p b j k", b=2, j=2)
        blk = arena[:, at:at + 2 * CMP_LEN * N_CMP].rearrange("p (v l c) -> p v l c", v=2, l=CMP_LEN)
        at += 2048
        ada_acc = arena[:, at:at + CH]
        at += CH
        assert at <= 22000, at
        cmp_w1 = xn[:].rearrange("p m n -> p (m n)").rearrange("p (v l e) -> p v l e", v=2, l=CMP_LEN)
        o = xn
        vec = sb("vec", 16 + 96 + 64 + FOX + 256 + 128 + 64 + 128)

        def v_(name):
            a, n = VEC[name]
            return vec[:, a:a + n]

        hT = arena[:, 0:KF * SEQ].rearrange("p (k s) -> p k s", s=SEQ)
        silu_g = arena[:, KF * SEQ:KF * SEQ + 1024]
        sig_g = arena[:, KF * SEQ + 1024:KF * SEQ + 2048]
        g_row = arena[:, 14336:14336 + D]
        xT_flat = xT[:].rearrange("p k s -> p (k s)")
        g_row2, diag2 = xT_flat[:, 2048:4096], xT_flat[:, 0:2048].rearrange("p (k n) -> p k n", n=P)
        g_tmp2 = silu_g.rearrange("p (m n) -> p m n", m=TT)
        g_tmp = arena[:, 16384:16384 + 1024].rearrange("p (m n) -> p m n", m=TT)
        diag = arena[:, 18432:18432 + 2048].rearrange("p (k n) -> p k n", n=P)


        def parts(name, byte, *shape):
            return nc.alloc_sbuf_tensor_at(name, [P, *shape], F32R, offset=byte)

        x_hi = parts("x_high", at_byte["xn"], KT, SEQ)
        x_lo = parts("x_low", at_byte["xT"], KT, SEQ)
        w_hi = parts("w_high", at_byte["arena"] + 4 * 12288, 2, KT, P)
        w_lo = parts("w_low", at_byte["arena"] + 4 * (12288 + 2 * KT * P), 2, KT, P)

        def four(parts_):
            return parts_.rearrange("p b k n -> p b (k n)").rearrange("p b (k n) -> p b k n", n=CH)

        wd_hi, wd_lo = four(w_hi[:]), four(w_lo[:])
        x_flat = x_hi[:].rearrange("p k s -> p (k s)")
        hd_hi, hd_lo = (x_flat[:, a * 2048:(a + 1) * 2048].rearrange("p (b k s) -> p b k s", b=2, s=SEQ)
                        for a in range(2))
        DOWN_UNITS = [(nb, part, k, min(4, KF - part * KT - k), k + 4 >= min(KT, KF - part * KT))
                      for nb in range(2) for part in range(3) for k in range(0, min(KT, KF - part * KT), 4)]
        N_FFN, N_DOWN = 22 * 4, len(DOWN_UNITS)

        c_act, mod, scale_col = small(16), small(96), small(16)
        stat, rstd = small(2), small(2)
        sums = small(2 * NPAIR * TT).rearrange("p (m i) -> p m i", m=TT)
        nmax = small(2 * NPAIR * TT).rearrange("p (m i) -> p m i", m=TT)
        fac = small(2 * NPAIR * TT).rearrange("p (m i) -> p m i", m=TT)
        gate = small(48).rearrange("p (m i) -> p m i", m=TT)
        logf = small(TT * FOX).rearrange("p (m i) -> p m i", m=TT)
        fz = small(TT * FOX).rearrange("p (m i) -> p m i", m=TT)
        fe = small(TT * FOX).rearrange("p (m i) -> p m i", m=TT)
        dil_e = small(DIL)
        dil_m = small(6)
        lam = small(4)
        kcT = small(N_CMP)
        vc = small(2 * DH).rearrange("p (g d) -> p g d", g=2)
        ada_tmp = sb("ada_tmp", CH)
        cz = ada_tmp[:, 0:6 * 4 * N_CMP].rearrange("p (n g v c) -> p n g v c", n=6, g=2, v=2)
        diff_ss = small(TT * DIFF).rearrange("p (m i) -> p m i", m=TT)
        crow = xT[0:1].rearrange("p k s -> p (k s)")[:, 0:2 * FOX * SEQ].rearrange("p (a h s) -> p a h s", a=2, h=FOX)

        S = {n: sem(n) for n in (
            "x_in", "const_in", "loaded0", "loaded1", "used0", "used1", "acc_free",
            "dve_step", "act_step", "ada_step", "ada_sum", "mod_ready",
            "c_exp", "stat_ready", "root_ready", "norm_ready", "tr_ready", "tr_free", 
            "tabs_in", "w1_in", "early_in0", "early_in1", "early_used", "mem_saved", "x_split", "high", "low", "unit_used", "gate_exp", "gate_done", "f_abs", "f_ln", "logf_ready",
            "crow_sum", "crow_ready", "ncrow_ready",
            "blk_ready", "cmp_hidden", "cmp_exp_in", "cmp_exp", "gelu_ready", "cmp_out", "kc_ready",
            "scores", "scored", "exps", "pt_sum", "pt_ready", "pv", "pv_read", "dil_in", "dil_exp",
            "lam_in", "lam_exp", "o_ready", "diff_in", "g_diag", "g_sum", "g_row_ready",
            "h_ready", "out_stored",
            "final_in", "mem_in", "gain_in", "lora_in", "bias_in", "bcst_in", "row_in0", "row_in1", "row_in2",
            "row_in3", "row_in4", "shift_in0", "shift_in1", "shift_in2", "zero_row", "x1_saved", "x1_back", "staged", "stored0", "stored1", "gates_in", "lerp", "w0_used",
            "a0_used", "pre_done", "masks_in", "x1_ready", "hroot_in", "hroot", "lora_sum", "lora_raw", "lora_lerp",
            "lora_ready", "head_ready", "z_used", "zw_in", "zw", "za_in", "za", "cum_sum", "c_end", "x2_free",
            "e_pos", "e_ex_in", "e_ex", "e_neg", "bt_sum", "bt", "p_sum", "p_mat", "y_sum", "y_mat", "ux_sum", "ux",
            "wz_sum", "wz", "yb_ready", "x2_done", "lora_out", "logw", "qt", "state", "o2", "g_prod", "l_mask", "dd",
            "dd_sum", "o1_sum", "qt_sum", "st_sum", "o2_sum", "up_half", "merged", "g_mask")}
        s_ = S
        LOADED, USED = [S["loaded0"], S["loaded1"]], [S["used0"], S["used1"]]
        block = ctx.enter_context(nc.Block())

        def wait_load(e, load):
            e.wait_ge(LOADED[load % 2], 16 * (load // 2 + 1))

        def wait_used(e, load):
            e.wait_ge(USED[load % 2], load // 2 + 1)

        small0 = small(2)
        DIL_AT = [qt * NPAIR + GROUPS[1][-1] + 3 for qt in range(TT)]

        def keys(n):
            qt, p = divmod(n, NPAIR)
            return N_CMP if PAIRS[p][0] == "cmp" else P * (qt + 1)

        AH, CHD, BH = 8, 4, 16
        W3 = 1024

        def tokens(at, n=W3):
            return arena[:, at:at + TT * n].rearrange("p (m n) -> p m n", m=TT)

        def tiles_at(at, n):
            return arena[:, at:at + n * SEQ].rearrange("p (t s) -> p t s", s=SEQ)

        R0 = 3 * TT * W3
        y_a, y_c, y_b = tokens(0), tokens(TT * W3), tokens(2 * TT * W3)
        mem_kv, c_q = tokens(R0, D), tokens(R0 + 4096)
        mem_x, mem_out = tokens(0, D), tokens(8192, D)
        mem_dram = nc.dram_tensor("mem_kept", (P, TT * D), F32, kind="Internal").ap()
        c_qT, c_kT = tiles_at(R0 + 6144, 8), tiles_at(R0 + 8192, 8)
        prob2 = arena[:, R0 + 10240:R0 + 11264].rearrange("p (b j k) -> p b j k", b=2, j=2)
        prob2T = arena[:, R0 + 11264:R0 + 12288].rearrange("p (b j k) -> p b j k", b=2, j=2)
        final_row = arena[:, 14336:14336 + D]
        c_gain = vec[:, 176:176 + 512].rearrange("p (a d) -> p a d", a=2)
        a_gain = ada_tmp[:, 0:256].rearrange("p (a d) -> p a d", a=2)
        mu_wa = vec[:, 700:701]
        a_qk, a_v = tokens(R0, D), tokens(R0 + 4096)
        a_qT, a_kT = tiles_at(R0 + 6144, 8), tiles_at(R0 + 8192, 8)
        a_bias = arena[:, R0 + 12288:R0 + 12288 + AH * TAB_W].rearrange("p (h w) -> p h w", w=TAB_W)
        b_r, b_k, b_v = tokens(R0), tokens(R0 + 2048), tokens(R0 + 4096)
        b_a, b_b = tokens(R0 + 6144), tokens(R0 + 8192)
        row_slot = [arena[:, R0 + 10240 + s * W3:R0 + 10240 + (s + 1) * W3] for s in range(5)]
        silu_z = arena[:, R0 + 8192:R0 + 8192 + W3]
        X1 = xn[:].rearrange("p m n -> p (m n)")[:, 0:2048].rearrange("p (m n) -> p m n", m=TT)
        X2 = xn[:].rearrange("p m n -> p (m n)")[:, 2048:4096].rearrange("p (m n) -> p m n", m=TT)
        lora_w = xn[:].rearrange("p m n -> p (m n)")[:, 0:2048].rearrange("p (k n) -> p k n", k=KT)
        lora = ada_tmp[:, 256:512]
        lora_d = arena[:, R0 + 15360:R0 + 15360 + SEQ]
        c_end = arena[:, R0 + 15616:R0 + 15616 + 32].rearrange("p (t c) -> p t c", t=8)
        AR = row_slot[0][:, 0:512].rearrange("p (m n) -> p m n", m=TT)
        BK = row_slot[0][:, 512:1024].rearrange("p (a s) -> p a s", a=2)
        WZ = row_slot[1][:, 0:512].rearrange("p (c a n) -> p c a n", c=4, a=2)
        ST = row_slot[1][:, 512:512 + 192].rearrange("p (c n) -> p c n", c=3)
        S_tmp = row_slot[1][:, 704:768]
        lev = row_slot[2][:, 0:768].rearrange("p (l n) -> p l n", l=6)
        XF = xn[:].rearrange("p m n -> p (m n)")
        Gs = XF[:, 0:2048].rearrange("p (u a n) -> p u a n", u=4, a=4)
        DD = XF[:, 2048:3072].rearrange("p (u a n) -> p u a n", u=4, a=2)
        Pm = XF[:, 3072:3584].rearrange("p (u n) -> p u n", u=4)
        Lm = XF[:, 3584:4096].rearrange("p (u n) -> p u n", u=4)
        Yb = XF[:, 3584:3840].rearrange("p (u n) -> p u n", u=4)
        UX = XF[:, 3072:3584].rearrange("p (u n) -> p u n", u=4)
        gmask = ada_tmp[:].rearrange("p (a n) -> p a n", a=4)
        b_cst = vec[:, 176:176 + 130]
        btri, bind = b_cst[:, 0:P], b_cst[:, P:P + 2]
        hs = small(96).rearrange("p (a m h) -> p a m h", a=3, m=TT)
        hs_a, hs_r, bonus = hs[:, 0], hs[:, 1], hs[:, 2]
        gates_ = arena[:, R0:R0 + TT * 6144].rearrange("p (m n) -> p m n", m=TT)
        yT = [xT[:, 0:8], xT[:, 8:16], tiles_at(R0 + 12288, 8)]
        x1_dram = nc.dram_tensor("x1_kept", (P, TT * D), F32, kind="Internal").ap()
        gates_dram = nc.dram_tensor("gates_kept", (12, P, TT * CH), F32, kind="Internal").ap()
        HF = h[:].rearrange("p m n -> p (m n)")
        stage = [HF[:, i * 1024:(i + 1) * 1024] for i in range(2)]
        silu_zb = [HF[:, 2048 + i * 1024:2048 + (i + 1) * 1024] for i in range(2)]

        SPLIT = {"c_q": 0, "a_qk": 2, "a_v": 6, "w_o": 8}
        t_hi = parts("tokens_high", at_byte["arena"], 2, 4, SEQ)
        t_lo = parts("tokens_low", at_byte["arena"] + 4 * 4096, 2, 4, SEQ)

        def unit0(name):
            return N_FFN + 2 * N_DOWN + 4 * SPLIT[name]

        def low0(name):
            return N_FFN * 3 // 4 + 2 * (N_DOWN - 6) + 3 * SPLIT[name]

        def units(first, pairs):
            return [(first + i, i // pairs, i % pairs) for i in range(TT * pairs)]

        U0 = TT * NPAIR
        C_UNITS = units(U0, CHD // 2)
        A_UNITS = units(U0 + len(C_UNITS), AH // 2)
        G0 = TT * len(GROUPS) - U0

        def pool_block2(pool):

            def repeated(dst, name, i=0, n=W3):
                return pool.dma_start(dst, A[name][i:i + 1, 0:n].broadcast_to([P, n]))

            pool.wait_ge(s_["h_ready"], 8)
            repeated(final_row, "final_g", 0, D).then_inc(s_["final_in"], 16)
            pool.wait_ge(s_["mem_saved"], 16)
            pool.dma_start(arena[:, R0:R0 + TT * D], mem_dram).then_inc(s_["mem_in"], 16)
            pool.dma_start(vec[:, 176:176 + 512], A["vec2"][:, 0:512]).then_inc(s_["gain_in"], 16)
            pool.dma_start(ada_tmp[:, 0:256], A["vec2"][:, 512:768]).then_inc(s_["gain_in"], 16)
            pool.dma_start(mu_wa, A["vec2"][:, 768:769], allow_slow_non_contiguous=True).then_inc(s_["gain_in"], 16)
            pool.wait_ge(s_["x1_ready"], 2)
            pool.dma_start(x1_dram, HF).then_inc(s_["x1_saved"], 16)
            pool.wait_ge(s_["tr_free"], 4 * 8 + 8)
            pool.dma_start(lora_w, A["lora_w"]).then_inc(s_["lora_in"], 16)
            pool.wait_ge(s_["acc_free"], FIRST_ACC["a_v"] + 4)
            pool.dma_start(a_bias.rearrange("p h w -> p (h w)"), A["a_bias"]).then_inc(s_["bias_in"], 16)
            pool.wait_ge(s_["pv_read"], G0 + A_UNITS[-1][0] + 1)
            pool.dma_start(b_cst, A["b_cst"]).then_inc(s_["bcst_in"], 16)
            pool.dma_start(row_slot[3], A["w2a2"]).then_inc(s_["row_in3"], 16)
            for slot, i in ((0, 0), (1, 1), (2, 2), (4, 3)):
                repeated(row_slot[slot], "b_rows", i).then_inc(s_[f"row_in{slot}"], 16)
            for i, (src, dst) in enumerate(((b_r, X1), (b_k, X2), (b_v, X1))):
                pool.wait_ge(s_["acc_free"], FIRST_ACC["b_in"] + 2 * i + 4)
                if i == 0:
                    pool.wait_ge(s_["lora_sum"], 1)
                    pool.memset(X1[0:1, 0], 0.0).then_inc(s_["zero_row"], 1)
                    pool.memset(X2[0:1, 0], 0.0).then_inc(s_["zero_row"], 1)
                if i == 2:
                    pool.wait_ge(s_["lerp"], 1)
                    pool.memset(X1[0:1, 0], 0.0).then_inc(s_["zero_row"], 1)
                pool.dma_start(dst[1:P, 0], src[0:P - 1, 0]).then_inc(s_[f"shift_in{i}"], 16)
                pool.dma_start(dst[1:P, 1], src[0:P - 1, 1]).then_inc(s_[f"shift_in{i}"], 16)
                pool.dma_start(dst[0:1, 1], src[P - 1:P, 0]).then_inc(s_[f"shift_in{i}"], 16)
            pool.wait_ge(s_["lerp"], 3)
            for slot, i in ((0, 5), (1, 6), (2, 7)):
                repeated(row_slot[slot], "b_rows", i).then_inc(s_[f"row_in{slot}"], 16)
            pool.wait_ge(s_["w0_used"], 1)
            repeated(row_slot[4], "b_rows", 4).then_inc(s_["row_in4"], 16)
            pool.wait_ge(s_["a0_used"], 1)
            repeated(row_slot[3], "b_rows", 8).then_inc(s_["row_in3"], 16)
            repeated(row_slot[4], "b_rows", 9).then_inc(s_["row_in4"], 16)
            pool.wait_ge(s_["pre_done"], 1)
            pool.dma_start(lev.rearrange("p l n -> p (l n)"), A["masks"][:, 512:1280]).then_inc(s_["masks_in"], 16)
            pool.dma_start(ada_tmp[:], A["masks"][:, 0:512]).then_inc(s_["masks_in"], 16)
            for g in range(12):
                pool.wait_ge(s_["staged"], g + 1)
                pool.dma_start(gates_dram[g], stage[g % 2]).then_inc(s_[f"stored{g % 2}"], 16)
            for s in range(2):
                pool.wait_ge(s_[f"stored{s}"], 96)
            pool.wait_ge(s_["yb_ready"], 1)
            for g in range(12):
                pool.dma_start(gates_[:, :, g * CH:(g + 1) * CH],
                               gates_dram[g].rearrange("p (m n) -> p m n", m=TT)).then_inc(s_["gates_in"], 16)
            pool.wait_ge(s_["z_used"], 6)
            pool.dma_start(HF, x1_dram).then_inc(s_["x1_back"], 16)

        def act_block2(act, step, copy, square_sums, read_transposes):
            A_ = nc.scalar.activation
            act.wait_ge(s_["h_ready"], 8)
            square_sums(h, 3)
            act.wait_ge(s_["x1_ready"], 2)
            square_sums(h, 4)

            def split_tokens(name, dst=None):
                base, n = PLAN[name]

                def read(i):
                    act.wait_ge(s_["unit_used"], unit0(name) + 4 * i + 6)
                    copy(dst[:, :, i * CH:(i + 1) * CH], psum[:, 2 * (i % 2):2 * (i % 2) + 2])\
                        .then_inc(s_["acc_free"], 1)

                for i in range(n):
                    act.wait_ge(LOADED[i % 2], 16 * ((base + i) // 2 + 1))
                    for q in range(4):
                        if q == 2 and i and dst is not None:
                            read(i - 1)
                        act.wait_ge(s_["unit_used"], unit0(name) + 4 * i + q + 1)
                        copy(t_hi[:, q % 2], xT[:, 4 * q:4 * q + 4])
                        copy(wd_hi[:, q % 2], W(i % 2)[:, 4 * q:4 * q + 4]).then_inc(s_["high"], 1)
                if dst is not None:
                    read(n - 1)

            def read_tokens(name, dst, first=0, count=None):
                base, n = PLAN[name]
                base, n = base + first, (n if count is None else count)
                for i in range(n):
                    wait_used(act, base + i)
                    copy(dst[:, :, i * CH:(i + 1) * CH], psum[:, 2 * (i % 2):2 * (i % 2) + 2])\
                        .then_inc(s_["acc_free"], 1)

            def head_roots(n):
                act.wait_ge(s_["hroot_in"], n + 1)
                A_(hs_a, hs_a, ACT.Sqrt).then_inc(s_["hroot"], 1)

            def unit_exps(n, qt, t, from_psum):
                act.wait_ge(s_["scored"], n + 1)
                if n - U0 >= 2 and from_psum:
                    act.wait_ge(s_["pt_sum"], n - 1)
                for j in range(2):
                    nk = SEQ if from_psum else P * (qt + 1)
                    src = psum[:, 2 * (n % 2) + j, 0:nk] if from_psum else prob2[:, n % 2, j, 0:nk]
                    A_(prob2[:, n % 2, j, 0:nk], src, ACT.Exp, bias=nmax[:, qt, 2 * t + j:2 * t + j + 1],
                       accum_out=sums[:, qt, 2 * t + j:2 * t + j + 1]).then_inc(s_["exps"], 1)

            def unit_probT(n, qt, from_psum):
                nk = SEQ if from_psum else P * (qt + 1)
                act.wait_ge(s_["pt_sum"], n + 1)
                act.wait_ge(s_["pv"], n - 1)
                copy(prob2T[:, n % 2, :, 0:nk], psum[:, TRB].rearrange("p (j k) -> p j k", j=2)[:, :, 0:nk])\
                    .then_inc(s_["pt_ready"], 1)

            def attention(list_, from_psum):
                for i in range(len(list_) + 1):
                    if i < len(list_):
                        unit_exps(*list_[i], from_psum)
                    if i:
                        unit_probT(*list_[i - 1][:2], from_psum)

            read_transposes(KT, v_("norm_2"))
            act.wait_ge(s_["lora_sum"], 1)
            copy(lora, psum[:, OB, 0:SEQ]).then_inc(s_["lora_raw"], 1)
            act.wait_ge(s_["lora_lerp"], 1)
            A_(lora[0:DH], lora[0:DH], ACT.Tanh).then_inc(s_["lora_ready"], 1)
            split_tokens("c_q", c_q)
            head_roots(0)
            act.wait_ge(s_["head_ready"], 1)
            read_transposes(8, dst=c_qT, factor=256 ** -0.5)
            head_roots(1)
            act.wait_ge(s_["head_ready"], 2)
            read_transposes(8, dst=c_kT)
            attention(C_UNITS, True)
            act.wait_ge(s_["pv"], C_UNITS[-1][0] + 1)
            split_tokens("a_qk", a_qk)
            split_tokens("a_v", a_v)
            head_roots(2)
            read_transposes(8, dst=a_qT, factor=128 ** -0.5)
            head_roots(3)
            read_transposes(8, dst=a_kT)
            attention(A_UNITS, False)
            act.wait_ge(s_["pv_read"], G0 + A_UNITS[-1][0] + 1)
            for i, dst in enumerate((b_r, b_k, b_v)):
                read_tokens("b_in", dst, 2 * i, 2)
            for i in range(4):
                wait_used(act, PLAN["z_in"][0] + i)
                if i:
                    act.wait_ge(s_["z_used"], i)
                A_(silu_z, psum[:, 2 * (i % 2):2 * (i % 2) + 2].rearrange("p b n -> p (b n)"), ACT.Silu)\
                    .then_inc(s_["acc_free"], 1)
            act.wait_ge(s_["zw_in"], 1)
            A_(X1, X1, ACT.Tanh, scale=0.5).then_inc(s_["zw"], 1)
            act.wait_ge(s_["za_in"], 1)
            A_(b_b, b_b, ACT.Tanh, scale=0.5).then_inc(s_["za"], 1)
            act.wait_ge(s_["hroot_in"], 5)
            A_(hs_a, hs_a, ACT.Sqrt).then_inc(s_["hroot"], 1)
            cum = psum[:, 0:4].rearrange("p (m b) n -> p m (b n)", m=TT)
            act.wait_ge(s_["cum_sum"], 1)
            A_(c_end.rearrange("p t c -> p (t c)"), psum[:, OB, 0:32], ACT.Exp).then_inc(s_["c_end"], 1)
            act.wait_ge(s_["x2_free"], 1)
            A_(X2, cum, ACT.Exp).then_inc(s_["e_pos"], 1)
            act.wait_ge(s_["e_ex_in"], 1)
            A_(X2, X2, ACT.Exp).then_inc(s_["e_ex"], 1)
            act.wait_ge(s_["x2_free"], 2)
            A_(X2, cum, ACT.Exp, scale=-1.0).then_inc(s_["e_neg"], 1)
            def between(t, step_name):
                while done[0] < BEFORE[t, step_name]:
                    i = done[0]
                    wait_used(act, PLAN["z_in"][0] + 4 + i)
                    src = psum[:, 0:2].rearrange("p b n -> p (b n)")
                    if i < 2:
                        if i == 0:
                            act.wait_ge(s_["x1_saved"], 16)
                        A_(silu_zb[i], src, ACT.Silu).then_inc(s_["acc_free"], 1)
                    else:
                        g = i - 2
                        if g >= 2:
                            act.wait_ge(s_[f"stored{g % 2}"], 16 * (g // 2))
                        A_(stage[g % 2], src, ACT.Sigmoid).then_inc(s_["acc_free"], 1)
                        act.wait_ge(s_["acc_free"], FIRST_ACC["gates"] + g + 3)
                        copy(small0[:, 0:1], cst[:, 0:1]).then_inc(s_["staged"], 1)
                    done[0] += 1

            done = [0]
            for t in range(8):
                between(t, "bt")
                for r, dst in enumerate((AR.rearrange("p m n -> p (m n)"), BK.rearrange("p a n -> p (a n)"))):
                    act.wait_ge(s_["bt_sum"], 2 * t + r + 1)
                    if r == 0 and t:
                        act.wait_ge(s_["o2_sum"], t)
                    copy(dst, psum[:, 4 + r]).then_inc(s_["bt"], 1)
                between(t, "g1")
                for l in range(6):
                    between(t, f"p{l}")
                    act.wait_ge(s_["p_sum"], 6 * t + l + 1)
                    copy(Pm.rearrange("p u n -> p (u n)"), psum[:, 4]).then_inc(s_["p_mat"], 1)
                between(t, "y")
                act.wait_ge(s_["y_sum"], t + 1)
                copy(Yb.rearrange("p u n -> p (u n)"), psum[:, 7, 0:256]).then_inc(s_["y_mat"], 1)
                act.wait_ge(s_["ux_sum"], t + 1)
                copy(UX.rearrange("p u n -> p (u n)"), psum[:, 4]).then_inc(s_["ux"], 1)
                between(t, "wz")
                act.wait_ge(s_["wz_sum"], t + 1)
                for c in range(4):
                    ins = copy(WZ[:, c].rearrange("p a n -> p (a n)"),
                               psum[:, 2 + c % 2, (c // 2) * P:(c // 2 + 1) * P])
                ins.then_inc(s_["wz"], 1)
                between(t, "s1")
                between(t, "s2")
                between(t, "o2")
            act.wait_ge(s_["hroot_in"], 6)
            A_(hs_a, hs_a, ACT.Sqrt).then_inc(s_["hroot"], 1)
            assert done[0] == N_BETWEEN
            for b in range(3):
                read_transposes(8, dst=yT[b])
            read_transposes(KT)
            split_tokens("w_o")
            act.wait_ge(s_["x2_done"], 4)
            act.dma_start(out.rearrange("(m p) n -> p m n", p=P), h[:]).then_inc(s_["out_stored"], 16)

        def pe_block2(pe, transposes, tokens_product, rounds):
            mm = nc.tensor.matmul

            def attention(list_, scores_of, v_of, from_psum):
                def scores(n, qt, t):
                    if n - U0 >= 2 or list_ is A_UNITS:
                        if from_psum or list_[0][0] + 2 > n:
                            pe.wait_ge(s_["exps"], 2 * (n - 1))
                        else:
                            pe.wait_ge(s_["scored"], n - 1)
                    for j in range(2):
                        ins = scores_of(psum[:, 2 * (n % 2) + j], qt, 2 * t + j)
                    ins.then_inc(s_["scores"], 1)

                def probT(n, qt, t):
                    nk = SEQ if from_psum else P * (qt + 1)
                    pe.wait_ge(s_["exps"], 2 * n + 2)
                    pe.wait_ge(s_["pt_ready"], n)
                    for j in range(2):
                        for a in range(0, nk, P):
                            ins = nc.tensor.transpose(psum[:, TRB, j * SEQ + a:j * SEQ + a + P],
                                                      prob2[:, n % 2, j, a:a + P], ident)
                    ins.then_inc(s_["pt_sum"], 1)

                def values(n, qt, t):
                    nk = SEQ if from_psum else P * (qt + 1)
                    pe.wait_ge(s_["pt_ready"], n + 1)
                    pe.wait_ge(s_["pv_read"], G0 + n - 1)
                    for j in range(2):
                        v, w = v_of(2 * t + j)
                        for m in range(nk // P):
                            ins = mm(psum[:, OB + n % 2, j * w:(j + 1) * w], prob2T[:, n % 2, j, m * P:(m + 1) * P],
                                     v[:, m], start=(m == 0), stop=(m == nk // P - 1))
                    ins.then_inc(s_["pv"], 1)

                for i in range(len(list_) + 2):
                    if i < len(list_):
                        scores(*list_[i])
                    if 1 <= i <= len(list_):
                        probT(*list_[i - 1])
                    if i >= 2:
                        values(*list_[i - 2])

            def split_product(name):
                base, n_loads = PLAN[name]
                with pe.Fori(0, n_loads // 2) as i:
                    for s in range(2):
                        pe.wait_ge(s_["acc_free"], i * 2 + (FIRST_ACC[name] + s + 1))
                        for q in range(4):
                            pe.wait_ge(s_["high"], i * 8 + (unit0(name) + 4 * s + q + 1))
                            for w, x in ((wd_hi, t_hi), (wd_hi, t_lo), (wd_lo, t_hi)):
                                if x is t_lo and q == 3:
                                    pe.wait_ge(USED[s], i + (base // 2 + 1))
                                elif x is t_lo:
                                    pe.wait_ge(s_["low"], i * 6 + (low0(name) + 3 * s + q + 1))
                                for m in range(TT):
                                    for k in range(4):
                                        ins = mm(psum[:, 2 * s + m], x[:, q % 2, k, m * P:(m + 1) * P], w[:, q % 2, k],
                                                 start=(q == 0 and k == 0 and w is wd_hi and x is t_hi),
                                                 stop=(q == 3 and k == 3 and w is wd_lo), skip_group_check=True)
                            ins.then_inc(s_["unit_used"], 1)

            pe.wait_ge(s_["norm_ready"], 8)
            transposes(xn, KT)
            pe.wait_ge(s_["tr_free"], rounds[0])
            pe.wait_ge(s_["lora_in"], 16)
            for k in range(KT):
                ins = mm(psum[:, OB, 0:SEQ], lora_w[:, k], xT[:, k], start=(k == 0), stop=(k == KT - 1))
            ins.then_inc(s_["lora_sum"], 1)
            split_product("c_q")
            for i, src in enumerate((c_q, mem_kv)):
                pe.wait_ge(s_["head_ready"], i + 1)
                transposes(src, 8)
            pe.wait_ge(s_["tr_free"], rounds[0])

            def c_scores(bank, qt, n):
                for a in range(2):
                    ins = mm(bank[:, 0:SEQ], c_qT[:, 2 * n + a, qt * P:(qt + 1) * P], c_kT[:, 2 * n + a],
                             start=(a == 0), stop=(a == 1))
                return ins

            attention(C_UNITS, c_scores, lambda n: (mem_kv[:, :, W3 + n * 256:W3 + (n + 1) * 256], 256), True)
            split_product("a_qk")
            split_product("a_v")
            for i in range(2):
                pe.wait_ge(s_["head_ready"], i + 3)
                transposes(a_qk[:, :, i * W3:(i + 1) * W3], 8)
            pe.wait_ge(s_["tr_free"], rounds[0])

            def a_scores(bank, qt, n):
                nk = P * (qt + 1)
                return mm(bank[:, 0:nk], a_qT[:, n, qt * P:(qt + 1) * P], a_kT[:, n, 0:nk], start=True, stop=True)

            attention(A_UNITS, a_scores, lambda n: (a_v[:, :, n * P:(n + 1) * P], P), False)
            tokens_product("b_in")
            tokens_product("z_in", 0, 4)
            pe.wait_ge(s_["acc_free"], FIRST_ACC["z_in"] + 4 + 2)
            pe.wait_ge(s_["row_in3"], 16)
            pe.wait_ge(s_["lora_ready"], 1)
            for a in range(2):
                r = slice(a * DH, (a + 1) * DH)
                for m in range(TT):
                    for c in range(2):
                        ins = mm(psum[:, 4 * a + 2 * m + c], lora[r, m * P:(m + 1) * P],
                                 row_slot[3][r, c * CH:(c + 1) * CH], start=True, stop=True)
                ins.then_inc(s_["lora_out"], 1)
            pe.wait_ge(s_["logw"], 1)
            pe.wait_ge(s_["bcst_in"], 16)
            for m in range(TT):
                for t in range(8):
                    mm(psum[:, OB, t * 4 + 2 * m:t * 4 + 2 * m + 2], X1[:, m, t * P:(t + 1) * P], bind,
                       start=True, stop=True)
            for m in range(TT):
                for c in range(2):
                    ins = mm(psum[:, 2 * m + c], btri, X1[:, m, c * CH:(c + 1) * CH], start=True, stop=True)
            ins.then_inc(s_["cum_sum"], 1)
            pe.wait_ge(s_["pre_done"], 1)

            def between(t, step_name):
                for i, q in BETWEEN[t, step_name]:
                    load = PLAN["z_in"][0] + 4 + i
                    m, k = divmod(q, KT)
                    if q == 0:
                        wait_load(pe, load)
                        pe.wait_ge(s_["acc_free"], FIRST_ACC["z_in"] + 4 + i + 2)
                    ins = mm(psum[:, m], xT[:, k, m * P:(m + 1) * P], W(load % 2)[:, k],
                             start=(k == 0), stop=(k == KT - 1))
                    if q == 2 * KT - 1:
                        ins.then_inc(USED[load % 2], 1)

            for t in range(8):
                cs = slice(t * P, (t + 1) * P)
                if t:
                    pe.wait_ge(s_["wz"], t)
                    pe.wait_ge(s_["qt"], t)
                for r, order in enumerate((((b_a, 0), (b_r, 0), (b_a, 1), (b_r, 1)),
                                           ((b_b, 0), (b_b, 1), (b_k, 0), (b_k, 1)))):
                    for i, (src, m) in enumerate(order):
                        ins = nc.tensor.transpose(psum[:, 4 + r, i * P:(i + 1) * P], src[:, m, cs], ident)
                    ins.then_inc(s_["bt_sum"], 1)
                pe.wait_ge(s_["bt"], 2 * t + 2)
                if t:
                    pe.wait_ge(s_["o2"], t)
                for u in range(4):
                    if u == 2:
                        ins.then_inc(s_["g_prod"], 1)
                        between(t, "g0")
                        pe.wait_ge(s_["g_mask"], 4 * t + 2)
                    r = slice((u // 2) * DH, (u // 2 + 1) * DH)
                    m = u % 2
                    for a in range(2):
                        ins = mm(psum[:, 2 + u % 2, a * 256:(a + 1) * 256], BK[r, a, m * P:(m + 1) * P], AR[r, m],
                                 start=True, stop=True)
                ins.then_inc(s_["g_prod"], 1)
                between(t, "g1")
                for l in range(6):
                    pe.wait_ge(s_["l_mask"], 6 * t + l + 1)
                    pe.wait_ge(s_["dd"], 7 * t + l + 1)
                    for u in range(4):
                        ins = mm(psum[:, 4, u * P:(u + 1) * P], Lm[:, u], DD[:, u, 0], start=True, stop=True)
                    ins.then_inc(s_["p_sum"], 1)
                    between(t, f"p{l}")
                    pe.wait_ge(s_["p_mat"], 6 * t + l + 1)
                    for u in range(4):
                        bank = psum[:, 5 + u // 2]
                        o_ = (u % 2) * 256
                        mm(bank[:, o_:o_ + P], DD[:, u, 1], Pm[:, u], start=True, stop=True)
                        ins = mm(bank[:, o_ + P:o_ + 256], Pm[:, u], DD[:, u, 1], start=True, stop=True)
                    ins.then_inc(s_["dd_sum"], 1)
                    between(t, f"d{l}")
                for u in range(4):
                    hc = slice(t * P + (u // 2) * DH, t * P + (u // 2 + 1) * DH)
                    ins = mm(psum[:, 7, u * DH:(u + 1) * DH], Gs[:, u, 2], b_v[:, u % 2, hc], start=True, stop=True)
                ins.then_inc(s_["y_sum"], 1)
                between(t, "y")
                pe.wait_ge(s_["dd"], 7 * t + 7)
                pe.wait_ge(s_["y_mat"], t + 1)
                for u in range(4):
                    hc = slice(t * P + (u // 2) * DH, t * P + (u // 2 + 1) * DH)
                    mm(psum[:, 4, u * P:u * P + DH], DD[:, u, 1], Yb[:, u], start=True, stop=True)
                    ins = mm(psum[:, 4, u * P + DH:(u + 1) * P], DD[:, u, 1], b_a[:, u % 2, hc], start=True, stop=True)
                ins.then_inc(s_["ux_sum"], 1)
                between(t, "ux")
                pe.wait_ge(s_["ux"], t + 1)
                for u in range(4):
                    hc = slice(t * P + (u // 2) * DH, t * P + (u // 2 + 1) * DH)
                    mm(psum[:, 7, u * DH:(u + 1) * DH], Gs[:, u, 1], UX[:, u, 0:DH], start=True, stop=False)
                    ins = mm(psum[:, 7, u * DH:(u + 1) * DH], Gs[:, u, 3], b_v[:, u % 2, hc], start=False, stop=True)
                ins.then_inc(s_["o1_sum"], 1)
                for u in range(4):
                    r = slice((u // 2) * DH, (u // 2 + 1) * DH)
                    ins = mm(psum[r, 5, (u % 2) * P:(u % 2 + 1) * P], UX[:, u, DH:P], Gs[:, u, 1],
                             start=True, stop=True)
                ins.then_inc(s_["qt_sum"], 1)
                between(t, "o1")
                pe.wait_ge(s_["g_mask"], 4 * t + 4)
                for c2 in range(2):
                    kr = slice(c2 * DH, (c2 + 1) * DH)
                    for u in range(4):
                        m = u % 2
                        hc = slice(t * P + (u // 2) * DH, t * P + (u // 2 + 1) * DH)
                        r = slice((u // 2) * DH, (u // 2 + 1) * DH)
                        at = m * P
                        mm(psum[r, 2 + c2, at:at + DH], UX[kr, u, DH:P], b_b[kr, m, hc], start=True, stop=True)
                        mm(psum[r, 2 + c2, at + DH:at + P], b_b[kr, m, hc], UX[kr, u, 0:DH], start=True, stop=False)
                        ins = mm(psum[r, 2 + c2, at + DH:at + P], b_k[kr, m, hc], b_v[kr, m, hc], start=False, stop=True)
                ins.then_inc(s_["wz_sum"], 1)
                between(t, "wz")
                pe.wait_ge(s_["wz"], t + 1)
                for c in range(1, 3):
                    pe.wait_ge(s_["state"], 3 * t + c)
                    for h2 in range(2):
                        r = slice(h2 * DH, (h2 + 1) * DH)
                        ins = mm(psum[r, 7, 256 + c * DH:256 + (c + 1) * DH], WZ[r, c, 0], ST[r, c - 1], start=True, stop=True)
                    ins.then_inc(s_["st_sum"], 1)
                    between(t, f"s{c}")
                pe.wait_ge(s_["state"], 3 * t + 3)
                pe.wait_ge(s_["qt"], t + 1)
                pe.wait_ge(s_["dd"], 7 * t + 7)
                for h2 in range(2):
                    r = slice(h2 * DH, (h2 + 1) * DH)
                    for c in range(1, 4):
                        kr = slice((c % 2) * DH, (c % 2 + 1) * DH)
                        ins = mm(psum[kr, 2 + h2, (c // 2) * DH:(c // 2 + 1) * DH],
                                 AR[r, c // 2, P + (c % 2) * DH:P + (c % 2 + 1) * DH], ST[r, c - 1],
                                 start=True, stop=True)
                ins.then_inc(s_["o2_sum"], 1)
                between(t, "o2")
            for i, y in enumerate((y_a, y_c, y_b)):
                if i == 2:
                    pe.wait_ge(s_["z_used"], 6)
                transposes(y, 8)
            pe.wait_ge(s_["tr_free"], rounds[0])
            base, acc = PLAN["ups"][0], FIRST_ACC["ups"]
            for i in range(6):
                load = base + i
                wait_load(pe, load)
                for n2 in range(2):
                    pe.wait_ge(s_["acc_free"], acc + 2 * i + n2 + 1)
                    for m in range(TT):
                        for k in range(8):
                            ins = mm(psum[:, 2 * n2 + m], yT[(0, 2, 1)[i // 2]][:, k, m * P:(m + 1) * P], W(load % 2)[:, 8 * n2 + k],
                                     start=(k == 0), stop=(k == 7))
                    if n2 == 0:
                        ins.then_inc(s_["up_half"], 1)
                ins.then_inc(USED[load % 2], 1)
            pe.wait_ge(s_["merged"], 12)
            transposes(xn, KT)
            pe.wait_ge(s_["tr_free"], rounds[0])
            split_product("w_o")

        def dve_block2(dve, step, rms, scale_tokens):
            V = nc.vector
            rms(3)
            dve.wait_ge(s_["final_in"], 16)
            for m in range(TT):
                V.scalar_tensor_tensor(h[:, m], h[:, m], rstd[:, m:m + 1], final_row, ALU.mult, ALU.mult)\
                    .then_inc(s_["x1_ready"], 1)
            rms(4)
            scale_tokens(h)
            dve.wait_ge(s_["gain_in"], 48)
            dve.wait_ge(s_["lora_raw"], 1)
            step(V.tensor_scalar(lora_d[:, 0:1], lora[:, 0:1], -1.0, None, ALU.mult))
            step(V.tensor_tensor(lora_d[:, 1:SEQ], lora[:, 0:SEQ - 1], lora[:, 1:SEQ], ALU.subtract)); step.wait()
            V.scalar_tensor_tensor(lora, lora_d, mu_wa, lora, ALU.mult, ALU.add).then_inc(s_["lora_lerp"], 1)

            def split_tokens(name, residual=None):
                base, n = PLAN[name]
                for i in range(n):
                    for q in range(4):
                        if q == 2 and i and residual:
                            residual(i - 1)
                        dve.wait_ge(s_["high"], unit0(name) + 4 * i + q + 1)
                        V.tensor_tensor(t_lo[:, q % 2], xT[:, 4 * q:4 * q + 4], t_hi[:, q % 2].bitcast(F32), ALU.subtract)
                        V.tensor_tensor(wd_lo[:, q % 2], W(i % 2)[:, 4 * q:4 * q + 4], wd_hi[:, q % 2].bitcast(F32),
                                        ALU.subtract).then_inc(USED[i % 2] if q == 3 else s_["low"], 1)
                if residual:
                    residual(n - 1)

            split_tokens("c_q")

            def head_norm(x, heads, gain, n, last, width=None, tmp=X1):
                w = W3 // heads
                xh = x.rearrange("p m (h d) -> p m h d", h=heads)
                th = tmp.rearrange("p m (h d) -> p m h d", h=heads)
                step(V.tensor_tensor(tmp, x, x, ALU.mult)); step.wait()
                step(V.tensor_reduce(hs_r[:, :, 0:heads], th, AX, ALU.add)); step.wait()
                if n == 0:
                    step(V.memset(hs_a, 1.0)); step.wait()
                V.tensor_scalar(hs_a[:, :, 0:heads], hs_r[:, :, 0:heads], 1.0 / w, EPS, ALU.mult, ALU.add)\
                    .then_inc(s_["hroot_in"], 1)
                dve.wait_ge(s_["hroot"], n + 1)
                step(V.reciprocal(hs_r[:, :, 0:heads], hs_a[:, :, 0:heads])); step.wait()
                for m in range(TT):
                    step(V.tensor_tensor(th[:, m], xh[:, m], hs_r[:, m, 0:heads].unsqueeze(2).broadcast_to([P, heads, w]),
                                         ALU.mult))
                step.wait()
                for m in range(TT):
                    ins = V.tensor_tensor(xh[:, m], th[:, m], gain.unsqueeze(1).broadcast_to([P, heads, w]), ALU.mult)
                    if m == 0:
                        step(ins)
                step.wait()
                ins.then_inc(s_["head_ready"], 1)
                dve.wait_ge(s_["head_ready"], n + 1)

            acc = FIRST_ACC["c_q"]
            dve.wait_ge(s_["acc_free"], acc + 4)
            head_norm(c_q, CHD, c_gain[:, 0], 0, False)
            dve.wait_ge(s_["mem_in"], 32)
            head_norm(mem_kv[:, :, 0:W3], CHD, c_gain[:, 1], 1, False)

            def finish(n, qt, t, w, y):
                dve.wait_ge(s_["pv"], n + 1)
                f = fac[:, qt, 2 * t:2 * t + 2]
                step(V.reciprocal(f, sums[:, qt, 2 * t:2 * t + 2])); step.wait()
                V.tensor_tensor(y[:, qt, 2 * t * w:(2 * t + 2) * w].rearrange("p (j d) -> p j d", j=2),
                                psum[:, OB + n % 2, 0:2 * w].rearrange("p (j d) -> p j d", j=2),
                                f.unsqueeze(2).broadcast_to([P, 2, w]), ALU.mult).then_inc(s_["pv_read"], 1)

            def attention(list_, score, w, y):
                for i in range(len(list_) + 2):
                    if i < len(list_):
                        score(*list_[i])
                    if i >= 2:
                        finish(*list_[i - 2], w, y)

            def c_score(n, qt, t):
                dve.wait_ge(s_["scores"], n + 1)
                V.tensor_reduce(nmax[:, qt, 2 * t:2 * t + 2], psum[:, 2 * (n % 2):2 * (n % 2) + 2, 0:SEQ], AX, ALU.max,
                                negate=True).then_inc(s_["scored"], 1)

            attention(C_UNITS, c_score, 256, y_c)
            split_tokens("a_qk")
            split_tokens("a_v")
            dve.wait_ge(s_["acc_free"], FIRST_ACC["a_v"] + 4)
            head_norm(a_qk[:, :, 0:W3], AH, a_gain[:, 0], 2, False)
            head_norm(a_qk[:, :, W3:2 * W3], AH, a_gain[:, 1], 3, False)
            dve.wait_ge(s_["bias_in"], 16)

            def a_score(n, qt, t):
                nk = P * (qt + 1)
                dve.wait_ge(s_["scores"], n + 1)
                dve.wait_ge(s_["pt_sum"], n - 1)
                for j in range(2):
                    tab = a_bias[:, 2 * t + j, 0:P] if qt == 0 else a_bias[:, 2 * t + j, P:3 * P]
                    step(V.tensor_tensor_reduce(prob2[:, n % 2, j, 0:nk], psum[:, 2 * (n % 2) + j, 0:nk], tab,
                                                1.0, -3.0e38, ALU.add, ALU.max, nmax[:, qt, 2 * t + j:2 * t + j + 1]))
                step.wait()
                V.tensor_scalar(nmax[:, qt, 2 * t:2 * t + 2], nmax[:, qt, 2 * t:2 * t + 2], -1.0, None, ALU.mult)\
                    .then_inc(s_["scored"], 1)

            attention(A_UNITS, a_score, P, y_a)

            def over(row):
                return row.unsqueeze(1).broadcast_to([P, TT, W3])

            def heads(x):
                return x.rearrange("p m (h d) -> p m h d", h=BH)

            for i, (x, prev) in enumerate(((b_r, X1), (b_k, X2), (b_v, X1))):
                dve.wait_ge(s_[f"shift_in{i}"], 48)
                dve.wait_ge(s_["zero_row"], 3 if i == 2 else 2)
                dve.wait_ge(s_[f"row_in{i}"], 16)
                step(V.tensor_tensor(prev, prev, x, ALU.subtract)); step.wait()
                step(V.tensor_tensor(prev, prev, over(row_slot[i]), ALU.mult)); step.wait()
                V.tensor_tensor(x, x, prev, ALU.add).then_inc(s_["lerp"], 1)
            for i in range(4):
                y = (y_a, y_c)[i // 2][:, :, (i % 2) * CH:(i % 2 + 1) * CH]
                dve.wait_ge(s_["acc_free"], FIRST_ACC["z_in"] + i + 3)
                V.tensor_tensor(y, y, silu_z.rearrange("p (m n) -> p m n", m=TT), ALU.mult).then_inc(s_["z_used"], 1)
            low = [psum[:, 4 * a:4 * a + 4].rearrange("p (m b) n -> p m (b n)", m=TT) for a in range(2)]
            dve.wait_ge(s_["lora_out"], 2)
            dve.wait_ge(s_["row_in4"], 16)
            dve.wait_ge(s_["lerp"], 3)
            V.tensor_tensor(X1, low[0], over(row_slot[4]), ALU.add).then_inc(s_["zw_in"], 1)
            dve.wait_ge(s_["zw_in"], 1)
            V.tensor_copy(small0[:, 0:1], cst[:, 0:1]).then_inc(s_["w0_used"], 1)
            dve.wait_ge(s_["z_used"], 4)
            dve.wait_ge(s_["row_in4"], 32)
            V.tensor_tensor(b_b, low[1], over(row_slot[4]), ALU.add).then_inc(s_["za_in"], 1)
            dve.wait_ge(s_["za_in"], 1)
            V.tensor_copy(small0[:, 1:2], cst[:, 0:1]).then_inc(s_["a0_used"], 1)
            dve.wait_ge(s_["zw"], 1)
            half = 0.5 * 0.6065306597126334
            V.tensor_scalar(X1, X1, -half, -half, ALU.mult, ALU.add).then_inc(s_["logw"], 1)
            dve.wait_ge(s_["za"], 1)
            step(V.tensor_scalar(b_b, b_b, 0.5, 0.5, ALU.mult, ALU.add))
            dve.wait_ge(s_["row_in0"], 32)
            step(V.tensor_tensor(b_a, b_k, over(row_slot[0]), ALU.mult)); step.wait()
            step(V.tensor_tensor(X2, b_a, b_a, ALU.mult)); step.wait()
            step(V.tensor_reduce(hs_r, heads(X2), AX, ALU.add)); step.wait()
            V.tensor_scalar(hs_a, hs_r, 1e-24, None, ALU.max).then_inc(s_["hroot_in"], 1)
            dve.wait_ge(s_["row_in1"], 32)
            step(V.scalar_tensor_tensor(X2, b_b, -1.0, over(row_slot[1]), ALU.add, ALU.mult)); step.wait()
            step(V.scalar_tensor_tensor(b_k, X2, 1.0, b_k, ALU.add, ALU.mult)); step.wait()
            dve.wait_ge(s_["row_in2"], 32)
            step(V.tensor_tensor(X2, b_r, b_k, ALU.mult)); step.wait()
            step(V.tensor_tensor(X2, X2, over(row_slot[2]), ALU.mult)); step.wait()
            step(V.tensor_reduce(bonus, heads(X2), AX, ALU.add)); step.wait()
            dve.wait_ge(s_["hroot"], 5)
            step(V.reciprocal(hs_r, hs_a)); step.wait()
            for m in range(TT):
                step(V.tensor_tensor(heads(b_a)[:, m], heads(b_a)[:, m],
                                     hs_r[:, m].unsqueeze(2).broadcast_to([P, BH, DH]), ALU.mult))
            step.wait()
            V.tensor_tensor(b_b, b_b, b_a, ALU.mult).then_inc(s_["x2_free"], 1)
            dve.wait_ge(s_["e_pos"], 1)
            step(V.tensor_tensor(b_r, b_r, X2, ALU.mult)); step.wait()
            cum = psum[:, 0:4].rearrange("p (m b) n -> p m (b n)", m=TT)
            V.tensor_tensor(X2, cum, X1, ALU.subtract).then_inc(s_["e_ex_in"], 1)
            dve.wait_ge(s_["e_ex"], 1)
            V.scalar_tensor_tensor(b_a, b_a, -1.0, X2, ALU.mult, ALU.mult).then_inc(s_["x2_free"], 1)
            dve.wait_ge(s_["e_neg"], 1)
            step(V.tensor_tensor(b_b, b_b, X2, ALU.mult))
            step.wait()
            dve.wait_ge(s_["x2_free"], 2)
            V.tensor_tensor(b_k, b_k, X2, ALU.mult).then_inc(s_["pre_done"], 1)
            dve.wait_ge(s_["pre_done"], 1)
            dve.wait_ge(s_["masks_in"], 32)

            for t in range(8):
                cs = slice(t * P, (t + 1) * P)
                for u in range(4):
                    dve.wait_ge(s_["g_prod"], 2 * t + u // 2 + 1)
                    if u == 0 and t:
                        dve.wait_ge(s_["o1_sum"], t)
                    ins = V.tensor_tensor(Gs[:, u], psum[:, 2 + u % 2].rearrange("p (a n) -> p a n", a=4), gmask, ALU.mult)
                    ins.then_inc(s_["g_mask"], 1)
                if t:
                    dve.wait_ge(s_["ux_sum"], t)
                    dve.wait_ge(s_["y_sum"], t)
                for a in range(2):
                    ins = V.tensor_copy(DD[:, :, a], ident.unsqueeze(1).broadcast_to([P, 4, P]))
                    if a == 0:
                        step(ins)
                        step.wait()
                ins.then_inc(s_["dd"], 1)
                dve.wait_ge(s_["g_mask"], 4 * t + 4)
                for l in range(6):
                    for ahead in ((0, 1) if l == 0 else (l + 1,)):
                        if ahead:
                            dve.wait_ge(s_["p_sum"], 6 * t + ahead)
                        elif t:
                            dve.wait_ge(s_["wz_sum"], t)
                        if ahead < 6:
                            V.tensor_tensor(Lm, Gs[:, :, 0], lev[:, ahead].unsqueeze(1).broadcast_to([P, 4, P]),
                                            ALU.mult).then_inc(s_["l_mask"], 1)
                    dve.wait_ge(s_["dd_sum"], 6 * t + l + 1)
                    flat = DD.rearrange("p u a n -> p (u a n)")
                    dve.wait_ge(s_["dd"], 7 * t + l + 1)
                    V.tensor_tensor(flat, flat, psum[:, 5:7].rearrange("p b n -> p (b n)"), ALU.add)\
                        .then_inc(s_["dd"], 1)
                dve.wait_ge(s_["o1_sum"], t + 1)
                for m in range(TT):
                    src = psum[:, 7, 0:256].rearrange("p (j m d) -> p m j d", j=2, m=TT)[:, m]
                    step(V.tensor_copy(y_b[:, m, cs].rearrange("p (j d) -> p j d", j=2), src))
                dve.wait_ge(s_["qt_sum"], t + 1)
                V.tensor_tensor(AR[:, :, P:2 * P], AR[:, :, P:2 * P], psum[:, 5, 0:256].rearrange("p (m n) -> p m n", m=TT),
                                ALU.add).then_inc(s_["qt"], 1)
                dve.wait_ge(s_["wz"], t + 1)
                dve.wait_ge(s_["c_end"], 1)
                if t:
                    dve.wait_ge(s_["o2_sum"], t)
                V.tensor_scalar(ST[:, 0], WZ[:, 0, 1], c_end[:, t, 0:1], None, ALU.mult).then_inc(s_["state"], 1)
                for c in range(1, 3):
                    dve.wait_ge(s_["state"], 3 * t + c)
                    step(V.tensor_tensor(S_tmp, ST[:, c - 1], WZ[:, c, 1], ALU.add)); step.wait()
                    dve.wait_ge(s_["st_sum"], 2 * t + c)
                    step(V.tensor_tensor(S_tmp, S_tmp, psum[:, 7, 256 + c * DH:256 + (c + 1) * DH], ALU.add)); step.wait()
                    V.tensor_scalar(ST[:, c], S_tmp, c_end[:, t, c:c + 1], None, ALU.mult).then_inc(s_["state"], 1)
                dve.wait_ge(s_["o2_sum"], t + 1)
                step.wait()
                for h2 in range(2):
                    hc = slice(t * P + h2 * DH, t * P + (h2 + 1) * DH)
                    bank = 2 + h2
                    step(V.tensor_tensor(y_b[DH:P, 0, hc], y_b[DH:P, 0, hc], psum[DH:P, bank, 0:DH], ALU.add))
                    ins = V.tensor_tensor(y_b[:, 1, hc], y_b[:, 1, hc], psum[:, bank, DH:P], ALU.add)
                    if h2 == 0:
                        step(ins)
                        step.wait()
                step.wait()
                ins.then_inc(s_["o2"], 1)
            dve.wait_ge(s_["o2"], 8)

            yh = heads(y_b)

            def per_head(m, v):
                return v[:, m].unsqueeze(2).broadcast_to([P, BH, DH])

            step(V.tensor_reduce(hs_r, yh, AX, ALU.add)); step.wait()
            step(V.tensor_scalar(hs_r, hs_r, 1.0 / DH, None, ALU.mult)); step.wait()
            for m in range(TT):
                step(V.tensor_tensor(yh[:, m], yh[:, m], per_head(m, hs_r), ALU.subtract))
            step.wait()
            step(V.tensor_tensor(X1, y_b, y_b, ALU.mult)); step.wait()
            step(V.tensor_reduce(hs_r, heads(X1), AX, ALU.add)); step.wait()
            V.tensor_scalar(hs_a, hs_r, 1.0 / DH, 64e-5, ALU.mult, ALU.add).then_inc(s_["hroot_in"], 1)
            dve.wait_ge(s_["row_in3"], 32)
            dve.wait_ge(s_["row_in4"], 48)
            for m in range(TT):
                step(V.tensor_tensor(heads(b_v)[:, m], heads(b_v)[:, m], per_head(m, bonus), ALU.mult))
            step.wait()
            step(V.tensor_tensor(b_v, b_v, over(row_slot[4]), ALU.add)); step.wait()
            dve.wait_ge(s_["hroot"], 6)
            step(V.reciprocal(hs_r, hs_a)); step.wait()
            for m in range(TT):
                step(V.tensor_tensor(yh[:, m], yh[:, m], per_head(m, hs_r), ALU.mult))
            step.wait()
            step(V.tensor_tensor(y_b, y_b, over(row_slot[3]), ALU.mult)); step.wait()
            V.tensor_tensor(y_b, y_b, b_v, ALU.add).then_inc(s_["yb_ready"], 1)
            dve.wait_ge(s_["yb_ready"], 1)
            for i in range(4, 6):
                y = y_b[:, :, (i % 2) * CH:(i % 2 + 1) * CH]
                dve.wait_ge(s_["acc_free"], FIRST_ACC["z_in"] + i + 3)
                V.tensor_tensor(y, y, silu_zb[i % 2].rearrange("p (m n) -> p m n", m=TT), ALU.mult).then_inc(s_["z_used"], 1)
            base, acc = PLAN["ups"][0], FIRST_ACC["ups"]
            dve.wait_ge(s_["gates_in"], 12 * 16)
            for i in range(6):
                for n2 in range(2):
                    if n2 == 0:
                        dve.wait_ge(s_["up_half"], i + 1)
                    else:
                        wait_used(dve, base + i)
                    b, nb = i // 2, 2 * (i % 2) + n2
                    c = slice(nb * CH, (nb + 1) * CH)
                    src = psum[:, 2 * n2:2 * n2 + 2]
                    g = gates_[:, :, b * D + nb * CH:b * D + (nb + 1) * CH]
                    if i == 0 and n2 == 0:
                        dve.wait_ge(s_["acc_free"], acc + 2)
                    V.tensor_tensor(g, src, g, ALU.mult).then_inc(s_["acc_free"], 1)
                    dve.wait_ge(s_["acc_free"], acc + 2 * i + n2 + 3)
                    if b == 0:
                        V.tensor_copy(xn[:, :, c], g).then_inc(s_["merged"], 1)
                    else:
                        if nb == 0:
                            dve.wait_ge(s_["merged"], 4 * b)
                        V.tensor_tensor(xn[:, :, c], xn[:, :, c], g, ALU.add).then_inc(s_["merged"], 1)
            acc = FIRST_ACC["w_o"]
            dve.wait_ge(s_["x1_back"], 16)

            def w_o_residual(nb):
                dve.wait_ge(s_["unit_used"], unit0("w_o") + 4 * nb + 6)
                c = slice(nb * CH, (nb + 1) * CH)
                s = nb % 2
                V.tensor_tensor(h[:, :, c], h[:, :, c], psum[:, 2 * s:2 * s + 2], ALU.add).then_inc(s_["x2_done"], 1)
                if nb < 2:
                    dve.wait_ge(s_["x2_done"], nb + 1)
                    V.tensor_copy(small0[:, 0:1], cst[:, 0:1]).then_inc(s_["acc_free"], 1)
                    dve.wait_ge(s_["acc_free"], acc + nb + 3)
            split_tokens("w_o", w_o_residual)

        FIRST_ACC = {}
        n = 0
        for name, count in (("mem", 4), ("w_in", 12), ("w_out", 4), ("ffn", 22), ("down", 4), ("c_q", 2),
                            ("a_qk", 4), ("a_v", 2), ("b_in", 6), ("z_in", 6), ("gates", 12), ("ups", 12),
                            ("w_o", 4)):
            FIRST_ACC[name] = n
            n += count

        @block.sync
        def _(sp):
            sp.dma_start(h[:], A["x"].rearrange("(m p) n -> p m n", p=P)).then_inc(s_["x_in"], 16)
            sp.dma_start(vec[:], A["vec"][:, 0:vec.shape[1]]).then_inc(s_["x_in"], 16)
            sp.dma_start(cst[:], A["const"]).then_inc(s_["const_in"], 16)
            for slot in range(2):
                sp.dma_start(Wb[:, slot], A["loads"][slot]).then_inc(LOADED[slot], 16)
            with sp.Fori(1, N_LOADS // 2) as i:
                for slot in range(2):
                    sp.wait_ge(USED[slot], i)
                    sp.dma_start(Wb[:, slot], A["loads"][i * 2 + slot]).then_inc(LOADED[slot], 16)
            sp.wait_ge(s_["out_stored"], 16)

        @block.gpsimd
        def _(pool):
            def early_half(n, half):
                k = slice(half * KT // 2, (half + 1) * KT // 2)
                return pool.dma_start(early[:, k], A["ada_early"][n, half].rearrange("p (k n) -> p k n", n=CH))

            pool.dma_start(mem_x, A["mem"].rearrange("(m p) n -> p m n", p=P)).then_inc(s_["mem_in"], 16)
            for half in range(2):
                early_half(0, half).then_inc(s_[f"early_in{half}"], 16)
            def early_loads(first, last):
                with pool.Fori(first, last) as n:
                    for half in range(2):
                        pool.wait_ge(s_["early_used"], n * 2 + (half - 1))
                        early_half(n, half).then_inc(s_[f"early_in{half}"], 16)

            early_loads(1, 9)
            pool.wait_ge(s_["acc_free"], FIRST_ACC["mem"] + 4 + 2)
            pool.dma_start(mem_dram, arena[:, 8192:8192 + TT * D]).then_inc(s_["mem_saved"], 16)
            pool.wait_ge(s_["tr_ready"], 16)
            for half in range(2):
                nc.gpsimd.dma_start(cmp_w1[half * DH:half * DH + DH], A["cmp_w1"]).then_inc(s_["w1_in"], 16)
            early_loads(9, N_EARLY)
            pool.wait_ge(s_["early_used"], 2 * N_EARLY)
            nc.gpsimd.dma_start(arena[:, 12288:12288 + A["tabs"].shape[1]], A["tabs"]).then_inc(s_["tabs_in"], 16)
            pool_block2(pool)

        @block.scalar
        def _(act):
            step = Steps(act, s_["act_step"])
            rounds = [0]

            def copy(out_, in_, scale=1.0):
                return nc.scalar.activation(out_, in_, ACT.Copy, scale=scale)

            def square_sums(src, n):
                for m in range(TT):
                    nc.scalar.activation(xn[:, m], src[:, m], ACT.Square, accum_out=stat[:, m:m + 1])\
                      .then_inc(s_["stat_ready"], 1)
                act.wait_ge(s_["root_ready"], 2 * n + 1)
                nc.scalar.activation(rstd[:], stat[:], ACT.Sqrt).then_inc(s_["root_ready"], 1)

            def read_transposes(n_tiles, scale=None, bias=None, dst=None, factor=1.0):
                dst = xT if dst is None else dst
                for r in range(n_tiles // 2):
                    bank = TRB + rounds[0] % 2
                    rounds[0] += 1
                    act.wait_ge(s_["tr_ready"], rounds[0])
                    src = psum[:, bank].rearrange("p (k s) -> p k s", k=2)
                    for j in range(2):
                        k = 2 * r + j
                        if scale is None:
                            ins = copy(dst[:, k], src[:, j], scale=factor)
                        elif bias is None:
                            ins = copy(dst[:, k], src[:, j], scale=scale[:, k:k + 1])
                        else:
                            ins = nc.scalar.activation(dst[:, k], src[:, j], ACT.Identity,
                                                       bias=bias[:, k:k + 1], scale=scale[:, k:k + 1])
                    ins.then_inc(s_["tr_free"], 1)

            act.wait_ge(s_["const_in"], 16)
            for i in range(2):
                copy(small0[:, i:i + 1], cst[:, 0:1]).then_inc(s_["acc_free"], 1)

            act.wait_ge(s_["x_in"], 32)
            nc.scalar.activation(c_act[:], v_("c"), ACT.Tanh, scale=0.5).then_inc(s_["c_exp"], 1)
            act.wait_ge(s_["mem_in"], 16)
            square_sums(mem_x, 0)
            read_transposes(KT, v_("mem_norm"))
            square_sums(h, 1)
            for i in range(4):
                wait_used(act, PLAN["mem"][0] + i)
                copy(mem_out[:, :, i * CH:(i + 1) * CH], psum[:, 2 * (i % 2):2 * (i % 2) + 2])\
                    .then_inc(s_["acc_free"], 1)
            act.wait_ge(s_["mod_ready"], 9)
            read_transposes(KT, scale_col, mod[:, 0:16])

            base, acc = PLAN["w_in"][0], FIRST_ACC["w_in"]
            for first, scale in ((0, DH ** -0.5), (4, 1.0)):
                with act.Fori(0, 2) as i:
                    for s in range(2):
                        act.wait_ge(USED[s], i + (base + first) // 2 + 1)
                        copy(qk[:, bass.ds(i * 8 + (first + s) * 4, 4), :],
                             psum[:, 2 * s:2 * s + 2].rearrange("p b (c s) -> p (b c) s", s=SEQ), scale=scale)\
                            .then_inc(s_["acc_free"], 1)
            act.wait_ge(s_["mem_saved"], 16)
            with act.Fori(0, 2) as i:
                for s in range(2):
                    act.wait_ge(USED[s], i + (base + 8) // 2 + 1)
                    copy(tm[:, :, bass.ds(i * 1024 + s * CH, CH)], psum[:, 2 * s:2 * s + 2])\
                        .then_inc(s_["acc_free"], 1)
            act.wait_ge(s_["acc_free"], acc + 14)
            nc.scalar.activation(gate[:], tm[:, :, V_GATE:V_GATE + 24], ACT.Tanh, scale=0.5)\
              .then_inc(s_["gate_exp"], 1)
            act.wait_ge(s_["f_abs"], 1)
            nc.scalar.activation(fe[:], fe[:], ACT.Exp).then_inc(s_["f_ln"], 1)
            act.wait_ge(s_["f_ln"], 1)
            nc.scalar.activation(fe[:], fe[:], ACT.Ln, bias=1.0).then_inc(s_["f_ln"], 1)
            act.wait_ge(s_["crow_sum"], 1)
            copy(crow[:, 0], psum[0:1, 0:4].rearrange("p b (c s) -> p (b c) s", s=SEQ)[:, 0:FOX])\
                .then_inc(s_["crow_ready"], 1)
            act.wait_ge(s_["cmp_hidden"], 1)
            for g in range(2):
                copy(cz[0:DH, 0, g], psum[0:DH, OB + g, 0:32].rearrange("p (v c) -> p v c", v=2)[:, :, 0:N_CMP])\
                    .then_inc(s_["cmp_exp_in"], 1)
            act.wait_ge(s_["cmp_exp_in"], 3)
            nc.scalar.activation(cz[0:DH, 3], cz[0:DH, 2], ACT.Tanh).then_inc(s_["cmp_exp"], 1)
            act.wait_ge(s_["cmp_out"], 1)
            copy(kcT[:], psum[:, OB, 0:N_CMP]).then_inc(s_["kc_ready"], 1)
            copy(vc[0:N_CMP], psum[0:N_CMP, OB + 1, 0:2 * DH].rearrange("p (g d) -> p g d", g=2))\
                .then_inc(s_["kc_ready"], 1)

            act.wait_ge(s_["lam_in"], 1)
            nc.scalar.activation(lam[:, 0:2], lam[:, 0:2], ACT.Exp).then_inc(s_["lam_exp"], 1)

            def exps(n):
                qt, p = divmod(n, NPAIR)
                nk = keys(n)
                act.wait_ge(s_["scored"], n + 1)
                for j in range(2):
                    nc.scalar.activation(prob[:, n % 2, j, 0:nk], prob[:, n % 2, j, 0:nk], ACT.Exp,
                                         bias=nmax[:, qt, 2 * p + j:2 * p + j + 1],
                                         accum_out=sums[:, qt, 2 * p + j:2 * p + j + 1]).then_inc(s_["exps"], 1)

            def read_probT(n):
                nk = keys(n)
                act.wait_ge(s_["pt_sum"], n + 1)
                if n >= 2:
                    act.wait_ge(s_["pv"], n - 1)
                rows_ = P if nk > N_CMP else N_CMP
                w = max(nk, P)
                copy(probT[0:rows_, n % 2, :, 0:w],
                     psum[0:rows_, TRB].rearrange("p (j k) -> p j k", j=2)[:, :, 0:w]).then_inc(s_["pt_ready"], 1)

            for n in range(TT * NPAIR + 1):
                if n < TT * NPAIR:
                    exps(n)
                if n >= 1:
                    read_probT(n - 1)
                if n in DIL_AT:
                    qt = DIL_AT.index(n)
                    act.wait_ge(s_["dil_in"], qt + 1)
                    nc.scalar.activation(dil_e[:], dil_e[:], ACT.Exp).then_inc(s_["dil_exp"], 1)
            act.wait_ge(s_["diff_in"], 1)
            nc.scalar.activation(diff_ss[:], diff_ss[:], ACT.Sqrt).then_inc(s_["diff_in"], 1)
            act.wait_ge(s_["o_ready"], 1)
            read_transposes(KT)

            def read_g_row(n):
                act.wait_ge(s_["g_sum"], n + 1)
                copy(g_row2 if n else g_row, psum[:, 4:8].rearrange("p b n -> p (b n)")).then_inc(s_["g_row_ready"], 1)

            read_g_row(0)
            act.wait_ge(s_["h_ready"], 4)
            square_sums(h, 2)
            act.wait_ge(s_["mod_ready"], 26)
            read_transposes(KT, scale_col, mod[:, 48:64])
            base, acc = PLAN["ffn"][0], FIRST_ACC["ffn"]
            for i in range(2):
                copy(small0[:, i:i + 1], cst[:, 0:1]).then_inc(s_["unit_used"], 1)
            with act.Fori(0, 11) as i:
                for s in range(2):
                    act.wait_ge(LOADED[s], i * 16 + 16 * (base // 2 + 1))
                    for q in range(4):
                        if s == 1 and q == 2:
                            act.wait_ge(s_["unit_used"], i * 8 + 6)
                            act.wait_ge(s_["acc_free"], i * 2 + acc + 2)
                            nc.scalar.activation(silu_g, psum[:, 0:2].rearrange("p b n -> p (b n)"), ACT.Silu)\
                              .then_inc(s_["acc_free"], 1)
                        act.wait_ge(s_["unit_used"], i * 8 + (4 * s + q + 1))
                        copy(w_hi[:, q % 2], W(s)[:, :, q * P:(q + 1) * P]).then_inc(s_["high"], 1)
            read_g_row(1)
            base = PLAN["down"][0]
            act.wait_ge(s_["unit_used"], N_FFN + 2)
            with act.Fori(0, 2) as i:
                for u, (nb, part, k, n, _) in enumerate(DOWN_UNITS):
                    load = 3 * nb + part
                    if k == 0:
                        act.wait_ge(LOADED[load % 2], i * 48 + 16 * ((base + load) // 2 + 1))
                    if u == 0:
                        act.wait_ge(s_["acc_free"], FIRST_ACC["ffn"] + 24)
                    act.wait_ge(s_["unit_used"], i * N_DOWN + (N_FFN + u + 1))
                    kk = part * KT + k
                    copy(hd_hi[:, u % 2, 0:n], hT[:, kk:kk + n])
                    copy(wd_hi[:, u % 2, 0:n], W(load % 2)[:, k:k + n]).then_inc(s_["high"], 1)
            act_block2(act, step, copy, square_sums, read_transposes)

        @block.tensor
        def _(pe):
            rounds = [0]

            def transposes(src, n_tiles):
                for r in range(n_tiles // 2):
                    bank = TRB + rounds[0] % 2
                    if rounds[0] >= 2:
                        pe.wait_ge(s_["tr_free"], rounds[0] - 1)
                    rounds[0] += 1
                    for j in range(2):
                        for m in range(TT):
                            k = 2 * r + j
                            ins = nc.tensor.transpose(psum[:, bank, (2 * j + m) * P:(2 * j + m + 1) * P],
                                                      src[:, m, k * P:(k + 1) * P], ident)
                    ins.then_inc(s_["tr_ready"], 1)

            def ada_early(i, s, first):
                pe.wait_ge(s_["early_used"], i * 4 + 2 * (8 + first + s + 1))
                pe.wait_ge(s_["mod_ready"], i * 2 + 9 + first + s)
                for j in range(4):
                    ins = nc.tensor.matmul(psum[:, TRB + 1, j:j + 1], ada_buf(s)[:, j * P:(j + 1) * P], ones[:, 0:1],
                                           start=True, stop=True)
                ins.then_inc(s_["ada_sum"], 1)

            def tokens_product(name, first=0, count=None, k_tiles=KT, act_T=None, beside=None):
                base, n = PLAN[name]
                acc = FIRST_ACC[name] + first
                count = n - first if count is None else count
                base += first
                act_T = xT if act_T is None else act_T
                with pe.Fori(0, count // 2) as i:
                    for s in range(2):
                        pe.wait_ge(LOADED[s], i * 16 + 16 * (base // 2 + 1))
                        pe.wait_ge(s_["acc_free"], i * 2 + (acc + s + 1))
                        for m in range(TT):
                            for k in range(k_tiles):
                                ins = nc.tensor.matmul(psum[:, 2 * s + m], act_T[:, k, m * P:(m + 1) * P],
                                                       W(s)[:, k], start=(k == 0), stop=(k == k_tiles - 1))
                        ins.then_inc(USED[s], 1)
                        if beside:
                            beside(i, s, first)

            def features_product(name, first=0, count=None, beside=None):
                base, n = PLAN[name]
                acc = FIRST_ACC[name] + first
                count = n - first if count is None else count
                base += first
                with pe.Fori(0, count // 2) as i:
                    for s in range(2):
                        pe.wait_ge(LOADED[s], i * 16 + 16 * (base // 2 + 1))
                        pe.wait_ge(s_["acc_free"], i * 2 + (acc + s + 1))
                        for c in range(4):
                            for k in range(KT):
                                ins = nc.tensor.matmul(psum[:, 2 * s + c // 2, (c % 2) * SEQ:(c % 2 + 1) * SEQ],
                                                       W(s)[:, k, c * P:(c + 1) * P], xT[:, k],
                                                       start=(k == 0), stop=(k == KT - 1))
                        ins.then_inc(USED[s], 1)
                        if beside:
                            beside(i, s, first)

            def ada_sum(i, load=None):
                if i < N_EARLY:
                    pe.wait_ge(s_["early_used"], 2 * i + 2)
                else:
                    wait_used(pe, load)
                if i:
                    pe.wait_ge(s_["mod_ready"], i + (i > 8))
                for j in range(4):
                    ins = nc.tensor.matmul(psum[:, OB if i < 8 else TRB + 1, j:j + 1], ada_buf(i)[:, j * P:(j + 1) * P], ones[:, 0:1],
                                           start=True, stop=True)
                ins.then_inc(s_["ada_sum"], 1)

            pe.wait_ge(s_["const_in"], 16)
            ada_sum(0)
            pe.wait_ge(s_["norm_ready"], 2)
            transposes(xn, KT)
            pe.wait_ge(s_["tr_free"], rounds[0])
            for i in range(4):
                wait_load(pe, PLAN["mem"][0] + i)
                pe.wait_ge(s_["acc_free"], FIRST_ACC["mem"] + i + 1)
                for m in range(TT):
                    for k in range(KT):
                        ins = nc.tensor.matmul(psum[:, 2 * (i % 2) + m], xT[:, k, m * P:(m + 1) * P], W(i % 2)[:, k],
                                               start=(k == 0), stop=(k == KT - 1))
                    if m == 1:
                        ins.then_inc(USED[i % 2], 1)
                    if 2 * i + m < 7:
                        ada_sum(2 * i + m + 1)
            pe.wait_ge(s_["mod_ready"], 8)
            pe.wait_ge(s_["norm_ready"], 4)
            transposes(xn, KT)
            pe.wait_ge(s_["tr_free"], rounds[0])
            features_product("w_in", 0, 8, beside=ada_early)
            tokens_product("w_in", 8, 4, beside=ada_early)

            pe.wait_ge(s_["logf_ready"], 1)
            pe.wait_ge(s_["acc_free"], FIRST_ACC["w_in"] + 14)
            for f in range(FOX):
                row = psum[0:1, f // 2, (f % 2) * SEQ:(f % 2 + 1) * SEQ]
                nc.tensor.matmul(row[:, 0:P], logf[:, 0, f:f + 1], tri, start=True, stop=True)
                nc.tensor.matmul(row[:, P:SEQ], logf[:, 0, f:f + 1], ones, start=True, stop=False)
                ins = nc.tensor.matmul(row[:, P:SEQ], logf[:, 1, f:f + 1], tri, start=False, stop=True)
            ins.then_inc(s_["crow_sum"], 1)

            pe.wait_ge(s_["w1_in"], 32)
            pe.wait_ge(s_["blk_ready"], 4)
            for g in range(2):
                for v in range(2):
                    for l in range(CMP_LEN):
                        r = slice(g * DH, g * DH + DH)
                        ins = nc.tensor.matmul(psum[0:DH, OB + g, v * 16:v * 16 + N_CMP], cmp_w1[r, v, l],
                                               blk[r, v, l], start=(l == 0), stop=(l == CMP_LEN - 1))
            ins.then_inc(s_["cmp_hidden"], 1)
            pe.wait_ge(s_["gelu_ready"], 1)
            w2 = v_("cmp_w2").rearrange("p (v e) -> p v e", v=2)
            for g in range(2):
                nc.tensor.matmul(psum[g * DH:(g + 1) * DH, OB, 0:N_CMP], w2[0:DH, 0], cz[0:DH, 5, g, 0],
                                 start=True, stop=True)
            for g in range(2):
                ins = nc.tensor.matmul(psum[0:N_CMP, OB + 1, g * DH:(g + 1) * DH], cz[0:DH, 5, g, 1],
                                       w2[0:DH, 1], start=True, stop=True)
            ins.then_inc(s_["cmp_out"], 1)
            pe.wait_ge(s_["kc_ready"], 2)
            pe.wait_ge(s_["crow_ready"], 1)
            pe.wait_ge(s_["ncrow_ready"], 1)

            def scores(n):
                qt, p = divmod(n, NPAIR)
                kind, t, q, k = PAIRS[p]
                nk = keys(n)
                if n >= 2:
                    pe.wait_ge(s_["scored"], n - 1)
                qs = slice(qt * P, qt * P + P)
                for j in range(2):
                    bank = psum[:, 2 * (n % 2) + j, 0:nk]
                    r = slice(j * DH, j * DH + DH)
                    fox = kind == "fd" and 2 * t + j < FOX
                    key = kcT[r, :] if kind == "cmp" else qk[r, k, 0:nk]
                    ins = nc.tensor.matmul(bank, qk[r, q, qs], key, start=True, stop=not fox)
                    if fox:
                        f = 2 * t + j
                        nc.tensor.matmul(bank, crow[:, 0, f, qs], ones[0:1, 0:1].broadcast_to([1, nk]),
                                         start=False, stop=False)
                        ins = nc.tensor.matmul(bank, ones[0:1, :], crow[:, 1, f, 0:nk], start=False, stop=True)
                ins.then_inc(s_["scores"], 1)

            def transpose_probs(n):
                nk = keys(n)
                pe.wait_ge(s_["exps"], 2 * n + 2)
                if n >= 1:
                    pe.wait_ge(s_["pt_ready"], n)
                for j in range(2):
                    for a in range(0, nk, P):
                        w = min(P, nk - a)
                        ins = nc.tensor.transpose(psum[0:w, TRB, j * SEQ + a:j * SEQ + a + P],
                                                  prob[:, n % 2, j, a:a + w], ident)
                ins.then_inc(s_["pt_sum"], 1)

            def values(n):
                qt, p = divmod(n, NPAIR)
                kind, t, _, _ = PAIRS[p]
                nk = keys(n)
                g = GROUP_OF[p]
                G = qt * len(GROUPS) + g
                pe.wait_ge(s_["pt_ready"], n + 1)
                if p == GROUPS[g][0] and G >= 2:
                    pe.wait_ge(s_["pv_read"], G - 1)
                for j in range(2):
                    i = 2 * (p - GROUPS[g][0]) + j
                    if kind == "cmp":
                        ins = nc.tensor.matmul(psum[:, OB + G % 2, i * DH:(i + 1) * DH], probT[0:N_CMP, n % 2, j, 0:P],
                                               vc[0:N_CMP, j], start=True, stop=True)
                        continue
                    at, w = value_of(kind, t, j)
                    for m in range(nk // P):
                        ins = nc.tensor.matmul(psum[:, OB + G % 2, i * w:(i + 1) * w],
                                               probT[:, n % 2, j, m * P:(m + 1) * P], tm[:, m, at:at + w],
                                               start=(m == 0), stop=(m == nk // P - 1))
                ins.then_inc(s_["pv"], 1)

            for n in range(TT * NPAIR + 2):
                if n < TT * NPAIR:
                    scores(n)
                if 1 <= n <= TT * NPAIR:
                    transpose_probs(n - 1)
                if n >= 2:
                    values(n - 2)
                if n and n % 10 == 0:
                    ada_sum(N_EARLY + n // 10 - 1, PLAN["ada_b"][0] + n // 10 - 1)
            pe.wait_ge(s_["mod_ready"], 25)
            pe.wait_ge(s_["o_ready"], 1)
            transposes(o, KT)
            pe.wait_ge(s_["tr_free"], rounds[0])

            def g_rows(n):
                pe.wait_ge(s_["g_diag"], n + 1)
                for b in range(4):
                    of = diag2 if n else diag
                    ins = nc.tensor.matmul(psum[:, 4 + b], ones, of[:, 4 * b:4 * b + 4].rearrange("p k n -> p (k n)"),
                                           start=True, stop=True)
                ins.then_inc(s_["g_sum"], 1)

            g_rows(0)
            tokens_product("w_out")
            pe.wait_ge(s_["norm_ready"], 6)
            pe.wait_ge(s_["g_row_ready"], 1)
            transposes(xn, KT)
            pe.wait_ge(s_["tr_free"], rounds[0])
            base, acc = PLAN["ffn"][0], FIRST_ACC["ffn"]
            pe.wait_ge(s_["x_split"], 2)
            with pe.Fori(0, 11) as i:
                for s in range(2):
                    pe.wait_ge(s_["acc_free"], i * 2 + (acc + s + 1))
                    for q in range(4):
                        if q < 3:
                            pe.wait_ge(s_["low"], i * 6 + (3 * s + q + 1))
                        else:
                            pe.wait_ge(USED[s], i + (base // 2 + 1))
                        for k in range(KT):
                            for w, x in ((w_hi, x_hi), (w_hi, x_lo), (w_lo, x_hi)):
                                ins = nc.tensor.matmul(psum[:, 2 * s + q // 2, (q % 2) * SEQ:(q % 2 + 1) * SEQ],
                                                       w[:, q % 2, k], x[:, k],
                                                       start=(k == 0 and w is w_hi and x is x_hi),
                                                       stop=(k == KT - 1 and w is w_lo))
                        ins.then_inc(s_["unit_used"], 1)
            g_rows(1)
            base = PLAN["down"][0]
            with pe.Fori(0, 2) as i:
                low = 0
                for u, (nb, part, k0, n, last) in enumerate(DOWN_UNITS):
                    load = 3 * nb + part
                    if part == 0 and k0 == 0:
                        pe.wait_ge(s_["acc_free"], i * 2 + (FIRST_ACC["down"] + nb + 1))
                    low += not last
                    pe.wait_ge(s_["high"], i * N_DOWN + (N_FFN + u + 1))
                    for w, x in ((wd_hi, hd_hi), (wd_hi, hd_lo), (wd_lo, hd_hi)):
                        if x is hd_lo and last:
                            pe.wait_ge(USED[load % 2], i * 3 + ((base + load) // 2 + 1))
                        elif x is hd_lo:
                            pe.wait_ge(s_["low"], i * (N_DOWN - 6) + (66 + low))
                        for m in range(TT):
                            for k in range(n):
                                kk = part * KT + k0 + k
                                ins = nc.tensor.matmul(psum[:, 2 * nb + m], x[:, u % 2, k, m * P:(m + 1) * P],
                                                       w[:, u % 2, k],
                                                       start=(kk == 0 and w is wd_hi and x is hd_hi),
                                                       stop=(kk == KF - 1 and w is wd_lo), skip_group_check=True)
                    ins.then_inc(s_["unit_used"], 1)
            pe_block2(pe, transposes, tokens_product, rounds)

        @block.vector
        def _(dve):
            step = Steps(dve, s_["dve_step"])
            V = nc.vector

            def rms(n, width=D):
                dve.wait_ge(s_["stat_ready"], 2 * n + 2)
                V.tensor_scalar(stat[:], stat[:], 1.0 / width, EPS, ALU.mult, ALU.add)\
                    .then_inc(s_["root_ready"], 1)
                dve.wait_ge(s_["root_ready"], 2 * n + 2)
                step(V.reciprocal(rstd[:], rstd[:]))
                step.wait()

            def scale_tokens(src):
                for m in range(TT):
                    V.tensor_scalar(xn[:, m], src[:, m], rstd[:, m:m + 1], None, ALU.mult)\
                        .then_inc(s_["norm_ready"], 1)

            ada_n, ada_steps = [0], [0]

            def ada_part(load, k0, k1):
                is_early = load is None
                n_early = ada_n[0]
                tile = early if is_early else W(load % 2)
                for k in range(k0, k1):
                    if is_early and k % (KT // 2) == 0:
                        dve.wait_ge(s_[f"early_in{k // (KT // 2)}"], 16 * (n_early + 1))
                    if k == 0:
                        if not is_early:
                            wait_load(dve, load)
                        if ada_n[0] >= 2:
                            dve.wait_ge(s_["ada_sum"], ada_n[0] - 1)
                        acc_ = ada_buf(ada_n[0])
                        ins = V.tensor_scalar(acc_, tile[:, 0], c_act[:, 0:1], None, ALU.mult)
                    else:
                        if is_early and k == KT // 2:
                            dve.wait_ge(s_["early_used"], 2 * n_early + 1)
                        else:
                            dve.wait_ge(s_["ada_step"], ada_steps[0])
                        acc_ = ada_buf(ada_n[0])
                        ins = V.scalar_tensor_tensor(acc_, tile[:, k], c_act[:, k:k + 1], acc_,
                                                     ALU.mult, ALU.add)
                    if is_early and (k + 1) % (KT // 2) == 0:
                        ins.then_inc(s_["early_used"], 1)
                    elif k < KT - 1:
                        ins.then_inc(s_["ada_step"], 1)
                        ada_steps[0] += 1
                    else:
                        ins.then_inc(USED[load % 2], 1)
                ada_n[0] += k1 == KT

            def ada_read(i):
                dve.wait_ge(s_["ada_sum"], i + 1)
                a = VEC["ada_b"][0]
                V.tensor_tensor(mod[:, 4 * i:4 * i + 4], psum[:, OB if i < 8 else TRB + 1, 0:4], vec[:, a + 4 * i:a + 4 * i + 4],
                                ALU.add).then_inc(s_["mod_ready"], 1)

            dve.wait_ge(s_["c_exp"], 1)
            step(V.tensor_scalar(c_act[:], c_act[:], 0.5, 0.5, ALU.mult, ALU.add)); step.wait()
            step(V.tensor_tensor(c_act[:], c_act[:], v_("c"), ALU.mult)); step.wait()
            rms(0)
            scale_tokens(mem_x)
            for i in range(8):
                ada_part(None, 0, KT)
                if i:
                    ada_read(i - 1)
                if i == 3:
                    rms(1)
                    scale_tokens(h)
            ada_read(7)
            dve.wait_ge(s_["mod_ready"], 8)
            V.scalar_tensor_tensor(scale_col[:], mod[:, 16:32], 1.0, v_("norm_mix"), ALU.add, ALU.mult)\
                .then_inc(s_["mod_ready"], 1)

            for i in range(8, N_EARLY):
                ada_part(None, 0, KT)
                if i > 8:
                    ada_read(i - 1)
            ada_read(N_EARLY - 1)

            acc = FIRST_ACC["w_in"]
            dve.wait_ge(s_["acc_free"], acc + 14)
            a = VEC["fox_b"][0]
            step(V.tensor_tensor(fz[:], tm[:, :, V_FOXF:V_FOXF + FOX],
                                 vec[:, a:a + FOX].unsqueeze(1).broadcast_to([P, TT, FOX]), ALU.add)); step.wait()
            V.scalar_tensor_tensor(fe[:], fz[:], -1.0, fz[:], ALU.mult, ALU.min).then_inc(s_["f_abs"], 1)
            dve.wait_ge(s_["f_ln"], 2)
            step(V.tensor_scalar(fz[:], fz[:], 0.0, None, ALU.min)); step.wait()
            V.tensor_tensor(logf[:], fz[:], fe[:], ALU.subtract).then_inc(s_["logf_ready"], 1)
            dve.wait_ge(s_["gate_exp"], 1)
            step(V.tensor_scalar(gate[:], gate[:], 0.5, 0.5, ALU.mult, ALU.add))
            dve.wait_ge(s_["crow_ready"], 1)
            V.tensor_scalar(crow[:, 1], crow[:, 0], -1.0, None, ALU.mult).then_inc(s_["ncrow_ready"], 1)
            pos = v_("cmp_pos").rearrange("p (v l) -> p v l", v=2)
            for v, tile in ((0, CMPK), (1, CMPV)):
                chunks = qk[:, tile].rearrange("p (c r) -> p r c", r=CMP_STRIDE)
                for half in range(2):
                    ls = slice(half * CMP_STRIDE, (half + 1) * CMP_STRIDE)
                    V.tensor_tensor(blk[:, v, ls], chunks[:, :, half:half + N_CMP],
                                    pos[:, v, ls].unsqueeze(2).broadcast_to([P, CMP_STRIDE, N_CMP]), ALU.add)\
                        .then_inc(s_["blk_ready"], 1)
            dve.wait_ge(s_["cmp_exp_in"], 2)
            z = [cz[0:DH, i] for i in range(6)]
            step(V.tensor_tensor(z[1], z[0], z[0], ALU.mult)); step.wait()
            step(V.tensor_scalar(z[1], z[1], 0.044715, 1.0, ALU.mult, ALU.add)); step.wait()
            V.scalar_tensor_tensor(z[2], z[1], 0.7978845608028654, z[0], ALU.mult, ALU.mult)\
                .then_inc(s_["cmp_exp_in"], 1)
            dve.wait_ge(s_["cmp_exp"], 1)
            step(V.tensor_scalar(z[4], z[3], 0.5, 0.5, ALU.mult, ALU.add)); step.wait()
            V.tensor_tensor(z[5], z[4], z[0], ALU.mult).then_inc(s_["gelu_ready"], 1)
            lv = v_("lam").rearrange("p (i d) -> p i d", i=4)
            for i in range(2):
                step(V.tensor_tensor_reduce(lv[:, 2 * i], lv[:, 2 * i], lv[:, 2 * i + 1], 1.0, 0.0, ALU.mult, ALU.add,
                                            lam[:, i:i + 1]))
            step.wait()
            V.tensor_copy(lam[:, 3:4], lam[:, 0:1]).then_inc(s_["lam_in"], 1)
            dve.wait_ge(s_["lam_exp"], 1)
            step(V.tensor_tensor(lam[:, 2:3], lam[:, 1:2], lam[:, 0:1], ALU.subtract)); step.wait()
            step(V.tensor_scalar(lam[:, 2:3], lam[:, 2:3], -LAM_INIT, None, ALU.add))
            dve.wait_ge(s_["tabs_in"], 16)

            def score(n):
                qt, p = divmod(n, NPAIR)
                kind, t, _, _ = PAIRS[p]
                nk = keys(n)
                dve.wait_ge(s_["scores"], n + 1)
                if n >= 2:
                    dve.wait_ge(s_["pt_sum"], n - 1)
                elif n == 0:
                    dve.wait_ge(s_["cmp_hidden"], 1)
                for j in range(2):
                    if kind == "cmp":
                        tab = cmp_tabs[:, t + 4 * j, qt]
                    else:
                        i = table_of(kind, t, j)
                        tab = tabs[:, i, 0:P] if qt == 0 else tabs[:, i, P:P + nk]
                    step(V.tensor_tensor_reduce(prob[:, n % 2, j, 0:nk], psum[:, 2 * (n % 2) + j, 0:nk], tab,
                                                1.0, -3.0e38, ALU.add, ALU.max,
                                                nmax[:, qt, 2 * p + j:2 * p + j + 1]))
                step.wait()
                V.tensor_scalar(nmax[:, qt, 2 * p:2 * p + 2], nmax[:, qt, 2 * p:2 * p + 2], -1.0, None, ALU.mult)\
                    .then_inc(s_["scored"], 1)

            def bank_of(G):
                return psum[:, OB + G % 2]

            def items(x, w):
                return x.rearrange("p (i d) -> p i d", d=w)

            def finish(G):
                qt, g = divmod(G, len(GROUPS))
                last = qt * NPAIR + GROUPS[g][-1]
                dve.wait_ge(s_["pv"], last + 1)
                i0, i1 = 2 * GROUPS[g][0], 2 * GROUPS[g][-1] + 2
                f = fac[:, qt, i0:i1]
                if g <= 1:
                    if g == 1:
                        m9 = nmax[:, qt, FOX:16].rearrange("p (g j) -> p j g", g=3)
                        step(V.tensor_reduce(dil_m[:, 0:3], m9, AX, ALU.min)); step.wait()
                        V.tensor_tensor(dil_e[:].rearrange("p (g j) -> p g j", g=3),
                                        dil_m[:, 0:3].unsqueeze(1).broadcast_to([P, 3, 3]),
                                        nmax[:, qt, FOX:16].rearrange("p (g j) -> p g j", g=3), ALU.subtract)\
                            .then_inc(s_["dil_in"], 1)
                    V.tensor_copy(o[:, qt, 512 * g:512 * g + 512], bank_of(G)).then_inc(s_["pv_read"], 1)
                    if g == 1:
                        step(V.reciprocal(fac[:, qt, 0:FOX], sums[:, qt, 0:FOX]))
                        dve.wait_ge(s_["dil_exp"], qt + 1)
                        fd = fac[:, qt, FOX:16]
                        step(V.tensor_tensor(fd, dil_e[:], sums[:, qt, FOX:16], ALU.mult)); step.wait()
                        step(V.tensor_reduce(dil_m[:, 3:6], fd.rearrange("p (g j) -> p j g", g=3), AX, ALU.add))
                        step.wait()
                        step(V.reciprocal(dil_m[:, 3:6], dil_m[:, 3:6])); step.wait()
                        step(V.tensor_tensor(fd.rearrange("p (g j) -> p g j", g=3),
                                             dil_e[:].rearrange("p (g j) -> p g j", g=3),
                                             dil_m[:, 3:6].unsqueeze(1).broadcast_to([P, 3, 3]), ALU.mult))
                        dve.wait_ge(s_["pv_read"], G + 1)
                        step.wait()
                        oo = items(o[:, qt, 0:1024], DH)
                        step(V.tensor_tensor(oo, oo, fac[:, qt, 0:16].unsqueeze(2).broadcast_to([P, 16, DH]), ALU.mult))
                    return
                step(V.reciprocal(f, sums[:, qt, i0:i1])); step.wait()
                if g <= 4:
                    branch = {2: 1, 3: 2, 4: 0}[g]
                    step(V.tensor_tensor(f, f, gate[:, qt, branch * 8:branch * 8 + 8], ALU.mult)); step.wait()
                    dst = items(o[:, qt, 1024:1536], DH)
                    if g == 4:
                        step(V.tensor_scalar(f, f, const("valid")[:, qt:qt + 1], None, ALU.mult)); step.wait()
                    tmp = items(ada_tmp if g > 2 else o[:, qt, 1024:1536], DH)
                    V.tensor_tensor(tmp, items(bank_of(G), DH), f.unsqueeze(2).broadcast_to([P, 8, DH]), ALU.mult)\
                        .then_inc(s_["pv_read"], 1)
                    if g > 2:
                        dve.wait_ge(s_["pv_read"], G + 1)
                        step(V.tensor_tensor(dst, dst, tmp, ALU.add)); step.wait()
                    return
                ff = f.rearrange("p (h a) -> p h a", a=2)
                step(V.tensor_scalar(ff[:, :, 1], ff[:, :, 1], lam[:, 2:3], None, ALU.mult)); step.wait()
                tmp = ada_tmp.rearrange("p (h a d) -> p h a d", h=2, a=2)
                V.tensor_tensor(items(ada_tmp, 2 * DH), items(bank_of(G), 2 * DH),
                                f.unsqueeze(2).broadcast_to([P, 4, 2 * DH]), ALU.mult).then_inc(s_["pv_read"], 1)
                dve.wait_ge(s_["pv_read"], G + 1)
                c0 = 1536 + (g - 5) * 256
                dst = o[:, qt, c0:c0 + 256].rearrange("p (h d) -> p h d", h=2)
                step(V.tensor_tensor(dst, tmp[:, :, 0], tmp[:, :, 1], ALU.add)); step.wait()

            ends = {qt * NPAIR + r[-1]: qt * len(GROUPS) + g for qt in range(TT) for g, r in enumerate(GROUPS)}
            for n in range(TT * NPAIR + 3):
                if n < TT * NPAIR:
                    score(n)
                if n - 3 in ends:
                    finish(ends[n - 3])
                a, b = divmod(n, 10)
                if a < PLAN["ada_b"][1]:
                    ada_part(PLAN["ada_b"][0] + a, KT * b // 10, KT * (b + 1) // 10)
                if b == 4 and 1 <= a <= PLAN["ada_b"][1]:
                    ada_read(N_EARLY + a - 1)
            step.wait()
            od = o[:, :, 1536:2048].rearrange("p m (h d) -> p m h d", h=DIFF)
            for m in range(TT):
                step(V.tensor_tensor(ada_tmp[:].rearrange("p (h d) -> p h d", h=DIFF), od[:, m], od[:, m], ALU.mult))
                step.wait()
                step(V.tensor_reduce(diff_ss[:, m], ada_tmp[:].rearrange("p (h d) -> p h d", h=DIFF), AX, ALU.add))
                step.wait()
            V.tensor_scalar(diff_ss[:], diff_ss[:], 1.0 / (2 * DH), EPS, ALU.mult, ALU.add).then_inc(s_["diff_in"], 1)
            dve.wait_ge(s_["diff_in"], 2)
            step(V.reciprocal(diff_ss[:], diff_ss[:])); step.wait()
            for m in range(TT):
                for f in range(DIFF):
                    step(V.scalar_tensor_tensor(od[:, m, f], od[:, m, f], diff_ss[:, m, f:f + 1], v_("subln"),
                                                ALU.mult, ALU.mult))
            step.wait()
            V.tensor_scalar(o[:, :, 1536:2048], o[:, :, 1536:2048], 1.0 - LAM_INIT, None, ALU.mult)\
                .then_inc(s_["o_ready"], 1)
            dve.wait_ge(s_["mod_ready"], 25)
            dve.wait_ge(s_["tr_free"], 16)
            V.scalar_tensor_tensor(scale_col[:], mod[:, 64:80], 1.0, v_("norm_ffn"), ALU.add, ALU.mult)\
                .then_inc(s_["mod_ready"], 1)

            def g_diag(n, col):
                V.tensor_tensor(diag2 if n else diag[:], ident.unsqueeze(1).broadcast_to([P, KT, P]),
                                mod[:, col:col + KT].unsqueeze(2).broadcast_to([P, KT, P]), ALU.mult)\
                    .then_inc(s_["g_diag"], 1)

            def residual(name, n, nb):
                acc = FIRST_ACC[name]
                row, tmp = (g_row2, g_tmp2) if n else (g_row, g_tmp)
                c = slice(nb * CH, nb * CH + CH)
                s = nb % 2
                V.tensor_tensor(tmp, psum[:, 2 * s:2 * s + 2], row[:, c].unsqueeze(1).broadcast_to([P, TT, CH]),
                                ALU.mult).then_inc(s_["acc_free"], 1)
                dve.wait_ge(s_["acc_free"], acc + nb + 3)
                V.tensor_tensor(h[:, :, c], h[:, :, c], tmp, ALU.add).then_inc(s_["h_ready"], 1)
                dve.wait_ge(s_["h_ready"], 4 * n + nb + 1)

            dve.wait_ge(s_["o_ready"], 1)
            dve.wait_ge(s_["pv"], TT * NPAIR)
            g_diag(0, 32)
            dve.wait_ge(s_["g_row_ready"], 1)
            for nb in range(4):
                wait_used(dve, PLAN["w_out"][0] + nb)
                residual("w_out", 0, nb)
            rms(2)
            scale_tokens(h)
            base, acc = PLAN["ffn"][0], FIRST_ACC["ffn"]
            dve.wait_ge(s_["g_row_ready"], 1)
            dve.wait_ge(s_["tr_free"], 32)
            V.tensor_copy(x_hi[:], xT[:]).then_inc(s_["x_split"], 1)
            dve.wait_ge(s_["x_split"], 1)
            V.tensor_tensor(x_lo[:], xT[:], x_hi[:].bitcast(F32), ALU.subtract).then_inc(s_["x_split"], 1)

            def gated(i):
                dve.wait_ge(s_["unit_used"], i * 8 + 10)
                dve.wait_ge(s_["acc_free"], i * 2 + (acc + 3))
                V.tensor_tensor(hT[:, bass.ds(i * 4, 4), :].rearrange("p k s -> p (k s)"), silu_g,
                                psum[:, 2:4].rearrange("p b n -> p (b n)"), ALU.mult).then_inc(s_["acc_free"], 1)

            def low_parts(i, gated_before):
                for s in range(2):
                    for q in range(4):
                        dve.wait_ge(s_["high"], i * 8 + (4 * s + q + 1))
                        ins = V.tensor_tensor(w_lo[:, q % 2], W(s)[:, :, q * P:(q + 1) * P],
                                              w_hi[:, q % 2].bitcast(F32), ALU.subtract)
                        if q < 3:
                            ins.then_inc(s_["low"], 1)
                        else:
                            ins.then_inc(USED[s], 1)
                        if gated_before and s == 0 and q == 1:
                            gated(i - 1)

            low_parts(0, False)
            with dve.Fori(1, 11) as i:
                low_parts(i, True)
            gated(10)
            dve.wait_ge(s_["g_sum"], 1)
            g_diag(1, 80)

            def down_residual(nb):
                dve.wait_ge(s_["g_row_ready"], 2)
                dve.wait_ge(s_["unit_used"], 2 + N_FFN + (nb + 1) * N_DOWN // 2)
                residual("down", 1, nb)

            for i in range(2):
                for u, (nb, part, k, n, last) in enumerate(DOWN_UNITS):
                    load = PLAN["down"][0] + 6 * i + 3 * nb + part
                    dve.wait_ge(s_["high"], N_FFN + i * N_DOWN + u + 1)
                    kk = part * KT + k
                    V.tensor_tensor(hd_lo[:, u % 2, 0:n], hT[:, kk:kk + n], hd_hi[:, u % 2, 0:n].bitcast(F32), ALU.subtract)
                    V.tensor_tensor(wd_lo[:, u % 2, 0:n], W(load % 2)[:, k:k + n], wd_hi[:, u % 2, 0:n].bitcast(F32),
                                    ALU.subtract).then_inc(USED[load % 2] if last else s_["low"], 1)
                    if part == 0 and k == 4 and (i or nb):
                        down_residual(2 * i + nb - 1)
            down_residual(3)
            dve_block2(dve, step, rms, scale_tokens)

    return nc


def layout(inputs):
    f = {k: np.asarray(v) for k, v in inputs.items()}
    one = {k: (v[0] if v.ndim and v.shape[0] == 1 else v) for k, v in f.items()}
    loads = np.zeros((N_LOADS, P, LOAD), np.float32)

    def put(name, w, first=0):
        t = tiles(w)
        loads[PLAN[name][0] + first:PLAN[name][0] + first + len(t), :, :t.shape[2]] = t

    ada = tiles(one["ada_w"])
    early = ada[:N_EARLY].reshape(N_EARLY, P, 2, LOAD // 2).transpose(0, 2, 1, 3)
    loads[PLAN["ada_b"][0]:PLAN["ada_b"][0] + PLAN["ada_b"][1]] = ada[N_EARLY:]
    put("w_in", take(one["w_in"], w_in_columns()))
    put("w_out", one["w_out"][w_out_rows()])
    fa, _ = PLAN["ffn"]
    loads[fa:fa + 22:2] = tiles(one["ffn_w_gate"])
    loads[fa + 1:fa + 22:2] = tiles(one["ffn_w_up"])
    da, _ = PLAN["down"]
    down = tiles(one["ffn_w_down"]).reshape(4, P, KF, CH)
    for nb in range(4):
        for part in range(3):
            piece = down[nb, :, part * KT:(part + 1) * KT].reshape(P, -1)
            loads[da + 3 * nb + part, :, :piece.shape[1]] = piece
    block2_layout(one, loads, put)
    const, tabs = constants()
    vec = np.zeros((P, N_VEC), np.float32)

    def vput(name, a):
        at, n = VEC[name]
        vec[:a.shape[0], at:at + n] = a

    vput("c", cols(one["c"].reshape(-1)))
    vput("ada_b", cols(one["ada_b"]))
    vput("norm_mix", cols(one["norm_mix_g"]))
    vput("norm_ffn", cols(one["norm_ffn_g"]))
    vput("norm_2", cols(one["norm_g_2"]))
    vput("mem_norm", cols(one["mem_norm_g_2"]))
    vput("fox_b", rows(one["fox_f_bias"]))
    vput("lam", rows(one["diff_lambda"]))
    vput("subln", rows(one["diff_subln_g"]))
    vput("cmp_pos", np.tile(one["nsa_cmp_pos"].transpose(2, 0, 1).reshape(DH, -1), (2, 1)))
    vput("cmp_w2", one["nsa_cmp_w2"].transpose(1, 0, 2).reshape(DH, -1))
    w1 = one["nsa_cmp_w1"].reshape(2, CMP_LEN, DH, DH).transpose(2, 0, 1, 3)
    arrays = {"x": one["x"], "loads": loads, "ada_early": early, "const": const, "tabs": tabs, "vec": vec, "cmp_w1": w1}
    arrays.update(block2_arrays(one))
    return {k: np.ascontiguousarray(v) for k, v in arrays.items()}


def block2_layout(one, loads, put):
    put("mem", one["w_mem_kv_2"])
    w = one["w_in_2"]
    put("a_qk", w[:, 0:2048])
    put("a_v", w[:, 2048:3072])
    put("z_in", w[:, 3072:4096])
    put("b_in", w[:, 4096:7168])
    put("z_in", w[:, 7168:8192], 4)
    put("c_q", w[:, 8320:9344])
    put("z_in", w[:, 9344:10368], 2)
    put("gates", w[:, 10368:16512])
    at = PLAN["ups"][0]
    for i, name in enumerate(("w_up_a_2", "w_up_b_2", "w_up_c_2")):
        t = tiles(one[name])
        for j in range(2):
            loads[at + 2 * i + j] = np.concatenate([t[2 * j], t[2 * j + 1]], 1)
    put("w_o", one["w_o_2"])


def block2_arrays(one):
    q, k = np.arange(SEQ)[:, None], np.arange(SEQ)[None]
    rel = np.concatenate([one["a_rel_bias_2"], np.full((8, 1), NEG, np.float32)], 1)
    index = np.where(k // 64 <= q // 64, np.clip(q - k, -128, 128) + 128, 257)
    bias = rel[:, index]
    t = np.concatenate([bias[:, :P, :P], bias[:, P:, :]], 2).transpose(1, 0, 2).reshape(P, -1)
    gains = np.concatenate([rows(one["c_q_g_2"]), rows(one["c_k_g_2"]), rows(one["a_q_g_2"]), rows(one["a_k_g_2"]),
                            np.concatenate([one["b_mu_w_2"], one["b_mu_a_2"]])[:, None]], 1)
    b_rows = np.stack([*one["b_mu_rkv_2"], one["b_w0_2"], one["b_a0_2"], one["b_k_k_2"], one["b_k_a_2"],
                       one["b_r_k_2"].reshape(-1), one["b_ln_w_2"], one["b_ln_b_2"]])
    s, c = np.arange(P)[:, None], np.arange(P)[None]
    same = s // 64 == c // 64
    b_cst = np.concatenate([same & (s <= c), s // 64 == np.arange(2)[None]], 1).astype(np.float32)
    strict, incl = same & (s < c), same & (s <= c)
    levels = [(s // (2 * b) == c // (2 * b)) & (s // b % 2 == 0) & (c // b % 2 == 1) for b in (1, 2, 4, 8, 16, 32)]
    masks = np.concatenate([strict, incl, strict, incl, *levels], 1).astype(np.float32)
    return {"final_g": one["final_norm_g"][None], "mem": one["mem_2"], "vec2": gains, "b_rows": b_rows,
            "w2a2": np.concatenate([one["b_w2_2"], one["b_a2_2"]]), "b_cst": b_cst, "masks": masks, "a_bias": t,
            "lora_w": one["w_in_2"][:, 8192:8320].reshape(KT, P, P).transpose(1, 0, 2)}


def kernel(**inputs):
    import concourse.bacc as bacc
    from concourse.bass_utils import run_bass_kernel_spmd

    arrays = layout(inputs)
    nc = bacc.Bacc("TRN2", target_bir_lowering=False, num_devices=1)
    A = {k: nc.dram_tensor(f"in_{k}", v.shape, F32, kind="ExternalInput").ap() for k, v in arrays.items()}
    out = nc.dram_tensor("out_x", (SEQ, D), F32, kind="ExternalOutput").ap()
    hybrid_blocks(nc, A, out)
    r = run_bass_kernel_spmd(nc, [{f"in_{k}": v for k, v in arrays.items()}], core_ids=[0])
    return r.results[0]["out_x"].reshape(1, SEQ, D)
```
